# Optimizing a Trainium2 kernel written in Bass

```python
import jax, jax.numpy as jnp
from jax import lax
import numpy as np

D_MODEL = 1024
BATCH = 1
SEQ = 512
DEPTH = 1

HEAD_DIM = 64
ATTN_HEADS = 8
ATTN_KV_HEADS = 2
ATTN_GROUP = ATTN_HEADS // ATTN_KV_HEADS
RET_HEADS = 8
ATTN_WIDTH = ATTN_HEADS * HEAD_DIM
KV_WIDTH = ATTN_KV_HEADS * HEAD_DIM
RET_WIDTH = RET_HEADS * HEAD_DIM
MIX_WIDTH = ATTN_WIDTH + RET_WIDTH
IN_PROJ = ATTN_WIDTH + 2 * KV_WIDTH + 4 * RET_WIDTH
WINDOW = 128
BLOCK = 128
RET_CHUNK = 128
ROPE_THETA = 10000.0
D_FF = -(-8 * D_MODEL // (3 * 256)) * 256
EPS = 1e-6
NEG_INF = -1e30


def rms_norm(x, w):
    xf = x.astype(jnp.float32)
    y = xf * lax.rsqrt(jnp.mean(xf * xf, axis=-1, keepdims=True) + EPS)
    return (y * w.astype(jnp.float32)).astype(x.dtype)

def rope(x, pos):
    d = x.shape[-1]
    inv_freq = ROPE_THETA ** (-jnp.arange(0, d, 2, dtype=jnp.float32) / d)
    ang = pos[:, None] * inv_freq[None, :]
    cos = jnp.concatenate([jnp.cos(ang), jnp.cos(ang)], -1)[None, :, None, :]
    sin = jnp.concatenate([jnp.sin(ang), jnp.sin(ang)], -1)[None, :, None, :]
    xf = x.astype(jnp.float32)
    x1, x2 = xf[..., : d // 2], xf[..., d // 2:]
    rot = jnp.concatenate([-x2, x1], axis=-1)
    return (xf * cos + rot * sin).astype(x.dtype)

def windowed_gqa_sink(q, k, v, sink):
    B, S, H, D = q.shape
    nb = S // BLOCK
    pad = ((0, 0), (BLOCK, BLOCK), (0, 0), (0, 0))
    kp = jnp.pad(k, pad).reshape(B, nb + 2, BLOCK, ATTN_KV_HEADS, D)
    vp = jnp.pad(v, pad).reshape(B, nb + 2, BLOCK, ATTN_KV_HEADS, D)
    kb = jnp.concatenate([kp[:, :-2], kp[:, 1:-1], kp[:, 2:]], axis=2)
    vb = jnp.concatenate([vp[:, :-2], vp[:, 1:-1], vp[:, 2:]], axis=2)
    qb = q.reshape(B, nb, BLOCK, ATTN_KV_HEADS, ATTN_GROUP, D)
    scale = D ** -0.5
    s = jnp.einsum('bnqkgd,bnjkd->bnkgqj', qb, kb).astype(jnp.float32) * scale
    q_pos = jnp.arange(nb)[:, None] * BLOCK + jnp.arange(BLOCK)[None, :]
    k_pos = jnp.arange(nb)[:, None] * BLOCK - BLOCK + jnp.arange(3 * BLOCK)[None, :]
    valid = (jnp.abs(q_pos[:, :, None] - k_pos[:, None, :]) <= WINDOW) \
        & (k_pos >= 0)[:, None, :] & (k_pos < S)[:, None, :]
    s = jnp.where(valid[None, :, None, None], s, NEG_INF)
    sink_l = sink.astype(jnp.float32).reshape(ATTN_KV_HEADS, ATTN_GROUP)[None, None, :, :, None, None]
    m = jnp.maximum(jnp.max(s, axis=-1, keepdims=True), sink_l)
    p = jnp.exp(s - m)
    p = p / (jnp.sum(p, axis=-1, keepdims=True) + jnp.exp(sink_l - m))
    o = jnp.einsum('bnkgqj,bnjkd->bnqkgd', p.astype(v.dtype), vb)
    return o.reshape(B, S, H * D)

def retention_direction(q, k, v, log_gamma, strict):
    B, H, S, D = q.shape
    C = RET_CHUNK
    nc = S // C
    qc = q.reshape(B, H, nc, C, D)
    kc = k.reshape(B, H, nc, C, D)
    vc = v.reshape(B, H, nc, C, D)
    idx = jnp.arange(C, dtype=jnp.float32)
    diff = idx[:, None] - idx[None, :]
    mask = diff > 0 if strict else diff >= 0
    lg = log_gamma[:, None, None]
    dmat = jnp.where(mask[None], jnp.exp(lg * jnp.maximum(diff, 0.0)[None]), 0.0)
    xi = jnp.exp(log_gamma[:, None] * (idx + 1.0)[None])
    zeta = jnp.exp(log_gamma[:, None] * (C - 1.0 - idx)[None])
    g_chunk = jnp.exp(log_gamma * C)[None, :, None, None]
    inner = jnp.einsum('bhcnd,bhcmd->bhcnm', qc, kc) * dmat[None, :, None]
    out_inner = jnp.einsum('bhcnm,bhcme->bhcne', inner, vc)
    kv = jnp.einsum('bhcmd,bhcme->bhcde', kc * zeta[None, :, None, :, None], vc)

    def step(r, kv_c):
        return g_chunk * r + kv_c, r

    _, states = lax.scan(step, jnp.zeros((B, H, D, D), jnp.float32), jnp.moveaxis(kv, 2, 0))
    states = jnp.moveaxis(states, 0, 2)
    cross = jnp.einsum('bhcnd,bhcde->bhcne', qc * xi[None, :, None, :, None], states)
    return (out_inner + cross).reshape(B, H, S, D)

def bidirectional_retention(q, k, v, log_fwd, log_bwd):
    fwd = retention_direction(q, k, v, log_fwd, False)
    bwd = retention_direction(jnp.flip(q, 2), jnp.flip(k, 2), jnp.flip(v, 2), log_bwd, True)
    return fwd + jnp.flip(bwd, 2)

def first_inputs(seed: int = 0) -> dict:
    key = jax.random.key(seed)
    ks = jax.random.split(key, 16)
    f32 = jnp.float32
    nrm = lambda k, shape, fan_in: jax.random.normal(k, shape, f32) * fan_in ** -0.5
    base_decay = np.log(1.0 - 2.0 ** (-5.0 - np.arange(RET_HEADS))).astype(np.float32)
    base_decay = jnp.asarray(base_decay)[None, :]
    return {
        "x": jax.random.normal(ks[0], (BATCH, SEQ, D_MODEL), f32),
        "attn_norm_w": 1.0 + 0.02 * jax.random.normal(ks[1], (DEPTH, D_MODEL), f32),
        "w_in": nrm(ks[2], (DEPTH, D_MODEL, IN_PROJ), D_MODEL),
        "q_norm_w": 1.0 + 0.02 * jax.random.normal(ks[3], (DEPTH, HEAD_DIM), f32),
        "k_norm_w": 1.0 + 0.02 * jax.random.normal(ks[4], (DEPTH, HEAD_DIM), f32),
        "attn_sink": 0.5 * jax.random.normal(ks[5], (DEPTH, ATTN_HEADS), f32),
        "ret_log_decay_fwd": base_decay * (1.0 + 0.05 * jax.random.normal(ks[6], (DEPTH, RET_HEADS), f32)),
        "ret_log_decay_bwd": base_decay * (1.0 + 0.05 * jax.random.normal(ks[7], (DEPTH, RET_HEADS), f32)),
        "ret_norm_w": 1.0 + 0.02 * jax.random.normal(ks[8], (DEPTH, RET_WIDTH), f32),
        "w_out": nrm(ks[9], (DEPTH, MIX_WIDTH, D_MODEL), MIX_WIDTH),
        "ffn_norm_w": 1.0 + 0.02 * jax.random.normal(ks[10], (DEPTH, D_MODEL), f32),
        "w_gate": nrm(ks[11], (DEPTH, D_MODEL, D_FF), D_MODEL),
        "w_up": nrm(ks[12], (DEPTH, D_MODEL, D_FF), D_MODEL),
        "w_down": nrm(ks[13], (DEPTH, D_FF, D_MODEL), D_FF),
    }

def first_block(x, attn_norm_w, w_in, q_norm_w, k_norm_w, attn_sink, ret_log_decay_fwd,
              ret_log_decay_bwd, ret_norm_w, w_out, ffn_norm_w, w_gate, w_up, w_down):
    B, S, _ = x.shape
    pos = jnp.arange(S, dtype=jnp.float32)
    split_at = np.cumsum([ATTN_WIDTH, KV_WIDTH, KV_WIDTH, RET_WIDTH, RET_WIDTH, RET_WIDTH]).tolist()
    h = x
    for l in range(DEPTH):
        n = rms_norm(h, attn_norm_w[l])
        proj = n @ w_in[l]
        aq, ak, av, rq, rk, rv, rg = jnp.split(proj, split_at, axis=-1)
        aq = rope(rms_norm(aq.reshape(B, S, ATTN_HEADS, HEAD_DIM), q_norm_w[l]), pos)
        ak = rope(rms_norm(ak.reshape(B, S, ATTN_KV_HEADS, HEAD_DIM), k_norm_w[l]), pos)
        av = av.reshape(B, S, ATTN_KV_HEADS, HEAD_DIM)
        y_attn = windowed_gqa_sink(aq, ak, av, attn_sink[l])
        rq = rope(rq.reshape(B, S, RET_HEADS, HEAD_DIM), pos)
        rk = rope(rk.reshape(B, S, RET_HEADS, HEAD_DIM), pos) * (HEAD_DIM ** -0.5)
        rv = rv.reshape(B, S, RET_HEADS, HEAD_DIM)
        to_bhsd = lambda t: jnp.transpose(t, (0, 2, 1, 3)).astype(jnp.float32)
        ret = bidirectional_retention(to_bhsd(rq), to_bhsd(rk), to_bhsd(rv),
                                      -jnp.abs(ret_log_decay_fwd[l].astype(jnp.float32)),
                                      -jnp.abs(ret_log_decay_bwd[l].astype(jnp.float32)))
        ret = jnp.transpose(ret, (0, 2, 1, 3)).astype(h.dtype)
        ret = rms_norm(ret, ret_norm_w[l].reshape(RET_HEADS, HEAD_DIM)).reshape(B, S, RET_WIDTH)
        y_ret = jax.nn.silu(rg) * ret
        h = h + jnp.concatenate([y_attn, y_ret], axis=-1) @ w_out[l]
        m = rms_norm(h, ffn_norm_w[l])
        h = h + (jax.nn.silu(m @ w_gate[l]) * (m @ w_up[l])) @ w_down[l]
    return h


D_FF_2 = 2816
MLSTM_HEADS = 4
MLSTM_DQK = 128
MLSTM_DV = 256
MLSTM_CHUNK = 64
CONV_WIDTH = 4
FOX_HEADS = 16
FOX_DH = 64
FOX_BLOCK = 128
N_MOD = 9
MLSTM_QK = MLSTM_HEADS * MLSTM_DQK
MLSTM_V = MLSTM_HEADS * MLSTM_DV
FOX_W = FOX_HEADS * FOX_DH
MIX_SPLITS = (MLSTM_QK, MLSTM_QK, MLSTM_V, MLSTM_V, MLSTM_HEADS, MLSTM_HEADS, FOX_W, FOX_W, FOX_W, FOX_HEADS, D_MODEL, D_MODEL)
MIX_WIDTH_2 = 2 * MLSTM_QK + 2 * MLSTM_V + 2 * MLSTM_HEADS + 3 * FOX_W + FOX_HEADS + 2 * D_MODEL


def _mix_offsets():
    offs = [0]
    for s in MIX_SPLITS:
        offs.append(offs[-1] + s)
    return offs

def rms_norm_2(x, g):
    xf = x.astype(jnp.float32)
    y = xf * lax.rsqrt(jnp.mean(xf * xf, axis=-1, keepdims=True) + EPS)
    return (y * g.astype(jnp.float32)).astype(x.dtype)

def swiglu(u, w_in, w_out):
    a, b = jnp.split(u @ w_in, 2, axis=-1)
    return (jax.nn.silu(a) * b) @ w_out

def causal_conv(x, w, b):
    y = lax.conv_general_dilated(x, w[:, None, :], window_strides=(1,), padding=[(CONV_WIDTH - 1, 0)],
                                 dimension_numbers=('NWC', 'WIO', 'NWC'), feature_group_count=x.shape[-1])
    return y + b

def mlstm_chunkwise(q, k, v, i_pre, f_pre):
    B, S, H, _ = q.shape
    L = MLSTM_CHUNK
    nc = S // L
    f32 = jnp.float32

    def to_chunks(t):
        t = jnp.moveaxis(t.astype(f32), 2, 1)
        t = t.reshape((B, H, nc, L) + t.shape[3:])
        return jnp.moveaxis(t, 2, 0)

    qc = to_chunks(q)
    kc = to_chunks(k) * (MLSTM_DQK ** -0.5)
    vc = to_chunks(v)
    ic = to_chunks(i_pre)
    lfc = to_chunks(jax.nn.log_sigmoid(f_pre.astype(f32)))
    causal = jnp.tril(jnp.ones((L, L), dtype=bool))

    def step(carry, inp):
        C, n, m = carry
        qt, kt, vt, it, lft = inp
        b = jnp.cumsum(lft, axis=-1)
        log_d = jnp.where(causal, b[..., :, None] - b[..., None, :] + it[..., None, :], -jnp.inf)
        log_inter = b + m[..., None]
        m_t = jnp.maximum(log_inter, jnp.max(log_d, axis=-1))
        w_inter = jnp.exp(log_inter - m_t)
        s = jnp.einsum('bhtd,bhsd->bhts', qt, kt) * jnp.exp(log_d - m_t[..., None])
        num = w_inter[..., None] * jnp.einsum('bhtd,bhde->bhte', qt, C) + jnp.einsum('bhts,bhse->bhte', s, vt)
        den = w_inter * jnp.einsum('bhtd,bhd->bht', qt, n) + jnp.sum(s, axis=-1)
        h = num / jnp.maximum(jnp.abs(den), jnp.exp(-m_t))[..., None]
        b_last = b[..., -1]
        log_w = b_last[..., None] - b + it
        m_new = jnp.maximum(b_last + m, jnp.max(log_w, axis=-1))
        w_k = jnp.exp(log_w - m_new[..., None])
        decay = jnp.exp(b_last + m - m_new)
        C_new = decay[..., None, None] * C + jnp.einsum('bhs,bhsd,bhse->bhde', w_k, kt, vt)
        n_new = decay[..., None] * n + jnp.einsum('bhs,bhsd->bhd', w_k, kt)
        return (C_new, n_new, m_new), h

    init = (jnp.zeros((B, H, MLSTM_DQK, MLSTM_DV), f32), jnp.zeros((B, H, MLSTM_DQK), f32), jnp.zeros((B, H), f32))
    _, h = lax.scan(step, init, (qc, kc, vc, ic, lfc))
    h = jnp.moveaxis(h, 0, 2).reshape(B, H, S, MLSTM_DV)
    return jnp.moveaxis(h, 1, 2)

def forgetting_attention(q, k, v, f_pre, q_g, k_g):
    B, S, H, Dh = q.shape
    f32 = jnp.float32
    q = jnp.moveaxis(rms_norm_2(q, q_g), 1, 2)
    k = jnp.moveaxis(rms_norm_2(k, k_g), 1, 2)
    v = jnp.moveaxis(v, 1, 2)
    F = jnp.moveaxis(jnp.cumsum(jax.nn.log_sigmoid(f_pre.astype(f32)), axis=1), 1, 2)
    nb = S // FOX_BLOCK
    qb = jnp.moveaxis(q.reshape(B, H, nb, FOX_BLOCK, Dh), 2, 0)
    Fb = jnp.moveaxis(F.reshape(B, H, nb, FOX_BLOCK), 2, 0)
    k_pos = jnp.arange(S)
    scale = Dh ** -0.5

    def block(args):
        q_blk, F_blk, blk_idx = args
        q_pos = blk_idx * FOX_BLOCK + jnp.arange(FOX_BLOCK)
        logits = jnp.einsum('bhqd,bhkd->bhqk', q_blk, k).astype(f32) * scale + (F_blk[..., :, None] - F[..., None, :])
        logits = jnp.where(k_pos[None, :] <= q_pos[:, None], logits, -jnp.inf)
        p = jax.nn.softmax(logits, axis=-1)
        return jnp.einsum('bhqk,bhkd->bhqd', p.astype(v.dtype), v)

    out = lax.map(block, (qb, Fb, jnp.arange(nb)))
    out = jnp.moveaxis(out, 0, 2).reshape(B, H, S, Dh)
    return jnp.moveaxis(out, 1, 2).reshape(B, S, H * Dh)

def hybrid_layer(x, c, w_ada, b_ada, ffn1_norm_g, ffn1_w_in, ffn1_w_out, mix_norm_g, w_mix, b_mix,
                 conv_w, conv_b, mlstm_norm_g, fox_q_norm_g, fox_k_norm_g, w_branch_a, w_branch_b, w_out,
                 ffn2_norm_g, ffn2_w_in, ffn2_w_out):
    B, S, _ = x.shape
    mod = jax.nn.silu(c) @ w_ada + b_ada
    sh1, sc1, g1, sh2, sc2, g2, sh3, sc3, g3 = [m[:, None, :] for m in jnp.split(mod, N_MOD, axis=-1)]

    u = rms_norm_2(x, ffn1_norm_g) * (1 + sc1) + sh1
    x = x + 0.5 * g1 * swiglu(u, ffn1_w_in, ffn1_w_out)

    u = rms_norm_2(x, mix_norm_g) * (1 + sc2) + sh2
    z = u @ w_mix + b_mix
    offs = _mix_offsets()
    q_m, k_m, v_m, o_m, i_m, f_m, q_f, k_f, v_f, f_f, g_a, g_b = [z[..., offs[j]:offs[j + 1]] for j in range(len(MIX_SPLITS))]

    qk_m = jax.nn.silu(causal_conv(jnp.concatenate([q_m, k_m], axis=-1), conv_w, conv_b))
    q_m, k_m = jnp.split(qk_m, 2, axis=-1)
    h_m = mlstm_chunkwise(q_m.reshape(B, S, MLSTM_HEADS, MLSTM_DQK), k_m.reshape(B, S, MLSTM_HEADS, MLSTM_DQK),
                          v_m.reshape(B, S, MLSTM_HEADS, MLSTM_DV), i_m, f_m)
    y_a = jax.nn.sigmoid(o_m) * rms_norm_2(h_m, mlstm_norm_g).reshape(B, S, MLSTM_V).astype(x.dtype)

    y_b = forgetting_attention(q_f.reshape(B, S, FOX_HEADS, FOX_DH), k_f.reshape(B, S, FOX_HEADS, FOX_DH),
                               v_f.reshape(B, S, FOX_HEADS, FOX_DH), f_f, fox_q_norm_g, fox_k_norm_g)

    merged = jax.nn.sigmoid(g_a) * (y_a @ w_branch_a) + jax.nn.sigmoid(g_b) * (y_b @ w_branch_b)
    x = x + g2 * (merged @ w_out)

    u = rms_norm_2(x, ffn2_norm_g) * (1 + sc3) + sh3
    x = x + 0.5 * g3 * swiglu(u, ffn2_w_in, ffn2_w_out)
    return x

def second_inputs(seed: int = 0) -> dict:
    key = jax.random.key(seed)
    ks = jax.random.split(key, 24)
    f32 = jnp.float32
    L = DEPTH
    D = D_MODEL

    def nrm(k, shape, scale):
        return jax.random.normal(k, shape, f32) * scale

    def gain(k, shape):
        return 1.0 + 0.05 * jax.random.normal(k, shape, f32)

    offs = _mix_offsets()
    b_mix = nrm(ks[9], (L, MIX_WIDTH_2), 0.02)
    b_mix = b_mix.at[:, offs[5]:offs[6]].add(jnp.linspace(3.0, 6.0, MLSTM_HEADS))
    b_mix = b_mix.at[:, offs[9]:offs[10]].add(jnp.linspace(2.0, 7.0, FOX_HEADS))
    return {
        "x": nrm(ks[0], (BATCH, SEQ, D), 1.0),
        "c": nrm(ks[1], (BATCH, D), 1.0),
        "w_ada": nrm(ks[2], (L, D, N_MOD * D), 0.5 * D ** -0.5),
        "b_ada": nrm(ks[3], (L, N_MOD * D), 0.02),
        "ffn1_norm_g": gain(ks[4], (L, D)),
        "ffn1_w_in": nrm(ks[5], (L, D, 2 * D_FF_2), D ** -0.5),
        "ffn1_w_out": nrm(ks[6], (L, D_FF_2, D), D_FF_2 ** -0.5),
        "mix_norm_g": gain(ks[7], (L, D)),
        "w_mix": nrm(ks[8], (L, D, MIX_WIDTH_2), D ** -0.5),
        "b_mix": b_mix,
        "conv_w": nrm(ks[10], (L, CONV_WIDTH, 2 * MLSTM_QK), CONV_WIDTH ** -0.5),
        "conv_b": nrm(ks[11], (L, 2 * MLSTM_QK), 0.02),
        "mlstm_norm_g": gain(ks[12], (L, MLSTM_HEADS, MLSTM_DV)),
        "fox_q_norm_g": gain(ks[13], (L, FOX_HEADS, FOX_DH)),
        "fox_k_norm_g": gain(ks[14], (L, FOX_HEADS, FOX_DH)),
        "w_branch_a": nrm(ks[15], (L, MLSTM_V, D), MLSTM_V ** -0.5),
        "w_branch_b": nrm(ks[16], (L, FOX_W, D), FOX_W ** -0.5),
        "w_out": nrm(ks[17], (L, D, D), D ** -0.5),
        "ffn2_norm_g": gain(ks[18], (L, D)),
        "ffn2_w_in": nrm(ks[19], (L, D, 2 * D_FF_2), D ** -0.5),
        "ffn2_w_out": nrm(ks[20], (L, D_FF_2, D), D_FF_2 ** -0.5),
    }

def second_block(x, c, w_ada, b_ada, ffn1_norm_g, ffn1_w_in, ffn1_w_out, mix_norm_g, w_mix, b_mix,
              conv_w, conv_b, mlstm_norm_g, fox_q_norm_g, fox_k_norm_g, w_branch_a, w_branch_b, w_out,
              ffn2_norm_g, ffn2_w_in, ffn2_w_out):
    for l in range(DEPTH):
        x = hybrid_layer(x, c, w_ada[l], b_ada[l], ffn1_norm_g[l], ffn1_w_in[l], ffn1_w_out[l], mix_norm_g[l],
                         w_mix[l], b_mix[l], conv_w[l], conv_b[l], mlstm_norm_g[l], fox_q_norm_g[l],
                         fox_k_norm_g[l], w_branch_a[l], w_branch_b[l], w_out[l], ffn2_norm_g[l],
                         ffn2_w_in[l], ffn2_w_out[l])
    return x


def setup_inputs(seed=0):
    out = dict(first_inputs(seed))
    for name, value in second_inputs(seed + 1).items():
        if name != "x":
            out[name + "_2"] = value
    return out


def reference(
    x, attn_norm_w, w_in, q_norm_w, k_norm_w, attn_sink, ret_log_decay_fwd, ret_log_decay_bwd,
    ret_norm_w, w_out, ffn_norm_w, w_gate, w_up, w_down, c_2, w_ada_2, b_ada_2, ffn1_norm_g_2,
    ffn1_w_in_2, ffn1_w_out_2, mix_norm_g_2, w_mix_2, b_mix_2, conv_w_2, conv_b_2,
    mlstm_norm_g_2, fox_q_norm_g_2, fox_k_norm_g_2, w_branch_a_2, w_branch_b_2, w_out_2,
    ffn2_norm_g_2, ffn2_w_in_2, ffn2_w_out_2,
):
    x = first_block(
        x, attn_norm_w, w_in, q_norm_w, k_norm_w, attn_sink, ret_log_decay_fwd,
        ret_log_decay_bwd, ret_norm_w, w_out, ffn_norm_w, w_gate, w_up, w_down,
    )
    return second_block(
        x, c_2, w_ada_2, b_ada_2, ffn1_norm_g_2, ffn1_w_in_2, ffn1_w_out_2, mix_norm_g_2,
        w_mix_2, b_mix_2, conv_w_2, conv_b_2, mlstm_norm_g_2, fox_q_norm_g_2, fox_k_norm_g_2,
        w_branch_a_2, w_branch_b_2, w_out_2, ffn2_norm_g_2, ffn2_w_in_2, ffn2_w_out_2,
    )


_drawn_inputs = setup_inputs


def setup_inputs(seed=0):
    import zlib

    import numpy as np

    out = dict(_drawn_inputs(seed))
    spreads = {}
    factors = {'attn_norm_w': 2.814,
     'q_norm_w': 8.0,
     'k_norm_w': 8.0,
     'attn_sink': 8.0,
     'ret_norm_w': 6.735,
     'ffn_norm_w': 4.19,
     'b_ada_2': 4.579,
     'ffn1_norm_g_2': 8.0,
     'mix_norm_g_2': 8.0,
     'conv_b_2': 64.0,
     'mlstm_norm_g_2': 64.0,
     'fox_q_norm_g_2': 8.0,
     'fox_k_norm_g_2': 8.0,
     'ffn2_norm_g_2': 8.0,
     'conv_w_2': 8.0}
    for name, (base, spread) in spreads.items():
        noise = np.random.default_rng([zlib.crc32(name.encode()), seed]).standard_normal(out[name].shape)
        drawn = base * np.exp(spread * noise) if base else spread * noise
        out[name] = __import__('jax').numpy.asarray(drawn.astype(out[name].dtype))
    for name, factor in factors.items():
        out[name] = (out[name] * factor).astype(out[name].dtype)
    return out
```

```python
from contextlib import ExitStack

import numpy as np
import concourse.bass as bass
from concourse import mybir

F32 = mybir.dt.float32
F32R = mybir.dt.float32r
BF16 = mybir.dt.bfloat16
ALU = mybir.AluOpType
ACT = mybir.ActivationFunctionType
AX = mybir.AxisListType

P = 128
S = 512
D = 1024
KC = D // P
NB = S // P
DH = 64
FF = 2816
FC = FF // P
HALF = FC // 2
WC = KC * P
DC = HALF * P
EPS = 1e-6
NEG = -1e30
AH = 8
RH = 8
MH = 4
DQK = 128
DV = 256
FH = 16
CONV = 4
NMOD = 9
REL = S + (NB - 1) * P
ADA_PARTS = KC

N_ATT, N_RET, N_OUT, N_FF, N_DOWN = 6, 16, 8, 2 * FC, 16
N_MLSTM, N_FOX, N_MERGE = 6 * MH, 24, 32
SLAB = {}
TILE = {}
_n = _q = 0
for _name, _count in (("att", N_ATT), ("ret", N_RET), ("out", N_OUT), ("ff0", N_FF), ("down0", N_DOWN),
                      ("ff1", N_FF), ("down1", N_DOWN), ("mlstm", N_MLSTM), ("fox", N_FOX),
                      ("merge", N_MERGE), ("out2", N_OUT), ("ff2", N_FF), ("down2", N_DOWN)):
    SLAB[_name], TILE[_name] = _n, _q
    _n += _count
    _q += _count // 2 if _name.startswith("down") else _count

COL = {}
_c = 0
for _name, _count in (("attn_norm", KC), ("ffn_norm", KC), ("ffn1_norm", KC), ("mix_norm", KC), ("ffn2_norm", KC),
                      ("q_norm", 1), ("k_norm", 1), ("ret_norm", RH // 2), ("sink", AH), ("decay_f", RH),
                      ("decay_b", RH), ("c", KC), ("b_ada", NMOD * KC), ("b_gates", 1), ("b_mlstm", 6 * MH),
                      ("conv_w", 2 * MH * CONV), ("conv_b", 2 * MH), ("mlstm_norm", 2 * MH), ("b_fox", 24),
                      ("fox_q", FH // 2), ("fox_k", FH // 2), ("b_merge", 16), ("sel", FH)):
    COL[_name] = _c
    _c += _count
NCOL = _c


PRIMED = ("act_lo", "ada_acc", "evac0", "evac1", "f_qk", "m_conv", "m_nMd", "m_out", "m_qk", "m_turned", "m_values",
          "m_weighted", "m_y", "mg", "mg_lo", "mod_sum", "norm_sum", "probs_scaled", "rope_out", "row_split", "ssum",
          "w_lo", "x_lo", "y_lo", "yb_lo")


def build(nc, x_in, cols_in, const_in, rel_in, w_in, wd_in, ada_in, gates_in, out):
    ctx = ExitStack()
    with ctx:
        def sb(name, shape, dt=F32, scope=ctx):
            return scope.enter_context(nc.sbuf_tensor(name, shape, dt))

        sems = {}

        def sem(name):
            if name not in sems:
                sems[name] = ctx.enter_context(nc.semaphore(name))
            return sems[name]

        def primed(count):
            return count + 1

        h = sb("h", [P, KC * S])
        xh = sb("xh", [P, KC, S], F32R)
        xl = sb("xl", [P, KC, S], F32R)
        raw = sb("raw", [P, 2, DC])
        whi = sb("whi", [P, 2, DC], F32R)
        wlo = sb("wlo", [P, 2, DC], F32R)
        col = sb("col", [P, NCOL])
        modc = sb("modc", [P, NMOD * KC])
        scl = sb("scl", [P, 3 * KC])
        gat = sb("gat", [P, 3 * KC])
        ident = sb("ident", [P, P])
        ones = sb("ones", [P, P])
        blk = sb("blk", [P, P])
        identb = sb("identb", [P, P], BF16)
        ge = sb("ge", [P, P])
        geb = sb("geb", [P, P], BF16)
        leb = sb("leb", [P, P], BF16)
        csil = sb("csil", [P, KC])
        ssum = sb("ssum", [P, S])
        sqn = sb("sqn", [P, 2, S])
        rstd = sb("rstd", [P, S])
        tmp = sqn
        gates_raw = sb("gates_raw", [P, KC * 96])
        stat = sb("stat", [P, 2, 8])
        lg = sb("lg", [P, 2 * RH])
        epsc = sb("epsc", [P, 1])

        ffs = ExitStack()
        acth = sb("acth", [P, FC, S], F32R, ffs)
        actl = sb("actl", [P, FC, S], F32R, ffs)
        gsil = sb("gsil", [P, 2, S], F32, ffs)
        aprod = sb("aprod", [P, 2, S], F32, ffs)
        adaw = sb("adaw", [P, 2, D], F32, ffs)
        adac = sb("adac", [P, D], F32, ffs)
        ffs.close()

        abs_ = ExitStack()
        yh = sb("yh", [P, KC, S], F32R, abs_)
        yl = sb("yl", [P, KC, S], F32R, abs_)
        decay = sb("decay", [P, 2 * REL], F32, abs_)
        rel = sb("rel", [P, 2 * REL], F32, abs_)
        cos = sb("cos", [P, S], F32, abs_)
        sin = sb("sin", [P, S], F32, abs_)
        rot = sb("rot", [P, P], F32, abs_)
        leconst = sb("leconst", [P, P], F32, abs_)
        rraw = sb("rraw", [P, 2, S], F32, abs_)
        rsq = sb("rsq", [P, S], F32, abs_)
        rr = sb("rr", [P, S], F32, abs_)
        rt = sb("rt", [P, 2, S], F32, abs_)
        qall = sb("qall", [P, AH // 2, S], F32, abs_)
        qf = sb("qf", [P, S], F32, abs_)
        kf = sb("kf", [P, S], F32, abs_)
        rqf = sb("rqf", [P, S], F32, abs_)
        rkf = sb("rkf", [P, S], F32, abs_)
        rvtok = sb("rvtok", [P, NB, P], F32, abs_)
        vraw = sb("vraw", [P, S], F32, abs_)
        vtok = sb("vtok", [P, NB, P], F32, abs_)
        prob = sb("prob", [P, 2, S], F32, abs_)
        pT = sb("pT", [P, 2, S], F32, abs_)
        rsil = sb("rsil", [P, S], F32, abs_)
        ry = sb("ry", [P, S], F32, abs_)
        abs_.close()

        mix = ExitStack()
        yah = sb("yah", [P, KC, S], F32R, mix)
        yal = sb("yal", [P, KC, S], F32R, mix)
        sel = sb("sel", [96, FH, P], BF16, mix)
        fsp = sb("fsp", [96, S], BF16, mix)
        mls = ExitStack()
        ghi = sb("ghi", [P, KC * 96], F32R, mls)
        glo = sb("glo", [P, KC * 96], F32R, mls)
        zg = sb("zg", [96, S], F32, mls)
        zt = sb("zt", [96, S], F32, mls)
        zi = sb("zi", [MH, S], F32, mls)
        scan = sb("scan", [48, 2, S // 2 + S], F32, mls)
        msM = sb("msM", [96, S], BF16, mls)
        msm = sb("msm", [96, S], BF16, mls)
        gsp = sb("gsp", [48, 3, S], BF16, mls)
        arow = sb("arow", [MH, S], F32, mls)
        frow = sb("frow", [MH, S], F32, mls)
        acol = sb("acol", [P, NB * MH], F32, mls)
        qz = sb("qz", [P, 2, S + CONV - 1], F32, mls)
        cv = sb("cv", [P, 2, S], F32, mls)
        qk = sb("qk", [P, 2, S], F32, mls)
        mvT = sb("mvT", [P, 2, S], F32, mls)
        mv = sb("mv", [P, NB, DV], F32, mls)
        nM = sb("nM", [P, S], F32, mls)
        nMd = sb("nMd", [P, S], F32, mls)
        emm = sb("emm", [P, S], F32, mls)
        Dm = sb("Dm", [P, 2, S], F32, mls)
        sT = sb("sT", [P, 2, S], F32, mls)
        hm = sb("hm", [P, 2, S], F32, mls)
        hsq = cv
        so = sb("so", [P, 2, S], F32, mls)
        mxr = sb("mxr", [P, 2, S], F32, mls)
        hn = mxr
        hrs = emm
        mls.close()
        ybh = sb("ybh", [P, KC, S], F32R, mix)
        ybl = sb("ybl", [P, KC, S], F32R, mix)
        fox = ExitStack()
        fraw = sb("fraw", [P, 2, S], F32, fox)
        fsq = sb("fsq", [P, 2, S], F32, fox)
        frs = sb("frs", [P, 2, S], F32, fox)
        fq = sb("fq", [P, 2, S], F32, fox)
        fk = sb("fk", [P, 2, S], F32, fox)
        fvraw = sb("fvraw", [P, S], F32, fox)
        fv = sb("fv", [P, NB, P], F32, fox)
        fprob = sb("fprob", [P, 2, S], F32, fox)
        fpT = sb("fpT", [P, 2, S], F32, fox)
        fox.close()
        mgh = sb("mgh", [P, KC, S], F32R, mix)
        mgl = sb("mgl", [P, KC, S], F32R, mix)
        sg = sb("sg", [P, 2, S], F32, mix)
        br = sb("br", [P, 2, S], F32, mix)
        mg = sb("mg", [P, 1, S], F32, mix)
        mix.close()

        bank = [ctx.enter_context(nc.psum_tensor(f"bank{i}", [P, S], F32)) for i in range(8)]
        proj = bank[0:2]

        def c1(name, i=0, rows=slice(0, P)):
            if isinstance(i, int):
                return col[rows, COL[name] + i:COL[name] + i + 1]
            return col[rows, bass.ds(i + COL[name], 1)]

        def chunk(t, m):
            flat = t[:].rearrange("p c s -> p (c s)") if len(t.shape) == 3 else t
            return flat[:, m * S:m * S + S] if isinstance(m, int) else flat[:, bass.ds(m * S, S)]

        BESIDE = ((0, 0, 4), (0, 4, 8), (1, 0, 3), (1, 3, 6), (1, 6, 8), (2, 0, 2), (2, 2, 4), (2, 4, 8))
        QT = 1 + AH // 2

        def keys(b):
            return max(0, b - 1), min(NB - 1, b + 1)

        def window(k):
            lo, hi = keys(k % NB)
            return (hi - lo + 1) * P

        block = ctx.enter_context(nc.Block())

        @block.sync
        def _(sp):
            for name in PRIMED:
                sp.sem_inc(sem(name), 1)
            sp.dma_start(col[:], cols_in).then_inc(sem("cols_in"), 16)
            for c in range(2):
                sp.dma_start(h[:, c * 4 * S:(c + 1) * 4 * S], x_in[:, c * 4 * S:(c + 1) * 4 * S]).then_inc(sem(f"x_in{c}"), 16)

            def load(n, s, src, width):
                if not isinstance(n, int) or n >= 2:
                    sp.wait_ge(sem("w_lo"), primed(n - 1))
                sp.dma_start(raw[:, s, 0:width], src).then_inc(sem(f"raw_in{s}"), 16)

            def downs_before(n0):
                return sum(N_DOWN for d in ("down0", "down1", "down2") if SLAB[d] < n0)

            def load_wide(i, per, n0, k):
                n = n0 - downs_before(n0) + k
                src = w_in[n] if i is None else w_in[bass.ds(i * per + n, 1)].rearrange("a p n -> (a p) n")
                load(n0 + k if i is None else i * per + (n0 + k), (n0 + k) % 2, src, WC)

            def wide_loop(n0, pairs):
                with sp.Fori(0, pairs) as i:
                    for k in range(2):
                        load_wide(i, 2, n0, k)

            def down_loop(run):
                n0 = SLAB[f"down{run}"]
                with sp.Fori(0, N_DOWN // 2) as i:
                    for k in range(2):
                        load(i * 2 + (n0 + k), k,
                             wd_in[bass.ds(i * 2 + (run * N_DOWN + k), 1)].rearrange("a p n -> (a p) n"), DC)

            for k in range(2):
                load_wide(None, 2, 0, k)
            sp.dma_start(gates_raw[:], gates_in).then_inc(sem("gates_in"), 16)
            wide_loop(2, (SLAB["ff0"] - 2) // 2)

            for s in range(4):
                load_wide(None, 4, SLAB["ff0"], s)
            with sp.Fori(0, NMOD) as i:
                for s in range(4):
                    load_wide(i, 4, SLAB["ff0"] + 4, s)
                    for k in range(2 * s, 2 * s + 2):
                        if k == 0:
                            sp.wait_ge(sem("mm_done"), SLAB["ff0"])
                        sp.wait_ge(sem("ada_acc"), primed(i * KC + max(k - 1, 0)))
                        sp.dma_start(adaw[:, k % 2, :], ada_in[bass.ds(i * KC + k, 1)].rearrange("a p n -> (a p) n")
                                     ).then_inc(sem(f"ada_in{k % 2}"), 16)
            wide_loop(SLAB["ff0"] + 4 * (NMOD + 1), (N_FF - 4 * (NMOD + 1)) // 2)
            down_loop(0)
            wide_loop(SLAB["ff1"], N_FF // 2)
            down_loop(1)
            wide_loop(SLAB["mlstm"], (SLAB["down2"] - SLAB["mlstm"]) // 2)
            down_loop(2)
            base = TILE["down2"] // 2
            with sp.Fori(0, KC // 2) as i:
                for s in range(2):
                    sp.wait_ge(sem(f"evac{s}"), primed(i + (base + 1)))
                    sp.dma_start(out[:, bass.ds(i * (2 * S) + s * S, S)], chunk(h, i * 2 + s)).then_inc(sem("stored"), 16)
            sp.wait_ge(sem("stored"), 16 * KC)

        @block.gpsimd
        def _(pool):
            def low_loop(n0, count, width):
                with pool.Fori(0, count // 2) as i:
                    for s in range(2):
                        pool.wait_ge(sem("w_hi"), i * 2 + (n0 + s + 1))
                        nc.gpsimd.tensor_tensor(wlo[:, s, 0:width], raw[:, s, 0:width], whi[:, s, 0:width].bitcast(F32),
                                                ALU.subtract).then_inc(sem("w_lo"), 1)

            low_loop(0, SLAB["down0"], WC)
            low_loop(SLAB["down0"], N_DOWN, DC)
            low_loop(SLAB["ff1"], N_FF, WC)
            low_loop(SLAB["down1"], N_DOWN, DC)
            low_loop(SLAB["mlstm"], SLAB["down2"] - SLAB["mlstm"], WC)
            low_loop(SLAB["down2"], N_DOWN, DC)

        @block.tensor
        def _(pe):
            def slab(n, s, b, uses, ih, il, chunks, first=True, last=True, ready=None, part=None):
                lo, hi = part or (0, len(chunks))
                if lo == 0:
                    pe.wait_ge(sem("w_lo"), primed(n + 1))
                if lo == 0 and first:
                    pe.wait_ge(sem(f"evac{b}"), primed(uses))
                for j in range(lo, hi):
                    k = chunks[j]
                    if ready:
                        pe.wait_ge(sem(ready[0]), primed(ready[1] + k + 1))
                    W = slice(j * P, j * P + P)
                    for a, (w, v) in enumerate(((whi, ih), (whi, il), (wlo, ih))):
                        mm = nc.tensor.matmul(proj[b][:], w[:, s, W], v[:, k, :], start=first and j == 0 and a == 0,
                                              stop=last and j == len(chunks) - 1 and a == 2, skip_group_check=True)
                if hi == len(chunks):
                    mm.then_inc(sem("mm_done"), 1)

            def wide(name, i, per, s, ready=None, ih=xh, il=xl, part=None):
                slab(i * per + (SLAB[name] + s), s % 2, s % 2, i * (per // 2) + (TILE[name] + s) // 2, ih, il,
                     range(KC), ready=ready, part=part)

            def norm_sum(r):
                pe.wait_ge(sem("ssum"), primed(KC * (r + 1)))
                nc.tensor.matmul(bank[4][:], ones[:], ssum[:], start=True, stop=True).then_inc(sem("norm_sum"), 1)

            def down(run):
                with pe.Fori(0, KC // 2) as i:
                    for s in range(2):
                        for f in range(2):
                            n = i * 4 + (SLAB[f"down{run}"] + 2 * s + f)
                            slab(n, f, s, i + (TILE[f"down{run}"] + s) // 2, acth, actl,
                                 range(f * HALF, f * HALF + HALF), first=f == 0, last=f == 1,
                                 ready=("act_lo", run * FC))

            def transpose_values(src, dst_bank, done):
                for b in range(NB):
                    tr = nc.tensor.transpose(dst_bank[:, b * P:(b + 1) * P], src[:, b * P:(b + 1) * P], ident[:])
                tr.then_inc(sem(done), 1)

            pe.wait_ge(sem("const_ready"), 1)
            norm_sum(0)

            def sums_and_turn(p):
                pe.wait_ge(sem(f"evac{p % 2}"), primed(p // 2 + 1))
                pe.wait_ge(sem("rope_out"), primed(p))
                nc.tensor.matmul(bank[5][:], blk[:], rsq[:], start=True, stop=True).then_inc(sem("rope_ss"), 1)
                nc.tensor.matmul(bank[6][:], rot[:], rraw[:, p % 2, :], start=True, stop=True).then_inc(sem("rope_rot"), 1)

            def win_scores(t, k):
                e, b = k // NB, k % NB
                lo, hi = keys(b)
                H = slice(e * DH, e * DH + DH)
                if k == 0:
                    pe.wait_ge(sem("q_cur"), t + 1)
                if k >= 2:
                    pe.wait_ge(sem("probs"), t * 8 + (k - 1))
                elif not isinstance(t, int) or t > 0:
                    pe.wait_ge(sem("ret_decayed"), t * 8 + (k - 1))
                dst = bank[2 + k % 2]
                W = window(k)
                mm = nc.tensor.matmul(dst[:, 0:W], qf[H, b * P:(b + 1) * P], kf[H, lo * P:(hi + 1) * P], start=True, stop=False,
                                      skip_group_check=True)
                if b > 0:
                    mm = nc.tensor.matmul(dst[:, 0:P], identb[:], geb[:], start=False, stop=b == NB - 1, skip_group_check=True)
                if b < NB - 1:
                    mm = nc.tensor.matmul(dst[:, W - P:W], identb[:], leb[:], start=False, stop=True, skip_group_check=True)
                mm.then_inc(sem("scores"), 1)

            def win_turn(t, k):
                pe.wait_ge(sem("probs_scaled"), primed(t * 8 + (k + 1)))
                if k >= 2:
                    pe.wait_ge(sem("pT_copied"), t * 8 + (k - 1))
                else:
                    pe.wait_ge(sem("rope_out"), primed(t * 2 + QT))
                for j in range(window(k) // P):
                    tr = nc.tensor.transpose(bank[5 + k % 2][:, j * P:(j + 1) * P], prob[:, k % 2, j * P:(j + 1) * P], ident[:])
                tr.then_inc(sem("pT_ready"), 1)

            def win_values(t, k):
                e, b = k // NB, k % NB
                lo, hi = keys(b)
                H = slice(e * DH, e * DH + DH)
                pe.wait_ge(sem("pT_copied"), t * 8 + (k + 1))
                if k == 0:
                    pe.wait_ge(sem("y_lo"), primed(t * 2))
                    pe.wait_ge(sem("vtok"), t + 1)
                for j in range(hi - lo + 1):
                    mm = nc.tensor.matmul(bank[7][H, b * P:(b + 1) * P], vtok[:, lo + j, H], pT[:, k % 2, j * P:(j + 1) * P],
                                          start=j == 0, stop=j == hi - lo, skip_group_check=True)
                mm.then_inc(sem("values"), 1)

            def ret_turn(t, j):
                pe.wait_ge(sem(f"evac{j}"), primed(t * 2 + (TILE["ret"] // 2 + 1)))
                pe.wait_ge(sem("rope_out"), primed(t * 2 + (QT + j)))
                nc.tensor.matmul(bank[4][:], rot[:], rraw[:, j, :], start=True, stop=True).then_inc(sem("rope_rot"), 1)

            def ret_scores(t, k):
                e, b = k // NB, k % NB
                H = slice(e * DH, e * DH + DH)
                if k >= 2:
                    pe.wait_ge(sem("ret_decayed"), t * 8 + (k - 1))
                nc.tensor.matmul(bank[2 + k % 2][:], rkf[H, b * P:(b + 1) * P], rqf[H, :], start=True, stop=True,
                                 skip_group_check=True).then_inc(sem("ret_scores"), 1)

            def ret_values(t, k):
                e, b = k // NB, k % NB
                H = slice(e * DH, e * DH + DH)
                pe.wait_ge(sem("ret_decayed"), t * 8 + (k + 1))
                if k == 0:
                    pe.wait_ge(sem("vtok"), t + 2)
                nc.tensor.matmul(bank[4][H, :], rvtok[:, b, H], prob[:, k % 2, :], start=b == 0, stop=b == NB - 1,
                                 skip_group_check=True).then_inc(sem("ret_values"), 1)

            def mixing_step(t, more=True):
                for k in range(8):
                    win_turn(t, k)
                    if k + 2 < 8:
                        win_scores(t, k + 2)
                    if k == 3:
                        ret_turn(t, 0)
                    j, lo, hi = BESIDE[k]
                    wide("ret", t, 4, j, part=(lo, hi))
                    if k == 5:
                        ret_turn(t, 1)
                    win_values(t, k)
                wide("ret", t, 4, 3)
                pe.wait_ge(sem("rope_out"), primed(t * 2 + (QT + 2)))
                ret_scores(t, 0)
                ret_scores(t, 1)
                pe.wait_ge(sem("evac0"), primed(t * 2 + (TILE["ret"] // 2 + 2)))
                transpose_values(vraw, bank[4], "vT")
                for k in range(8):
                    ret_values(t, k)
                    if k + 2 < 8:
                        ret_scores(t, k + 2)
                    elif more:
                        win_scores(t + 1, k - 6)
                pe.wait_ge(sem("ret_sq"), t + 1)
                nc.tensor.matmul(bank[7][:], blk[:], rsq[:], start=True, stop=True).then_inc(sem("ret_ss"), 1)

            for p in range(N_ATT):
                wide("att", 0, 2, p, ready=("x_lo", 0) if p == 0 else None, part=(0, KC // 2))
                if p > 0:
                    sums_and_turn(p - 1)
                if p == N_ATT - 1:
                    win_scores(0, 0)
                    win_scores(0, 1)
                wide("att", 0, 2, p, ready=("x_lo", 0) if p == 0 else None, part=(KC // 2, KC))
            pe.wait_ge(sem("evac1"), primed(N_ATT // 2))
            transpose_values(vraw, bank[4], "vT")
            with pe.Fori(0, AH // 2 - 1) as t:
                mixing_step(t)
            mixing_step(AH // 2 - 1, more=False)

            with pe.Fori(0, N_OUT // 2) as i:
                for s in range(2):
                    wide("out", i, 2, s, ready=("y_lo", 0), ih=yh, il=yl)
            norm_sum(1)

            def mod_sum(i):
                pe.wait_ge(sem("ada_acc"), primed(i * KC + KC))
                for c in range(KC):
                    mm = nc.tensor.matmul(bank[2][:, c:c + 1], adac[:, c * P:(c + 1) * P], ones[:, 0:1], start=True, stop=True,
                                          skip_group_check=True)
                mm.then_inc(sem("mod_sum"), 1)

            def ff_step(run, i, i0, mod=None):
                for s in range(4):
                    if s == 2 and mod is not None:
                        mod_sum(mod)
                    n = SLAB[f"ff{run}"] + 4 * i0 + s
                    slab(i * 4 + n, s % 2, s % 2, i * 2 + (TILE[f"ff{run}"] + 4 * i0 + s) // 2, xh, xl, range(KC),
                         ready=("x_lo", KC * NORM[run]) if s == 0 else None)

            NORM = (1, 2, 4)
            ff_step(0, 0, 0)
            with pe.Fori(0, NMOD) as i:
                ff_step(0, i, 1, mod=i)
            ff_step(0, 0, NMOD + 1)
            down(0)

            norm_sum(2)
            with pe.Fori(0, FC // 2) as i:
                ff_step(1, i, 0)
            down(1)
            norm_sum(3)

            pe.wait_ge(sem("gates_split"), 2)
            for k in range(KC):
                pe.wait_ge(sem("x_lo"), primed(KC * 3 + k + 1))
                for a, (w, v) in enumerate(((ghi, xh), (ghi, xl), (glo, xh))):
                    mm = nc.tensor.matmul(bank[4][0:96, :], w[:, k * 96:(k + 1) * 96], v[:, k, :], start=k == 0 and a == 0,
                                          stop=k == KC - 1 and a == 2)
            mm.then_inc(sem("gates"), 1)

            def mlstm_units(hd):
                def scores(b):
                    if b >= 2:
                        pe.wait_ge(sem("m_weighted"), primed(hd * NB + (b - 1)))
                    nc.tensor.matmul(bank[2 + b % 2][:, 0:S - b * P], qk[:, 1, b * P:(b + 1) * P], qk[:, 0, b * P:S],
                                     start=True, stop=True).then_inc(sem("m_scores"), 1)

                def values(b):
                    pe.wait_ge(sem("m_weighted"), primed(hd * NB + (b + 1)))
                    if b == 0:
                        pe.wait_ge(sem("m_out"), primed(hd * 2))
                    for j in range(3):
                        w = mv[:, b, j * P:(j + 1) * P] if j < 2 else ones[:]
                        mm = nc.tensor.matmul(bank[5 + j][:, b * P:S], w, sT[:, b % 2, 0:S - b * P], start=b == 0, stop=b == NB - 1,
                                              skip_group_check=True)
                    mm.then_inc(sem("m_values"), 1)

                scores(0)
                scores(1)
                for b in range(NB):
                    values(b)
                    if b + 2 < NB:
                        scores(b + 2)

            with pe.Fori(0, MH) as hd:
                for s in range(4):
                    wide("mlstm", hd, 6, s)
                pe.wait_ge(sem("sel_ready"), FH)
                pe.wait_ge(sem("m_rows"), 6)
                nc.tensor.matmul(bank[4][:], sel[:, bass.ds(hd, 1), :].rearrange("p a n -> p (a n)"), msM[:], start=True,
                                 stop=True).then_inc(sem("m_bcast"), 1)
                for b in range(NB):
                    tr = nc.tensor.transpose(bank[7][:, b * MH:(b + 1) * MH], arow[:, b * P:(b + 1) * P], ident[0:MH, 0:MH])
                tr.then_inc(sem("m_acol"), 1)
                for j in range(2):
                    pe.wait_ge(sem(f"evac{j}"), primed(hd * 3 + (TILE["mlstm"] // 2 + 2)))
                    transpose_values(mvT[:, j, :], bank[2 + j], "m_turned")
                pe.wait_ge(sem("m_nM"), hd + 1)
                nc.tensor.matmul(bank[4][:], sel[:, bass.ds(hd, 1), :].rearrange("p a n -> p (a n)"), msm[:], start=True,
                                 stop=True).then_inc(sem("m_bcast"), 1)
                pe.wait_ge(sem("m_acols"), hd + 1)
                pe.wait_ge(sem("m_qk"), primed(hd * 2 + 2))
                pe.wait_ge(sem("m_v"), hd * 2 + 2)
                mlstm_units(hd)
                wide("mlstm", hd, 6, 4)
                pe.wait_ge(sem("m_sq"), hd + 1)
                nc.tensor.matmul(bank[4][:], ones[:], hsq[:, 0, :], start=True, stop=False)
                nc.tensor.matmul(bank[4][:], ones[:], hsq[:, 1, :], start=False, stop=True).then_inc(sem("m_ss"), 1)
                wide("mlstm", hd, 6, 5)

            UA = AH * NB

            def fox_scores(t, tt, k):
                e, b = k // NB, k % NB
                H = slice(e * DH, e * DH + DH)
                W = (b + 1) * P
                pe.wait_ge(sem("probs"), t * 8 + (UA + k - 1))
                if k == 0:
                    pe.wait_ge(sem("f_qk"), primed(t * 2 + 2))
                dst = bank[2 + k % 2]
                nc.tensor.matmul(dst[:, 0:W], fq[H, tt, b * P:W], fk[H, tt, 0:W], start=True, stop=False, skip_group_check=True)
                nc.tensor.matmul(dst[:, 0:W], sel[:, bass.ds(t * 2 + e, 1), :].rearrange("p a n -> p (a n)"), fsp[:, 0:W],
                                 start=False, stop=False, skip_group_check=True)
                nc.tensor.matmul(dst[:, W - P:W], identb[:], leb[:], start=False, stop=True,
                                 skip_group_check=True).then_inc(sem("scores"), 1)

            def fox_turn(t, k):
                b = k % NB
                pe.wait_ge(sem("probs_scaled"), primed(t * 8 + (UA + k + 1)))
                pe.wait_ge(sem("pT_copied"), t * 8 + (UA + k - 1))
                for j in range(b + 1):
                    tr = nc.tensor.transpose(bank[5 + k % 2][:, j * P:(j + 1) * P], fprob[:, k % 2, j * P:(j + 1) * P], ident[:])
                tr.then_inc(sem("pT_ready"), 1)

            def fox_values(t, k):
                e, b = k // NB, k % NB
                H = slice(e * DH, e * DH + DH)
                pe.wait_ge(sem("pT_copied"), t * 8 + (UA + k + 1))
                if k == 0:
                    pe.wait_ge(sem("f_v"), t + 1)
                    pe.wait_ge(sem("yb_lo"), primed(t))
                for j in range(b + 1):
                    mm = nc.tensor.matmul(bank[7][H, b * P:(b + 1) * P], fv[:, j, H], fpT[:, k % 2, j * P:(j + 1) * P],
                                          start=j == 0, stop=j == b, skip_group_check=True)
                mm.then_inc(sem("values"), 1)

            def fox_sums(p, i, s, j):
                pe.wait_ge(sem(f"evac{s % 2}"), primed(i * 3 + (TILE["fox"] + s) // 2 + 1))
                if j == 1:
                    pe.wait_ge(sem("f_ln"), p * 2 + 1)
                nc.tensor.matmul(bank[4][:], blk[:], fsq[:, j, :], start=True, stop=True).then_inc(sem("f_ss"), 1)

            def fox_turn_values(t, i, s):
                pe.wait_ge(sem(f"evac{s % 2}"), primed(i * 3 + (TILE["fox"] + s) // 2 + 1))
                transpose_values(fvraw, bank[4], "f_vT")

            def fox_pair(i, tt, more=True):
                t = i * 2 + tt
                for k in range(8):
                    fox_turn(t, k)
                    if k + 2 < 8:
                        fox_scores(t, tt, k + 2)
                    if k == 0:
                        fox_turn_values(t, i, 3 * tt + 2)
                    if more:
                        s = 3 * tt + 3
                        if k == 3:
                            fox_sums(t + 1, i, s, 0)
                        j, lo, hi = BESIDE[k]
                        wide("fox", i, 6, s + j, part=(lo, hi))
                        if k == 5:
                            fox_sums(t + 1, i, s + 1, 1)
                    fox_values(t, k)
                    if more and k >= 6:
                        fox_scores(t + 1, 1 - tt, k - 6)

            for s in range(3):
                wide("fox", 0, 6, s)
                if s > 0:
                    fox_sums(0, 0, s - 1, s - 1)
            pe.wait_ge(sem("f_rows"), 3)
            fox_scores(0, 0, 0)
            fox_scores(0, 0, 1)
            with pe.Fori(0, FH // 4 - 1) as i:
                for tt in range(2):
                    fox_pair(i, tt)
            fox_pair(FH // 4 - 1, 0)
            fox_pair(FH // 4 - 1, 1, more=False)

            with pe.Fori(0, KC) as m:
                wide("merge", m, 4, 0)
                wide("merge", m, 4, 1, ih=yah, il=yal, ready=("m_y", 0))
                wide("merge", m, 4, 2)
                wide("merge", m, 4, 3, ih=ybh, il=ybl, ready=("yb_lo", 0))
            with pe.Fori(0, N_OUT // 2) as i:
                for s in range(2):
                    wide("out2", i, 2, s, ih=mgh, il=mgl, ready=("mg_lo", 0))
            norm_sum(4)
            with pe.Fori(0, FC // 2) as i:
                ff_step(2, i, 0)
            down(2)

        @block.scalar
        def _(act):
            def split(i, per, n0, k, width):
                s = (n0 + k) % 2
                act.wait_ge(sem(f"raw_in{s}"), i * (8 * per) + ((n0 + k) // 2 * 16 + 16))
                if not isinstance(i, int) or i * per + n0 + k >= 2:
                    act.wait_ge(sem("mm_done"), i * per + (n0 + k - 1))
                nc.scalar.activation(whi[:, s, 0:width], raw[:, s, 0:width], ACT.Copy).then_inc(sem("w_hi"), 1)

            def width(name):
                return DC if name.startswith("down") else WC

            def steps(name, per, count, body, after=None, i0=0):
                def ahead_in(i, last):
                    def ahead(k):
                        if last and k >= per - 2:
                            if after:
                                split(0, 2, SLAB[after], k - (per - 2), width(after))
                        else:
                            split(i, per, SLAB[name] + i0 * per + 2, k, width(name))
                    return ahead

                with act.Fori(0, count - 1) as i:
                    body(i, ahead_in(i, False))
                body(count - 1, ahead_in(count - 1, True))

            def matmuls(n):
                act.wait_ge(sem("mm_done"), n)

            def square_chunk(r, m, k):
                if r > 0 or m > 0:
                    act.wait_ge(sem("ssum"), primed(m + (KC * r - 1)))
                nc.scalar.activation(sqn[:, k, :], chunk(h, m), ACT.Square).then_inc(sem("sq"), 1)

            def inverse_root(name, i, src, dst, width):
                nc.scalar.activation(dst, src, ACT.Ln, scale=1.0 / width, bias=epsc[:]).then_inc(sem(name + "_ln"), 1)
                act.wait_ge(sem(name + "_ln"), i + 1)
                nc.scalar.activation(dst, dst, ACT.Exp, scale=-0.5).then_inc(sem(name + "_rstd"), 1)

            def norm(r, shift=None):
                act.preload_act_table_set("natural_log_exp_and_others")
                act.wait_ge(sem("norm_sum"), primed(r + 1))
                inverse_root("norm", r, bank[4][:], rstd[:], D)
                for c in range(KC):
                    act.wait_ge(sem("x_scaled"), KC * r + c + 1)
                    if shift is None:
                        nc.scalar.activation(xh[:, c, :], tmp[:, c % 2, :], ACT.Copy).then_inc(sem("x_hi"), 1)
                    else:
                        nc.scalar.activation(xh[:, c, :], tmp[:, c % 2, :], ACT.Identity,
                                             bias=modc[:, shift * KC + c:shift * KC + c + 1]).then_inc(sem("x_hi"), 1)

            for dst, at, n in ((ident, 0, P), (blk, P, P), (rot, 2 * P, P), (ge, 3 * P, P), (leconst, 4 * P, P),
                               (cos, 5 * P, S), (sin, 5 * P + S, S)):
                act.dma_start(dst[:], const_in[:, at:at + n]).then_inc(sem("const_in"), 16)
            act.dma_start(rel[:], rel_in).then_inc(sem("rel_in"), 16)
            act.wait_ge(sem("cols_in"), 16)
            nc.scalar.activation(csil[:], col[:, COL["c"]:COL["c"] + KC], ACT.Silu).then_inc(sem("c_silu"), 1)
            act.wait_ge(sem("eps"), 1)
            for c in range(KC):
                if c % 4 == 0:
                    act.wait_ge(sem(f"x_in{c // 4}"), 16)
                square_chunk(0, c, c % 2)
            for k in range(2):
                split(0, 2, 0, k, WC)
            norm(0)

            def rope_tile(p):
                matmuls(p + 1)
                act.wait_ge(sem("rope_out"), primed(max(p - 1, 0)))
                nc.scalar.activation(rsq[:], proj[p % 2][:], ACT.Square)
                nc.scalar.activation(rraw[:, p % 2, :], proj[p % 2][:], ACT.Identity,
                                     scale=c1("q_norm" if p else "k_norm")).then_inc(sem(f"evac{p % 2}"), 1)
                split(0, 2, 0, p + 2, WC)

            def rope_roots(p):
                act.wait_ge(sem("rope_ss"), p + 1)
                if p > 0:
                    act.wait_ge(sem("rope_out"), primed(p))
                inverse_root("rope", p, bank[5][:], rr[:], DH)

            def win_exps(t, k):
                e = k // NB
                act.wait_ge(sem("negmax"), t * 8 + (k + 1))
                if k >= 2:
                    act.wait_ge(sem("pT_ready"), t * 8 + (k - 1))
                st = stat[:, k % 2, :]
                nc.scalar.activation(prob[:, k % 2, 0:window(k)], bank[2 + k % 2][:, 0:window(k)], ACT.Exp, bias=st[:, 1:2],
                                     accum_out=st[:, 2:3]).then_inc(sem("probs"), 1)
                nc.scalar.activation(st[:, 3:4], c1("sink", t + e * (AH // 2)), ACT.Exp, bias=st[:, 1:2]).then_inc(sem("sink_exp"), 1)

            def win_copy(t, k):
                act.wait_ge(sem("pT_ready"), t * 8 + (k + 1))
                if k >= 2:
                    act.wait_ge(sem("values"), t * 8 + (k - 1))
                nc.scalar.activation(pT[:, k % 2, 0:window(k)], bank[5 + k % 2][:, 0:window(k)], ACT.Copy).then_inc(sem("pT_copied"), 1)

            def ret_decays(t):
                act.wait_ge(sem("decay_log"), t * 4 + 4)
                for e in range(2):
                    at, lo, hi = e * REL, S - P, S
                    fwd = lg[:, bass.ds(t * 2 + e, 1)]
                    bwd = lg[:, bass.ds(t * 2 + (RH + e), 1)]
                    nc.scalar.activation(decay[:, at:at + lo], rel[:, REL:REL + lo], ACT.Exp, scale=bwd)
                    nc.scalar.activation(decay[:, at + hi:at + REL], rel[:, hi:REL], ACT.Exp, scale=fwd)
                    nc.scalar.activation(decay[:, at + lo:at + hi], decay[:, at + lo:at + hi], ACT.Exp).then_inc(sem("decay"), 1)

            def ret_tile(t, j):
                matmuls(t * 4 + (SLAB["ret"] + j + 1))
                act.wait_ge(sem("rope_out"), primed(t * 2 + QT))
                nc.scalar.activation(rraw[:, j, :], proj[j][:], ACT.Copy, scale=DH ** -0.5 if j else 1.0).then_inc(sem(f"evac{j}"), 1)
                split(t, 4, SLAB["ret"], j + 2, WC)

            def mixing_step(t, more=True):
                n = SLAB["ret"]
                for k in range(8):
                    win_copy(t, k)
                    if k + 2 < 8:
                        win_exps(t, k + 2)
                    if k == 1:
                        ret_tile(t, 0)
                    if k == 2:
                        ret_decays(t)
                    if k == 4:
                        ret_tile(t, 1)
                act.wait_ge(sem("values"), t * 8 + 8)
                nc.scalar.activation(chunk(yh, t * 2), bank[7][:], ACT.Copy).then_inc(sem("y_hi"), 1)
                matmuls(t * 4 + (n + 3))
                nc.scalar.activation(vraw[:], proj[0][:], ACT.Copy).then_inc(sem("evac0"), 1)
                split(t, 4, n, 4, WC)
                act.preload_act_table(ACT.Silu)
                matmuls(t * 4 + (n + 4))
                nc.scalar.activation(rsil[:], proj[1][:], ACT.Silu).then_inc(sem("evac1"), 1)
                act.wait_ge(sem("vT"), t + 2)
                nc.scalar.activation(rvtok[:].rearrange("p b n -> p (b n)"), bank[4][:], ACT.Copy).then_inc(sem("vtok"), 1)
                split(t, 4, n, 5, WC)
                act.preload_act_table_set("natural_log_exp_and_others")
                if more:
                    win_exps(t + 1, 0)
                act.wait_ge(sem("ret_values"), t * 8 + 8)
                nc.scalar.activation(rsq[:], bank[4][:], ACT.Square).then_inc(sem("ret_sq"), 1)
                if more:
                    win_exps(t + 1, 1)
                act.wait_ge(sem("ret_ss"), t + 1)
                inverse_root("ret", t, bank[7][:], rr[:], DH)
                act.wait_ge(sem("ret_y"), t + 1)
                nc.scalar.activation(chunk(yh, t * 2 + 1), ry[:], ACT.Copy).then_inc(sem("y_hi"), 1)

            for p in range(QT):
                rope_tile(p)
                if p == QT - 1:
                    win_exps(0, 0)
                rope_roots(p)
            matmuls(N_ATT)
            nc.scalar.activation(vraw[:], proj[1][:], ACT.Copy).then_inc(sem("evac1"), 1)
            split(0, 2, 0, N_ATT + 1, WC)
            win_exps(0, 1)
            act.wait_ge(sem("vT"), 1)
            nc.scalar.activation(vtok[:].rearrange("p b n -> p (b n)"), bank[4][:], ACT.Copy).then_inc(sem("vtok"), 1)
            act.wait_ge(sem("rel_in"), 16)
            with act.Fori(0, AH // 2 - 1) as t:
                mixing_step(t)
            mixing_step(AH // 2 - 1, more=False)

            def square_added(r, name, q, i, s):
                act.wait_ge(sem(f"evac{s}"), primed(i + ((TILE[name] + s) // 2 + 1)))
                square_chunk(r, i * 2 + s, s)

            def out_step(r, name):
                def step(i, ahead):
                    for s in range(2):
                        ahead(s)
                        square_added(r, name, 0, i, s)
                return step

            def down_step(r, name):
                def step(i, ahead):
                    for s in range(2):
                        ahead(2 * s)
                        ahead(2 * s + 1)
                        if r is not None:
                            square_added(r, name, 0, i, s)
                return step

            def ff_step(run, i0):
                def step(i, ahead):
                    for jj in range(2):
                        matmuls(i * 4 + (SLAB[f"ff{run}"] + 4 * i0 + 2 * jj + 1))
                        nc.scalar.activation(gsil[:, jj, :], proj[0][:], ACT.Silu).then_inc(sem("evac0"), 1)
                        ahead(2 * jj)
                        ahead(2 * jj + 1)
                        j = i * 2 + (2 * i0 + jj)
                        act.wait_ge(sem("evac1"), primed(i * 2 + (TILE[f"ff{run}"] // 2 + 2 * i0 + jj + 1)))
                        nc.scalar.activation(chunk(acth, j), aprod[:, jj, :], ACT.Copy).then_inc(sem("act_hi"), 1)
                return step

            steps("out", 2, N_OUT // 2, out_step(1, "out"), "ff0")
            norm(1)
            act.preload_act_table(ACT.Silu)
            steps("ff0", 4, FC // 2, ff_step(0, 0), "down0")
            steps("down0", 4, N_DOWN // 4, down_step(2, "down0"), "ff1")

            norm(2, shift=0)
            act.preload_act_table(ACT.Silu)
            steps("ff1", 4, FC // 2, ff_step(1, 0), "down1")
            steps("down1", 4, N_DOWN // 4, down_step(3, "down1"), "mlstm")
            norm(3, shift=3)

            act.wait_ge(sem("gates"), 1)
            nc.scalar.activation(zg[:], bank[4][0:96, :], ACT.Identity, bias=c1("b_gates", rows=slice(0, 96))).then_inc(sem("gates_out"), 1)
            nc.scalar.activation(zi[:], bank[4][64:64 + MH, :], ACT.Identity,
                                 bias=c1("b_gates", rows=slice(64, 64 + MH))).then_inc(sem("gates_out"), 1)
            act.wait_ge(sem("g_abs"), 1)
            nc.scalar.activation(zt[0:48, :], zt[0:48, :], ACT.Exp, scale=-1.0).then_inc(sem("g_exp"), 1)
            act.wait_ge(sem("g_exp"), 1)
            nc.scalar.activation(zt[0:48, :], zt[0:48, :], ACT.Ln, bias=ones[0:48, 0:1]).then_inc(sem("g_ln"), 1)
            act.wait_ge(sem("rows_clear"), 3)
            for which, dst, rows, done in ((0, fsp, slice(32, 48), "f_rows"), (1, msM, slice(0, MH), "m_rows"),
                                           (2, msm, slice(0, MH), "m_rows")):
                act.wait_ge(sem("row_split"), primed(3 * which + 3))
                for j in range(3):
                    n = rows.stop - rows.start
                    nc.scalar.activation(dst[32 * j:32 * j + n, :], gsp[rows, j, :], ACT.Copy).then_inc(sem(done), 1)

            def mlstm_step(hd, ahead):
                n = SLAB["mlstm"]
                for j in range(2):
                    matmuls(hd * 6 + (n + j + 1))
                    act.wait_ge(sem("m_conv"), primed(hd * 2))
                    if j == 0:
                        act.wait_ge(sem("pads"), 1)
                    nc.scalar.activation(qz[:, j, CONV - 1:], proj[j][:], ACT.Identity, bias=c1("b_mlstm", hd * 6 + j)).then_inc(sem(f"evac{j}"), 1)
                    ahead(j)
                for j in range(2):
                    matmuls(hd * 6 + (n + j + 3))
                    act.wait_ge(sem("m_turned"), primed(hd * 2))
                    nc.scalar.activation(mvT[:, j, :], proj[j][:], ACT.Identity, bias=c1("b_mlstm", hd * 6 + (j + 2))).then_inc(sem(f"evac{j}"), 1)
                    ahead(j + 2)
                act.preload_act_table(ACT.Silu)
                for j in range(2):
                    act.wait_ge(sem("m_conv"), primed(hd * 2 + (j + 1)))
                    act.wait_ge(sem("m_values"), primed(hd * NB))
                    nc.scalar.activation(qk[:, j, :], cv[:, j, :], ACT.Silu).then_inc(sem("m_qk"), 1)
                act.wait_ge(sem("m_bcast"), hd * 2 + 1)
                act.wait_ge(sem("m_nMd"), primed(hd))
                nc.scalar.activation(nM[:], bank[4][:], ACT.Copy).then_inc(sem("m_nM"), 1)
                act.wait_ge(sem("m_acol"), hd + 1)
                nc.scalar.activation(acol[:], bank[7][:, 0:NB * MH], ACT.Copy).then_inc(sem("m_acols"), 1)
                for j in range(2):
                    act.wait_ge(sem("m_turned"), primed(hd * 2 + (j + 1)))
                    nc.scalar.activation(mv[:, :, j * P:(j + 1) * P], bank[2 + j][:].rearrange("p (b n) -> p b n", b=NB),
                                         ACT.Copy).then_inc(sem("m_v"), 1)
                act.preload_act_table_set("natural_log_exp_and_others")
                act.wait_ge(sem("m_bcast"), hd * 2 + 2)
                act.wait_ge(sem("m_out"), primed(hd * 2))
                nc.scalar.activation(emm[:], bank[4][:], ACT.Exp).then_inc(sem("m_emm"), 1)
                act.wait_ge(sem("m_nMd"), primed(hd + 1))
                act.wait_ge(sem("m_acols"), hd + 1)
                for b in range(NB):
                    act.wait_ge(sem("m_weighted"), primed(hd * NB + max(b - 1, 0)))
                    a = acol[:, bass.ds(hd + b * MH, 1)] if not isinstance(hd, int) else acol[:, hd + b * MH:hd + b * MH + 1]
                    if b < NB - 1:
                        nc.scalar.activation(Dm[:, b % 2, P:S - b * P], nM[:, (b + 1) * P:S], ACT.Exp, bias=a)
                    nc.scalar.activation(Dm[:, b % 2, 0:P], nMd[:, b * P:(b + 1) * P], ACT.Exp, bias=a).then_inc(sem("m_D"), 1)
                act.preload_act_table(ACT.Sigmoid)
                matmuls(hd * 6 + (n + 5))
                act.wait_ge(sem("m_y"), primed(hd * 2))
                nc.scalar.activation(so[:, 0, :], proj[0][:], ACT.Sigmoid, bias=c1("b_mlstm", hd * 6 + 4)).then_inc(sem("evac0"), 1)
                ahead(4)
                act.wait_ge(sem("m_out"), primed(hd * 2 + 2))
                nc.scalar.activation(hsq[:, 0, :], hm[:, 0, :], ACT.Square)
                nc.scalar.activation(hsq[:, 1, :], hm[:, 1, :], ACT.Square).then_inc(sem("m_sq"), 1)
                matmuls(hd * 6 + (n + 6))
                nc.scalar.activation(so[:, 1, :], proj[1][:], ACT.Sigmoid, bias=c1("b_mlstm", hd * 6 + 5)).then_inc(sem("evac1"), 1)
                ahead(5)
                act.preload_act_table_set("natural_log_exp_and_others")
                act.wait_ge(sem("m_ss"), hd + 1)
                inverse_root("m", hd, bank[4][:], hrs[:], DV)
                for j in range(2):
                    act.wait_ge(sem("m_gated"), hd * 2 + (j + 1))
                    nc.scalar.activation(chunk(yah, hd * 2 + j), hn[:, j, :], ACT.Copy).then_inc(sem("m_yhi"), 1)

            steps("mlstm", 6, MH, mlstm_step, "fox")

            UA = AH * NB

            def fox_exps(t, k):
                W = (k % NB + 1) * P
                act.wait_ge(sem("negmax"), t * 8 + (UA + k + 1))
                act.wait_ge(sem("pT_ready"), t * 8 + (UA + k - 1))
                st = stat[:, k % 2, :]
                nc.scalar.activation(fprob[:, k % 2, 0:W], bank[2 + k % 2][:, 0:W], ACT.Exp, bias=st[:, 1:2],
                                     accum_out=st[:, 2:3]).then_inc(sem("probs"), 1)

            def fox_copy(t, k):
                W = (k % NB + 1) * P
                act.wait_ge(sem("pT_ready"), t * 8 + (UA + k + 1))
                act.wait_ge(sem("values"), t * 8 + (UA + k - 1))
                nc.scalar.activation(fpT[:, k % 2, 0:W], bank[5 + k % 2][:, 0:W], ACT.Copy).then_inc(sem("pT_copied"), 1)

            def fox_tile(p, i, s, j):
                matmuls(i * 6 + (SLAB["fox"] + s + 1))
                act.wait_ge(sem("f_qk"), primed(p * 2))
                bias = c1("b_fox", i * 6 + s)
                nc.scalar.activation(fsq[:, j, :], proj[s % 2][:], ACT.Square, bias=bias)
                nc.scalar.activation(fraw[:, j, :], proj[s % 2][:], ACT.Identity, bias=bias).then_inc(sem(f"evac{s % 2}"), 1)
                split(i, 6, SLAB["fox"], s + 2, WC)

            def fox_values(i, s):
                matmuls(i * 6 + (SLAB["fox"] + s + 1))
                nc.scalar.activation(fvraw[:], proj[s % 2][:], ACT.Identity, bias=c1("b_fox", i * 6 + s)).then_inc(sem(f"evac{s % 2}"), 1)

            def fox_roots(p, j):
                act.wait_ge(sem("f_ss"), p * 2 + (j + 1))
                nc.scalar.activation(frs[:, j, :], bank[4][:], ACT.Ln, scale=1.0 / DH, bias=epsc[:]).then_inc(sem("f_ln"), 1)
                act.wait_ge(sem("f_ln"), p * 2 + (j + 1))
                nc.scalar.activation(frs[:, j, :], frs[:, j, :], ACT.Exp, scale=-0.5).then_inc(sem("f_rstd"), 1)

            def fox_pair(i, tt, more=True):
                t = i * 2 + tt
                s = 3 * tt + 3
                for k in range(8):
                    fox_copy(t, k)
                    if k == 0:
                        act.wait_ge(sem("f_vT"), t + 1)
                        nc.scalar.activation(fv[:].rearrange("p b n -> p (b n)"), bank[4][:], ACT.Copy).then_inc(sem("f_v"), 1)
                    if k + 2 < 8:
                        fox_exps(t, k + 2)
                    if more:
                        if k == 1:
                            fox_tile(t + 1, i, s, 0)
                        if k == 3:
                            fox_roots(t + 1, 0)
                        if k == 4:
                            fox_tile(t + 1, i, s + 1, 1)
                        if k == 5:
                            fox_roots(t + 1, 1)
                        if k == 7:
                            fox_exps(t + 1, 0)
                            fox_values(i, s + 2)
                act.wait_ge(sem("values"), t * 8 + (UA + 8))
                nc.scalar.activation(chunk(ybh, t), bank[7][:], ACT.Copy).then_inc(sem("yb_hi"), 1)
                if more:
                    fox_exps(t + 1, 1)
                    split(i, 6, SLAB["fox"], s + 4, WC)

            act.preload_act_table_set("natural_log_exp_and_others")
            fox_tile(0, 0, 0, 0)
            fox_tile(0, 0, 1, 1)
            fox_roots(0, 0)
            fox_values(0, 2)
            fox_roots(0, 1)
            split(0, 6, SLAB["fox"], 4, WC)
            fox_exps(0, 0)
            fox_exps(0, 1)
            with act.Fori(0, FH // 4 - 1) as i:
                for tt in range(2):
                    fox_pair(i, tt)
            fox_pair(FH // 4 - 1, 0)
            fox_pair(FH // 4 - 1, 1, more=False)

            def merge_step(m, ahead):
                n = SLAB["merge"]
                for j in range(2):
                    matmuls(m * 4 + (n + 2 * j + 1))
                    nc.scalar.activation(sg[:, j, :], proj[0][:], ACT.Sigmoid, bias=c1("b_merge", m * 2 + j)).then_inc(sem("evac0"), 1)
                    ahead(2 * j)
                    ahead(2 * j + 1)
                act.wait_ge(sem("mg"), primed(m + 1))
                nc.scalar.activation(chunk(mgh, m), mg[:, 0, :], ACT.Copy).then_inc(sem("mg_hi"), 1)

            act.preload_act_table(ACT.Sigmoid)
            steps("merge", 4, KC, merge_step, "out2")
            steps("out2", 2, N_OUT // 2, out_step(4, "out2"), "ff2")
            norm(4, shift=6)
            act.preload_act_table(ACT.Silu)
            steps("ff2", 4, FC // 2, ff_step(2, 0), "down2")
            steps("down2", 4, N_DOWN // 4, down_step(None, "down2"))

        @block.vector
        def _(dve):
            V = nc.vector

            def matmuls(n):
                dve.wait_ge(sem("mm_done"), n)

            V.memset(ones[:], 1.0)
            V.memset(epsc[:], EPS).then_inc(sem("eps"), 1)
            dve.wait_ge(sem("cols_in"), 16)
            V.tensor_scalar(lg[:], col[:, COL["decay_f"]:COL["decay_f"] + 2 * RH], -1.0, None, ALU.mult).then_inc(sem("lg"), 1)
            dve.wait_ge(sem("lg"), 1)
            V.tensor_tensor(lg[:], lg[:], col[:, COL["decay_f"]:COL["decay_f"] + 2 * RH], ALU.min).then_inc(sem("lg"), 1)
            V.tensor_scalar(c1("q_norm"), c1("q_norm"), DH ** -0.5, None, ALU.mult).then_inc(sem("q_scale"), 1)
            V.tensor_scalar(col[:, COL["fox_q"]:COL["fox_q"] + FH // 2], col[:, COL["fox_q"]:COL["fox_q"] + FH // 2], DH ** -0.5, None,
                            ALU.mult).then_inc(sem("q_scale"), 1)
            dve.wait_ge(sem("const_in"), 16 * 7)
            V.tensor_copy(identb[:], ident[:])
            V.tensor_copy(geb[:], ge[:])
            V.tensor_copy(leb[:], leconst[:]).then_inc(sem("const_ready"), 1)

            def add_square(r, m, k):
                dve.wait_ge(sem("sq"), m + (KC * r + 1))
                dve.wait_ge(sem("ssum"), primed(m + KC * r))
                V.tensor_tensor(ssum[:], ssum[:], sqn[:, k, :], ALU.add).then_inc(sem("ssum"), 1)

            def clear_sum(r):
                dve.wait_ge(sem("norm_sum"), primed(r))
                V.memset(ssum[:], 0.0).then_inc(sem("ssum_clear"), 1)
                dve.wait_ge(sem("ssum_clear"), r + 1)

            def norm(r, weight, shift=None):
                def scaled(c):
                    dve.wait_ge(sem("x_lo"), primed(KC * r + max(c - 1, 0)))
                    V.scalar_tensor_tensor(tmp[:, c % 2, :], chunk(h, c), weight(c), rstd[:], ALU.mult, ALU.mult).then_inc(sem("x_scaled"), 1)

                def low(c):
                    dve.wait_ge(sem("x_hi"), KC * r + c + 1)
                    sh = 0.0 if shift is None else modc[:, shift * KC + c:shift * KC + c + 1]
                    V.scalar_tensor_tensor(xl[:, c, :], tmp[:, c % 2, :], sh, xh[:, c, :].bitcast(F32), ALU.add,
                                           ALU.subtract).then_inc(sem("x_lo"), 1)

                dve.wait_ge(sem("norm_rstd"), r + 1)
                scaled(0)
                for c in range(KC):
                    if c + 1 < KC:
                        scaled(c + 1)
                    low(c)

            clear_sum(0)
            for c in range(KC):
                add_square(0, c, c % 2)
            norm(0, lambda c: c1("attn_norm", c))

            def roped(p, slot, turned):
                dve.wait_ge(sem("rope_rot"), p + 1)
                dve.wait_ge(sem("rope_out"), primed(p))
                V.tensor_tensor(rt[:, 0, :], bank[turned][:], sin[:], ALU.mult).then_inc(sem("rope_part"), 1)
                V.tensor_tensor(rt[:, 1, :], rraw[:, slot, :], cos[:], ALU.mult).then_inc(sem("rope_part"), 1)
                dve.wait_ge(sem("rope_part"), p * 2 + 2)

            def normed_rope(p, dst):
                roped(p, p % 2, 6)
                V.tensor_tensor(rt[:, 0, :], rt[:, 0, :], rt[:, 1, :], ALU.add).then_inc(sem("rope_sum"), 1)
                dve.wait_ge(sem("rope_sum"), p + 1)
                dve.wait_ge(sem("rope_rstd"), p + 1)
                V.tensor_tensor(dst, rt[:, 0, :], rr[:], ALU.mult).then_inc(sem("rope_out"), 1)

            def ret_rope(t, j):
                p = t * 2 + (QT + j)
                roped(p, j, 4)
                V.tensor_tensor((rqf, rkf)[j][:], rt[:, 0, :], rt[:, 1, :], ALU.add).then_inc(sem("rope_out"), 1)

            def queries(t):
                V.tensor_copy(qf[:], chunk(qall, t)).then_inc(sem("q_cur"), 1)

            def maxima(u, k, width, sink=None):
                st = stat[:, k % 2, :]
                dve.wait_ge(sem("scores"), u + (k + 1))
                if not isinstance(u, int) or u + k > 0:
                    dve.wait_ge(sem("probs_scaled"), primed(u + (k - 1)))
                V.tensor_reduce(st[:, 0:1], bank[2 + k % 2][:, 0:width], AX.X, ALU.max).then_inc(sem("rowmax"), 1)
                dve.wait_ge(sem("rowmax"), u + (k + 1))
                if sink is not None:
                    V.tensor_scalar(st[:, 1:2], st[:, 0:1], sink, -1.0, ALU.max, ALU.mult).then_inc(sem("negmax"), 1)
                else:
                    V.tensor_scalar(st[:, 1:2], st[:, 0:1], -1.0, None, ALU.mult).then_inc(sem("negmax"), 1)

            def win_maxima(t, k):
                maxima(t * 8, k, window(k), c1("sink", t + (k // NB) * (AH // 2)))

            def win_scale(t, k):
                st = stat[:, k % 2, :]
                W = window(k)
                dve.wait_ge(sem("sink_exp"), t * 8 + (k + 1))
                V.tensor_tensor(st[:, 4:5], st[:, 2:3], st[:, 3:4], ALU.add).then_inc(sem("den"), 1)
                dve.wait_ge(sem("den"), t * 8 + (k + 1))
                V.reciprocal(st[:, 5:6], st[:, 4:5]).then_inc(sem("rden"), 1)
                dve.wait_ge(sem("rden"), t * 8 + (k + 1))
                V.tensor_scalar(prob[:, k % 2, 0:W], prob[:, k % 2, 0:W], st[:, 5:6], None, ALU.mult).then_inc(sem("probs_scaled"), 1)

            def ret_decay_logs(t):
                bands = [decay[:, e * REL + S - P:e * REL + S] for e in range(2)]
                for e in range(2):
                    V.tensor_scalar(bands[e], rel[:, S - P:S], lg[:, bass.ds(t * 2 + e, 1)], None, ALU.mult).then_inc(sem("decay_log"), 1)
                for e in range(2):
                    dve.wait_ge(sem("decay_log"), t * 4 + 2)
                    V.scalar_tensor_tensor(bands[e], rel[:, REL + S - P:REL + S], lg[:, bass.ds(t * 2 + (RH + e), 1)], bands[e], ALU.mult,
                                           ALU.add).then_inc(sem("decay_log"), 1)

            def mixing_step(t, more=True):
                ret_decay_logs(t)
                for k in range(8):
                    if k > 0:
                        win_scale(t, k)
                    if k + 2 < 8:
                        win_maxima(t, k + 2)
                    if k in (4, 6):
                        ret_rope(t, (k - 4) // 2)
                if more:
                    queries(t + 1)
                dve.wait_ge(sem("y_hi"), t * 2 + 1)
                V.tensor_tensor(chunk(yl, t * 2), bank[7][:], chunk(yh, t * 2).bitcast(F32), ALU.subtract).then_inc(sem("y_lo"), 1)
                dve.wait_ge(sem("decay"), t * 2 + 2)
                for k in range(8):
                    e, b = k // NB, k % NB
                    at = e * REL + S - P - b * P
                    dve.wait_ge(sem("ret_scores"), t * 8 + (k + 1))
                    if k >= 2:
                        dve.wait_ge(sem("ret_values"), t * 8 + (k - 1))
                    V.tensor_tensor(prob[:, k % 2, :], bank[2 + k % 2][:], decay[:, at:at + S], ALU.mult).then_inc(sem("ret_decayed"), 1)
                if more:
                    win_maxima(t + 1, 0)
                    win_scale(t + 1, 0)
                    win_maxima(t + 1, 1)
                dve.wait_ge(sem("ret_rstd"), t + 1)
                V.tensor_tensor(ry[:], bank[4][:], rr[:], ALU.mult).then_inc(sem("ret_normed"), 1)
                dve.wait_ge(sem("ret_normed"), t + 1)
                V.scalar_tensor_tensor(ry[:], ry[:], c1("ret_norm", t), rsil[:], ALU.mult, ALU.mult).then_inc(sem("ret_y"), 1)
                dve.wait_ge(sem("y_hi"), t * 2 + 2)
                V.tensor_tensor(chunk(yl, t * 2 + 1), ry[:], chunk(yh, t * 2 + 1).bitcast(F32), ALU.subtract).then_inc(sem("y_lo"), 1)

            dve.wait_ge(sem("lg"), 2)
            for p in range(QT):
                if p == QT - 1:
                    win_maxima(0, 0)
                    win_maxima(0, 1)
                    win_scale(0, 0)
                normed_rope(p, qall[:, p - 1, :] if p else kf[:])
                if p == 1:
                    dve.wait_ge(sem("rope_out"), primed(2))
                    queries(0)
            dve.wait_ge(sem("rel_in"), 16)
            with dve.Fori(0, AH // 2 - 1) as t:
                mixing_step(t)
            mixing_step(AH // 2 - 1, more=False)

            def add_tile(name, per, r, gate, i, s):
                m = i * 2 + s
                matmuls(i * (2 * per) + (SLAB[name] + per * (s + 1)))
                V.scalar_tensor_tensor(chunk(h, m), proj[s][:], gate(m), chunk(h, m), ALU.mult, ALU.add).then_inc(sem(f"evac{s}"), 1)
                if r is not None:
                    add_square(r, m, s)

            def add_tiles(name, per, r, gate):
                if r is not None:
                    clear_sum(r)
                with dve.Fori(0, KC // 2) as i:
                    for s in range(2):
                        add_tile(name, per, r, gate, i, s)

            def ff_product(run, i, i0, jj):
                j = i * 2 + (2 * i0 + jj)
                matmuls(i * 4 + (SLAB[f"ff{run}"] + 4 * i0 + 2 * jj + 2))
                dve.wait_ge(sem("evac0"), primed(i * 2 + (TILE[f"ff{run}"] // 2 + 2 * i0 + jj + 1)))
                dve.wait_ge(sem("act_lo"), primed(j + run * FC))
                V.tensor_tensor(aprod[:, jj, :], proj[1][:], gsil[:, jj, :], ALU.mult).then_inc(sem("evac1"), 1)

            def ff_low(run, i, i0, jj):
                j = i * 2 + (2 * i0 + jj)
                dve.wait_ge(sem("act_hi"), j + (run * FC + 1))
                V.tensor_tensor(chunk(actl, j), aprod[:, jj, :], chunk(acth, j).bitcast(F32), ALU.subtract).then_inc(sem("act_lo"), 1)

            def ada_parts(i, ks):
                for k in ks:
                    dve.wait_ge(sem(f"ada_in{k % 2}"), i * (KC * 8) + (k // 2 * 16 + 16))
                    if k == 0:
                        V.tensor_scalar(adac[:], adaw[:, 0, :], csil[:, 0:1], None, ALU.mult).then_inc(sem("ada_acc"), 1)
                    else:
                        dve.wait_ge(sem("ada_acc"), primed(i * KC + k))
                        V.scalar_tensor_tensor(adac[:], adaw[:, k % 2, :], csil[:, k:k + 1], adac[:], ALU.mult,
                                               ALU.add).then_inc(sem("ada_acc"), 1)

            def mod_column(v):
                dve.wait_ge(sem("mod_sum"), primed(v + 1))
                V.tensor_tensor(modc[:, bass.ds(v * KC, KC)], bank[2][:, 0:KC], col[:, bass.ds(v * KC + COL["b_ada"], KC)],
                                ALU.add).then_inc(sem("mod"), 1)

            def ff_beside_ada(i, i0, v):
                for jj in range(2):
                    ff_product(0, i, i0, jj)
                    if jj == 0 and i0 > 0:
                        mod_column(i)
                    ada_parts(v, range(4 * jj, 4 * jj + 2))
                    ff_low(0, i, i0, jj)
                    ada_parts(v, range(4 * jj + 2, 4 * jj + 4))

            add_tiles("out", 1, 1, lambda m: 1.0)
            norm(1, lambda c: c1("ffn_norm", c))
            dve.wait_ge(sem("c_silu"), 1)
            ff_beside_ada(0, 0, 0)
            with dve.Fori(0, NMOD - 1) as i:
                ff_beside_ada(i, 1, i + 1)
            for i0 in (NMOD, NMOD + 1):
                for jj in range(2):
                    ff_product(0, 0, i0, jj)
                    if i0 == NMOD and jj == 0:
                        mod_column(NMOD - 1)
                    ff_low(0, 0, i0, jj)
            dve.wait_ge(sem("mod"), NMOD)
            for r, name in enumerate(("ffn1_norm", "mix_norm", "ffn2_norm")):
                sc = modc[:, (3 * r + 1) * KC:(3 * r + 2) * KC]
                V.scalar_tensor_tensor(scl[:, r * KC:(r + 1) * KC], sc, 1.0, col[:, COL[name]:COL[name] + KC], ALU.add,
                                       ALU.mult).then_inc(sem("mod_cols"), 1)
                V.tensor_scalar(gat[:, r * KC:(r + 1) * KC], modc[:, (3 * r + 2) * KC:(3 * r + 3) * KC], 1.0 if r == 1 else 0.5, None,
                                ALU.mult).then_inc(sem("mod_cols"), 1)
            dve.wait_ge(sem("mod_cols"), 6)
            add_tiles("down0", 2, 2, lambda m: 1.0)

            def ff_products(run):
                with dve.Fori(0, FC // 2) as i:
                    for jj in range(2):
                        ff_product(run, i, 0, jj)
                        ff_low(run, i, 0, jj)

            def gate(r):
                return lambda m: gat[:, bass.ds(m + r * KC, 1)]

            norm(2, lambda c: scl[:, c:c + 1], shift=0)
            ff_products(1)
            add_tiles("down1", 2, 3, gate(0))

            dve.wait_ge(sem("gates_in"), 16)
            V.tensor_copy(ghi[:], gates_raw[:]).then_inc(sem("gates_split"), 1)
            dve.wait_ge(sem("gates_split"), 1)
            V.tensor_tensor(glo[:], gates_raw[:], ghi[:].bitcast(F32), ALU.subtract).then_inc(sem("gates_split"), 1)
            norm(3, lambda c: scl[:, KC + c:KC + c + 1], shift=3)
            for t_ in (fsp, msM, msm):
                V.memset(t_[:], 0.0).then_inc(sem("rows_clear"), 1)
            V.memset(qz[:, :, 0:CONV - 1], 0.0).then_inc(sem("pads"), 1)
            V.memset(scan[:], 0.0).then_inc(sem("scan"), 1)
            for g in range(FH):
                V.tensor_scalar(sel[:, g, :], ones[0:96, :], c1("sel", g, rows=slice(0, 96)), None, ALU.mult).then_inc(sem("sel_ready"), 1)

            PAD = S // 2
            dve.wait_ge(sem("gates_out"), 2)
            V.scalar_tensor_tensor(zt[0:48, :], zg[0:48, :], -1.0, zg[0:48, :], ALU.mult, ALU.max).then_inc(sem("g_abs"), 1)
            dve.wait_ge(sem("g_ln"), 1)
            dve.wait_ge(sem("scan"), 1)
            V.scalar_tensor_tensor(scan[:, 0, PAD:], zg[0:48, :], 0.0, zt[0:48, :], ALU.min, ALU.subtract).then_inc(sem("scan"), 1)

            def scan_rows(rows, op, done):
                for j in range(S.bit_length() - 1):
                    a, b, d = j % 2, (j + 1) % 2, 1 << j
                    dve.wait_ge(sem("scan"), done + j)
                    V.tensor_tensor(scan[rows, b, PAD:], scan[rows, a, PAD:], scan[rows, a, PAD - d:PAD + S - d], op).then_inc(sem("scan"), 1)
                dve.wait_ge(sem("scan"), done + S.bit_length() - 1)

            def split_rows(which, rows, src):
                rest = [src, zt[rows, :], zg[rows, :]]
                dve.wait_ge(sem("row_split"), primed(3 * which))
                for j in range(3):
                    V.tensor_copy(gsp[rows, j, :], rest[j]).then_inc(sem("row_split"), 1)
                    if j < 2:
                        dve.wait_ge(sem("row_split"), primed(3 * which + j + 1))
                        V.tensor_tensor(rest[j + 1], rest[j], gsp[rows, j, :], ALU.subtract).then_inc(sem("row_rest"), 1)
                        dve.wait_ge(sem("row_rest"), 2 * which + j + 1)

            scan_rows(slice(0, 48), ALU.add, 2)
            steps_done = 2 + S.bit_length() - 1
            F = scan[:, 1, PAD:]
            H4 = slice(0, MH)
            V.tensor_tensor(arow[:], zi[:], scan[H4, 1, PAD:], ALU.subtract).then_inc(sem("arow"), 1)
            V.tensor_copy(frow[:], scan[H4, 1, PAD:]).then_inc(sem("frow"), 1)
            split_rows(0, slice(32, 48), scan[32:48, 1, PAD:])
            dve.wait_ge(sem("arow"), 1)
            dve.wait_ge(sem("frow"), 1)
            V.tensor_copy(scan[H4, 0, PAD:], arow[:]).then_inc(sem("scan"), 1)
            scan_rows(H4, ALU.max, steps_done + 1)
            split_rows(1, H4, scan[H4, 1, PAD:])
            V.tensor_tensor(frow[:], frow[:], scan[H4, 1, PAD:], ALU.add).then_inc(sem("frow"), 1)
            dve.wait_ge(sem("frow"), 2)
            dve.wait_ge(sem("m_rows"), 3)
            split_rows(2, H4, frow[:])

            with dve.Fori(0, MH) as hd:
                for j in range(2):
                    dve.wait_ge(sem(f"evac{j}"), primed(hd * 3 + (TILE["mlstm"] // 2 + 1)))
                    dve.wait_ge(sem("m_qk"), primed(hd * 2))
                    cw = lambda tap: c1("conv_w", hd * (2 * CONV) + (j * CONV + tap))
                    V.tensor_scalar(cv[:, j, :], qz[:, j, 0:S], cw(0), c1("conv_b", hd * 2 + j), ALU.mult, ALU.add).then_inc(sem("m_tap"), 1)
                    for tap in range(1, CONV):
                        dve.wait_ge(sem("m_tap"), hd * (2 * (CONV - 1)) + (j * (CONV - 1) + tap))
                        V.scalar_tensor_tensor(cv[:, j, :], qz[:, j, tap:tap + S], cw(tap), cv[:, j, :], ALU.mult,
                                               ALU.add).then_inc(sem("m_tap" if tap < CONV - 1 else "m_conv"), 1)
                dve.wait_ge(sem("m_nM"), hd + 1)
                for b in range(NB):
                    ins = V.tensor_tensor(nMd[:, b * P:(b + 1) * P], nM[:, b * P:(b + 1) * P], ge[:], ALU.add)
                ins.then_inc(sem("m_nMd"), 1)
                for b in range(NB):
                    W = S - b * P
                    dve.wait_ge(sem("m_D"), hd * NB + (b + 1))
                    dve.wait_ge(sem("m_scores"), hd * NB + (b + 1))
                    dve.wait_ge(sem("m_values"), primed(hd * NB + max(b - 1, 0)))
                    V.scalar_tensor_tensor(sT[:, b % 2, 0:W], bank[2 + b % 2][:, 0:W], DQK ** -0.5, Dm[:, b % 2, 0:W], ALU.mult,
                                           ALU.mult).then_inc(sem("m_weighted"), 1)
                dve.wait_ge(sem("m_values"), primed(hd * NB + NB))
                dve.wait_ge(sem("m_emm"), hd + 1)
                dve.wait_ge(sem("m_y"), primed(hd * 2))
                V.tensor_scalar(mxr[:, 0, :], bank[7][:], -1.0, None, ALU.mult).then_inc(sem("m_den"), 1)
                dve.wait_ge(sem("m_den"), hd * 4 + 1)
                V.tensor_tensor(mxr[:, 0, :], mxr[:, 0, :], bank[7][:], ALU.max).then_inc(sem("m_den"), 1)
                dve.wait_ge(sem("m_den"), hd * 4 + 2)
                V.tensor_tensor(mxr[:, 0, :], mxr[:, 0, :], emm[:], ALU.max).then_inc(sem("m_den"), 1)
                dve.wait_ge(sem("m_den"), hd * 4 + 3)
                V.reciprocal(mxr[:, 1, :], mxr[:, 0, :]).then_inc(sem("m_den"), 1)
                dve.wait_ge(sem("m_den"), hd * 4 + 4)
                for j in range(2):
                    V.tensor_tensor(hm[:, j, :], bank[5 + j][:], mxr[:, 1, :], ALU.mult).then_inc(sem("m_out"), 1)
                dve.wait_ge(sem("m_rstd"), hd + 1)
                dve.wait_ge(sem("evac1"), primed(hd * 3 + (TILE["mlstm"] // 2 + 3)))
                for j in range(2):
                    V.scalar_tensor_tensor(hn[:, j, :], hm[:, j, :], c1("mlstm_norm", hd * 2 + j), hrs[:], ALU.mult, ALU.mult).then_inc(sem("m_normed"), 1)
                for j in range(2):
                    dve.wait_ge(sem("m_normed"), hd * 2 + 2)
                    V.tensor_tensor(hn[:, j, :], hn[:, j, :], so[:, j, :], ALU.mult).then_inc(sem("m_gated"), 1)
                for j in range(2):
                    dve.wait_ge(sem("m_yhi"), hd * 2 + (j + 1))
                    V.tensor_tensor(chunk(yal, hd * 2 + j), hn[:, j, :], chunk(yah, hd * 2 + j).bitcast(F32), ALU.subtract).then_inc(sem("m_y"), 1)

            UA = AH * NB

            def fox_maxima(t, k):
                maxima(t * 8 + UA, k, (k % NB + 1) * P)

            def fox_scale(t, k):
                st = stat[:, k % 2, :]
                W = (k % NB + 1) * P
                dve.wait_ge(sem("probs"), t * 8 + (UA + k + 1))
                V.reciprocal(st[:, 5:6], st[:, 2:3]).then_inc(sem("rden"), 1)
                dve.wait_ge(sem("rden"), t * 8 + (UA + k + 1))
                V.tensor_scalar(fprob[:, k % 2, 0:W], fprob[:, k % 2, 0:W], st[:, 5:6], None, ALU.mult).then_inc(sem("probs_scaled"), 1)

            def fox_normed(p, par, j):
                dve.wait_ge(sem("f_rstd"), p * 2 + (j + 1))
                V.scalar_tensor_tensor((fq, fk)[j][:, par, :], fraw[:, j, :], c1(("fox_q", "fox_k")[j], p), frs[:, j, :], ALU.mult,
                                       ALU.mult).then_inc(sem("f_qk"), 1)

            def fox_pair(i, tt, more=True):
                t = i * 2 + tt
                for k in range(8):
                    if k > 0:
                        fox_scale(t, k)
                    if k + 2 < 8:
                        fox_maxima(t, k + 2)
                    if more and k >= 5 and k < 7:
                        fox_normed(t + 1, 1 - tt, k - 5)
                if more:
                    fox_maxima(t + 1, 0)
                    fox_scale(t + 1, 0)
                    fox_maxima(t + 1, 1)
                dve.wait_ge(sem("yb_hi"), t + 1)
                V.tensor_tensor(chunk(ybl, t), bank[7][:], chunk(ybh, t).bitcast(F32), ALU.subtract).then_inc(sem("yb_lo"), 1)

            for j in range(2):
                fox_normed(0, 0, j)
            fox_maxima(0, 0)
            fox_maxima(0, 1)
            fox_scale(0, 0)
            with dve.Fori(0, FH // 4 - 1) as i:
                for tt in range(2):
                    fox_pair(i, tt)
            fox_pair(FH // 4 - 1, 0)
            fox_pair(FH // 4 - 1, 1, more=False)

            with dve.Fori(0, KC) as m:
                for j in range(2):
                    matmuls(m * 4 + (SLAB["merge"] + 2 * j + 2))
                    dve.wait_ge(sem("mg"), primed(m))
                    dve.wait_ge(sem("evac0"), primed(m * 2 + (TILE["merge"] // 2 + j + 1)))
                    V.tensor_tensor(br[:, j, :], proj[1][:], sg[:, j, :], ALU.mult).then_inc(sem("evac1"), 1)
                dve.wait_ge(sem("evac1"), primed(m * 2 + (TILE["merge"] // 2 + 2)))
                dve.wait_ge(sem("mg_lo"), primed(m))
                V.tensor_tensor(mg[:, 0, :], br[:, 0, :], br[:, 1, :], ALU.add).then_inc(sem("mg"), 1)
                dve.wait_ge(sem("mg_hi"), m + 1)
                V.tensor_tensor(chunk(mgl, m), mg[:, 0, :], chunk(mgh, m).bitcast(F32), ALU.subtract).then_inc(sem("mg_lo"), 1)
            add_tiles("out2", 1, 4, gate(1))
            norm(4, lambda c: scl[:, 2 * KC + c:2 * KC + c + 1], shift=6)
            ff_products(2)
            add_tiles("down2", 2, None, gate(2))


def constants():
    p = np.arange(P)
    ident = np.eye(P, dtype=np.float32)
    blk = (p[:, None] // DH == p[None, :] // DH).astype(np.float32)
    rot = np.zeros((P, P), np.float32)
    for o in range(P):
        if o % DH < DH // 2:
            rot[o + DH // 2, o] = -1.0
        else:
            rot[o - DH // 2, o] = 1.0
    ge = np.where(p[None, :] >= p[:, None], 0.0, NEG).astype(np.float32)
    le = np.where(p[None, :] <= p[:, None], 0.0, NEG).astype(np.float32)
    inv = (np.float32(10000.0) ** (-np.arange(0, DH, 2, dtype=np.float32) / np.float32(DH))).astype(np.float32)
    ang = inv[p % (DH // 2)][:, None] * np.arange(S, dtype=np.float32)[None, :]
    const = np.concatenate([ident, blk, rot, ge, le, np.cos(ang), np.sin(ang)], 1).astype(np.float32)
    diff = np.arange(REL)[None, :] - (REL - S) - p[:, None]
    rel = np.concatenate([np.maximum(diff, 0), np.maximum(-diff, 0)], 1).astype(np.float32)
    sel = np.zeros((P, FH), np.float32)
    for g in range(FH):
        sel[[g, 32 + g, 64 + g], g] = -1.0
    return const, rel, sel


def kernel(**inputs):
    import concourse.bacc as bacc
    from concourse.bass_utils import run_bass_kernel_spmd

    a = {k: np.asarray(v) for k, v in inputs.items()}

    def tile(w, cols):
        w = w[:, cols]
        return w.reshape(-1, P, w.shape[1]).transpose(1, 0, 2).reshape(P, -1)

    def tiles(w):
        return [tile(w, slice(m * P, (m + 1) * P)) for m in range(w.shape[1] // P)]

    def pairs(w, v):
        return [t for both in zip(tiles(w), tiles(v)) for t in both]

    w_in, w_mix, b_mix = a["w_in"][0], a["w_mix_2"][0], a["b_mix_2"][0]
    pair = [np.r_[t * DH:(t + 1) * DH, (t + 4) * DH:(t + 5) * DH] for t in range(AH // 2)]
    kv0 = AH * DH
    att = [tile(w_in, c) for c in (slice(kv0, kv0 + P), *pair, slice(kv0 + P, kv0 + 2 * P))]
    r0 = kv0 + 2 * P
    RW = RH * DH
    ret = [tile(w_in, slice(r0 + j * RW + t * P, r0 + j * RW + (t + 1) * P)) for t in range(RH // 2) for j in range(4)]
    order = np.concatenate([c for t in range(AH // 2) for c in (pair[t], np.arange(AH * DH + t * P, AH * DH + (t + 1) * P))])
    out1 = tiles(a["w_out"][0][order])
    o = np.cumsum([0, 512, 512, 1024, 1024, MH, MH, D, D, D, FH, D, D])
    m_at = [s for hd in range(MH) for s in (o[0] + hd * P, o[1] + hd * P, o[2] + hd * DV, o[2] + hd * DV + P,
                                            o[3] + hd * DV, o[3] + hd * DV + P)]
    f_at = [o[j] + t * P for t in range(FH // 2) for j in (6, 7, 8)]
    g_at = [o[j] + m * P for m in range(KC) for j in (10, 11)]
    gates = tiles(np.ascontiguousarray(w_mix[:, o[10]:o[12]]))
    wa, wb = tiles(a["w_branch_a_2"][0]), tiles(a["w_branch_b_2"][0])
    merge = [t for m in range(KC) for t in (gates[m], wa[m], gates[KC + m], wb[m])]
    f1, f2 = a["ffn1_w_in_2"][0], a["ffn2_w_in_2"][0]
    w_all = np.stack(att + ret + out1 + pairs(a["w_gate"][0], a["w_up"][0]) + pairs(f1[:, :FF], f1[:, FF:])
                     + [tile(w_mix, slice(c, c + P)) for c in m_at + f_at] + merge + tiles(a["w_out_2"][0])
                     + pairs(f2[:, :FF], f2[:, FF:]))
    wd_all = np.stack([tile(w[f * DC:(f + 1) * DC], slice(m * P, (m + 1) * P))
                       for w in (a["w_down"][0], a["ffn1_w_out_2"][0], a["ffn2_w_out_2"][0]) for m in range(KC) for f in range(2)])
    ada = a["w_ada_2"][0].reshape(KC, P, NMOD, D).transpose(2, 0, 1, 3).reshape(NMOD * KC, P, D)

    gate_rows = ((0, slice(o[5], o[6])), (32, slice(o[9], o[10])), (64, slice(o[4], o[5])))
    gw = np.zeros((D, 96), np.float32)
    gb = np.zeros((P, 1), np.float32)
    for at, c in gate_rows:
        gw[:, at:at + c.stop - c.start] = w_mix[:, c]
        gb[at:at + c.stop - c.start, 0] = b_mix[c]

    def columns(v):
        return v.reshape(-1, P).T

    def everywhere(v):
        return np.broadcast_to(v[None, :], (P, v.size))

    const, rel, sel = constants()
    conv = a["conv_w_2"][0].reshape(CONV, 2, MH, P).transpose(3, 2, 1, 0).reshape(P, -1)
    convb = a["conv_b_2"][0].reshape(2, MH, P).transpose(2, 1, 0).reshape(P, -1)
    at_cols = lambda starts: np.stack([b_mix[c:c + P] for c in starts], 1)
    cols = np.concatenate([
        columns(a["attn_norm_w"][0]), columns(a["ffn_norm_w"][0]), columns(a["ffn1_norm_g_2"][0]), columns(a["mix_norm_g_2"][0]),
        columns(a["ffn2_norm_g_2"][0]), np.tile(a["q_norm_w"][0], 2)[:, None], np.tile(a["k_norm_w"][0], 2)[:, None],
        columns(a["ret_norm_w"][0]), everywhere(a["attn_sink"][0]), everywhere(a["ret_log_decay_fwd"][0]),
        everywhere(a["ret_log_decay_bwd"][0]), columns(a["c_2"][0]), columns(a["b_ada_2"][0]), gb, at_cols(m_at), conv, convb,
        columns(a["mlstm_norm_g_2"][0].reshape(-1)), at_cols(f_at), columns(a["fox_q_norm_g_2"][0].reshape(-1)),
        columns(a["fox_k_norm_g_2"][0].reshape(-1)), at_cols(g_at), sel], 1)
    assert cols.shape == (P, NCOL)
    x = a["x"][0].reshape(S, KC, P).transpose(2, 1, 0).reshape(P, KC * S)

    arrays = {"x": x, "cols": cols, "const": const, "rel": rel, "w": w_all, "wd": wd_all, "ada": ada, "gates": tile(gw, slice(0, 96))}
    arrays = {k: np.ascontiguousarray(v) for k, v in arrays.items()}
    nc = bacc.Bacc("TRN2", target_bir_lowering=False, num_devices=1)
    args = [nc.dram_tensor(k + "_dram", v.shape, F32, kind="ExternalInput").ap() for k, v in arrays.items()]
    out = nc.dram_tensor("out_dram", (P, KC * S), F32, kind="ExternalOutput").ap()
    arrays = {k + "_dram": v for k, v in arrays.items()}
    build(nc, *args, out)
    r = run_bass_kernel_spmd(nc, [arrays], core_ids=[0])
    got = r.results[0]["out_dram"]
    return np.ascontiguousarray(got.reshape(P, KC, S).transpose(2, 1, 0).reshape(1, S, D))
```

```python
from contextlib import ExitStack

import numpy as np
import concourse.bass as bass
from concourse import mybir

F32 = mybir.dt.float32
F32R = mybir.dt.float32r
BF16 = mybir.dt.bfloat16
ALU = mybir.AluOpType
ACT = mybir.ActivationFunctionType
AX = mybir.AxisListType

P = 128
S = 512
D = 1024
KC = D // P
NB = S // P
DH = 64
FF = 2816
FC = FF // P
HALF = FC // 2
WC = KC * P
DC = HALF * P
EPS = 1e-6
NEG = -1e30
AH = 8
RH = 8
MH = 4
DQK = 128
DV = 256
FH = 16
CONV = 4
NMOD = 9
REL = S + (NB - 1) * P
ADA_PARTS = KC

N_ATT, N_RET, N_OUT, N_FF, N_DOWN = 6, 16, 8, 2 * FC, 16
N_MLSTM, N_FOX, N_MERGE = 6 * MH, 24, 32
SLAB = {}
TILE = {}
_n = _q = 0
for _name, _count in (("att", N_ATT), ("ret", N_RET), ("out", N_OUT), ("ff0", N_FF), ("down0", N_DOWN),
                      ("ff1", N_FF), ("down1", N_DOWN), ("mlstm", N_MLSTM), ("fox", N_FOX),
                      ("merge", N_MERGE), ("out2", N_OUT), ("ff2", N_FF), ("down2", N_DOWN)):
    SLAB[_name], TILE[_name] = _n, _q
    _n += _count
    _q += _count // 2 if _name.startswith("down") else _count

COL = {}
_c = 0
for _name, _count in (("attn_norm", KC), ("ffn_norm", KC), ("ffn1_norm", KC), ("mix_norm", KC), ("ffn2_norm", KC),
                      ("q_norm", 1), ("k_norm", 1), ("ret_norm", RH // 2), ("sink", AH), ("decay_f", RH),
                      ("decay_b", RH), ("c", KC), ("b_ada", NMOD * KC), ("b_gates", 1), ("b_mlstm", 6 * MH),
                      ("conv_w", 2 * MH * CONV), ("conv_b", 2 * MH), ("mlstm_norm", 2 * MH), ("b_fox", 24),
                      ("fox_q", FH // 2), ("fox_k", FH // 2), ("b_merge", 16), ("sel", FH)):
    COL[_name] = _c
    _c += _count
NCOL = _c


PRIMED = ("act_lo", "ada_acc", "evac0", "evac1", "f_qk", "m_conv", "m_nMd", "m_out", "m_qk", "m_turned", "m_values",
          "m_weighted", "m_gated", "m_normed", "m_y", "mg", "mg_lo", "mod_sum", "norm_sum", "probs_scaled", "rope_out", "row_split", "ssum",
          "w_lo", "x_lo0", "x_lo1", "y_lo", "yb_lo")


def build(nc, x_in, cols_in, const_in, rel_in, w_in, wd_in, ada_in, gates_in, out):
    ctx = ExitStack()
    with ctx:
        def sb(name, shape, dt=F32, scope=ctx):
            return scope.enter_context(nc.sbuf_tensor(name, shape, dt))

        sems = {}

        def sem(name):
            if name not in sems:
                sems[name] = ctx.enter_context(nc.semaphore(name))
            return sems[name]

        def primed(count):
            return count + 1

        h = sb("h", [P, KC * S])
        xh = sb("xh", [P, KC, S], F32R)
        xl = sb("xl", [P, KC, S], F32R)
        raw = sb("raw", [P, 2, DC])
        whi = sb("whi", [P, 2, DC], F32R)
        wlo = sb("wlo", [P, 2, DC], F32R)
        col = sb("col", [P, NCOL])
        modc = sb("modc", [P, NMOD * KC])
        scl = sb("scl", [P, 3 * KC])
        gat = sb("gat", [P, 3 * KC])
        ident = sb("ident", [P, P])
        ones = sb("ones", [P, P])
        blk = sb("blk", [P, P])
        identb = sb("identb", [P, P], BF16)
        ge = sb("ge", [P, P])
        geb = sb("geb", [P, P], BF16)
        leb = sb("leb", [P, P], BF16)
        csil = sb("csil", [P, KC])
        ssum = sb("ssum", [P, S])
        sqn = sb("sqn", [P, 2, S])
        rstd = sb("rstd", [P, S])
        tmp = (sqn[:, 0, :], sqn[:, 1, :], ssum[:])
        gates_raw = sb("gates_raw", [P, KC * 96])
        stat = sb("stat", [P, 2, 8])
        lg = sb("lg", [P, 2 * RH])
        epsc = sb("epsc", [P, 1])

        ffs = ExitStack()
        acth = sb("acth", [P, FC, S], F32R, ffs)
        actl = sb("actl", [P, FC, S], F32R, ffs)
        gsil = sb("gsil", [P, 2, S], F32, ffs)
        aprod = sb("aprod", [P, 2, S], F32, ffs)
        adaw = sb("adaw", [P, 2, D], F32, ffs)
        adac = sb("adac", [P, D], F32, ffs)
        ffs.close()

        abs_ = ExitStack()
        yh = sb("yh", [P, KC, S], F32R, abs_)
        yl = sb("yl", [P, KC, S], F32R, abs_)
        decay = sb("decay", [P, 2 * REL], F32, abs_)
        rel = sb("rel", [P, 2 * REL], F32, abs_)
        cos = sb("cos", [P, S], F32, abs_)
        sin = sb("sin", [P, S], F32, abs_)
        rot = sb("rot", [P, P], F32, abs_)
        leconst = sb("leconst", [P, P], F32, abs_)
        rraw = sb("rraw", [P, 2, S], F32, abs_)
        rsq = sb("rsq", [P, S], F32, abs_)
        rr = sb("rr", [P, S], F32, abs_)
        rt = sb("rt", [P, 2, S], F32, abs_)
        qall = sb("qall", [P, AH // 2, S], F32, abs_)
        qf = sb("qf", [P, S], F32, abs_)
        kf = sb("kf", [P, S], F32, abs_)
        rqf = sb("rqf", [P, S], F32, abs_)
        rkf = sb("rkf", [P, S], F32, abs_)
        rvtok = sb("rvtok", [P, NB, P], F32, abs_)
        vraw = sb("vraw", [P, S], F32, abs_)
        vtok = sb("vtok", [P, NB, P], F32, abs_)
        prob = sb("prob", [P, 2, S], F32, abs_)
        pT = sb("pT", [P, 2, S], F32, abs_)
        rsil = sb("rsil", [P, S], F32, abs_)
        ry = sb("ry", [P, S], F32, abs_)
        abs_.close()

        mix = ExitStack()
        yah = sb("yah", [P, KC, S], F32R, mix)
        yal = sb("yal", [P, KC, S], F32R, mix)
        sel = sb("sel", [96, FH, P], BF16, mix)
        fsp = sb("fsp", [96, S], BF16, mix)
        mls = ExitStack()
        ghi = sb("ghi", [P, KC * 96], F32R, mls)
        glo = sb("glo", [P, KC * 96], F32R, mls)
        zg = sb("zg", [96, S], F32, mls)
        zt = sb("zt", [96, S], F32, mls)
        zi = sb("zi", [MH, S], F32, mls)
        zrow = sb("zrow", [48, S], F32, mls)
        lf = sb("lf", [48, S], F32, mls)
        cs = sb("cs", [48, S], F32, mls)
        gsp = sb("gsp", [48, 3, S], BF16, mls)
        msM = sb("msM", [96, S], BF16, mls)
        msm = sb("msm", [96, S], BF16, mls)
        arow = sb("arow", [MH, S], F32, mls)
        acol = sb("acol", [P, NB * MH], F32, mls)
        qz = sb("qz", [P, 2, S + CONV - 1], F32, mls)
        cv = sb("cv", [P, 2, S], F32, mls)
        qk = sb("qk", [P, 2, S], F32, mls)
        mvT = sb("mvT", [P, 2, S], F32, mls)
        mv = sb("mv", [P, NB, DV], F32, mls)
        nM = sb("nM", [P, S], F32, mls)
        nMd = sb("nMd", [P, S], F32, mls)
        emm = sb("emm", [P, S], F32, mls)
        Dm = sb("Dm", [P, 2, S], F32, mls)
        sT = sb("sT", [P, 2, S], F32, mls)
        hm = sb("hm", [P, 2, S], F32, mls)
        hsq = cv
        so = sb("so", [P, 2, S], F32, mls)
        mxr = sb("mxr", [P, 2, S], F32, mls)
        hn = mxr
        hrs = emm
        mls.close()
        fox = ExitStack()
        fraw = sb("fraw", [P, 2, S], F32, fox)
        fsq = sb("fsq", [P, 2, S], F32, fox)
        frs = sb("frs", [P, 2, S], F32, fox)
        fq = sb("fq", [P, 2, S], F32, fox)
        fk = sb("fk", [P, 2, S], F32, fox)
        fvraw = sb("fvraw", [P, S], F32, fox)
        fv = sb("fv", [P, NB, P], F32, fox)
        fprob = sb("fprob", [P, 2, S], F32, fox)
        fpT = sb("fpT", [P, 2, S], F32, fox)
        ybh = sb("ybh", [P, KC, S], F32R, fox)
        ybl = sb("ybl", [P, KC, S], F32R, fox)
        fox.close()
        mgh = sb("mgh", [P, KC, S], F32R, mix)
        mgl = sb("mgl", [P, KC, S], F32R, mix)
        sb("yb_kept", [P, 2, KC, S], F32R, mix)
        sg = sb("sg", [P, 2, S], F32, mix)
        br = sb("br", [P, 2, S], F32, mix)
        mg = sb("mg", [P, 1, S], F32, mix)
        mix.close()

        bank = [ctx.enter_context(nc.psum_tensor(f"bank{i}", [P, S], F32)) for i in range(8)]
        proj = bank[0:2]

        def c1(name, i=0, rows=slice(0, P)):
            if isinstance(i, int):
                return col[rows, COL[name] + i:COL[name] + i + 1]
            return col[rows, bass.ds(i + COL[name], 1)]

        def chunk(t, m):
            flat = t[:].rearrange("p c s -> p (c s)") if len(t.shape) == 3 else t
            return flat[:, m * S:m * S + S] if isinstance(m, int) else flat[:, bass.ds(m * S, S)]

        BESIDE = ((0, 0, 4), (0, 4, 8), (1, 0, 3), (1, 3, 6), (1, 6, 8), (2, 0, 2), (2, 2, 4), (2, 4, 8))
        QT = 1 + AH // 2

        def keys(b):
            return max(0, b - 1), min(NB - 1, b + 1)

        def window(k):
            lo, hi = keys(k % NB)
            return (hi - lo + 1) * P

        block = ctx.enter_context(nc.Block())

        @block.sync
        def _(sp):
            for name in PRIMED:
                sp.sem_inc(sem(name), 1)
            for c in range(4):
                sp.dma_start(h[:, c * 2 * S:(c + 1) * 2 * S], x_in[:, c * 2 * S:(c + 1) * 2 * S]).then_inc(sem(f"x_in{c}"), 16)
            sp.dma_start(col[:], cols_in).then_inc(sem("cols_in"), 16)

            def load(n, s, src, width):
                if not isinstance(n, int) or n >= 2:
                    sp.wait_ge(sem("w_lo"), primed(n - 1))
                sp.dma_start(raw[:, s, 0:width], src).then_inc(sem(f"raw_in{s}"), 16)

            def downs_before(n0):
                return sum(N_DOWN for d in ("down0", "down1", "down2") if SLAB[d] < n0)

            def load_wide(i, per, n0, k):
                n = n0 - downs_before(n0) + k
                src = w_in[n] if i is None else w_in[bass.ds(i * per + n, 1)].rearrange("a p n -> (a p) n")
                load(n0 + k if i is None else i * per + (n0 + k), (n0 + k) % 2, src, WC)

            def wide_loop(n0, pairs):
                with sp.Fori(0, pairs) as i:
                    for k in range(2):
                        load_wide(i, 2, n0, k)

            def down_loop(run):
                n0 = SLAB[f"down{run}"]
                with sp.Fori(0, N_DOWN // 2) as i:
                    for k in range(2):
                        load(i * 2 + (n0 + k), k,
                             wd_in[bass.ds(i * 2 + (run * N_DOWN + k), 1)].rearrange("a p n -> (a p) n"), DC)

            for k in range(2):
                load_wide(None, 2, 0, k)
            sp.dma_start(gates_raw[:], gates_in).then_inc(sem("gates_in"), 16)
            wide_loop(2, (SLAB["ff0"] - 2) // 2)

            for s in range(4):
                load_wide(None, 4, SLAB["ff0"], s)
            with sp.Fori(0, NMOD) as i:
                for s in range(4):
                    load_wide(i, 4, SLAB["ff0"] + 4, s)
                    for k in range(2 * s, 2 * s + 2):
                        if k == 0:
                            sp.wait_ge(sem("mm_done"), SLAB["ff0"])
                        sp.wait_ge(sem("ada_acc"), primed(i * KC + max(k - 1, 0)))
                        sp.dma_start(adaw[:, k % 2, :], ada_in[bass.ds(i * KC + k, 1)].rearrange("a p n -> (a p) n")
                                     ).then_inc(sem(f"ada_in{k % 2}"), 16)
            wide_loop(SLAB["ff0"] + 4 * (NMOD + 1), (N_FF - 4 * (NMOD + 1)) // 2)
            down_loop(0)
            wide_loop(SLAB["ff1"], N_FF // 2)
            down_loop(1)
            wide_loop(SLAB["mlstm"], (SLAB["down2"] - SLAB["mlstm"]) // 2)
            down_loop(2)
            base = TILE["down2"] // 2
            with sp.Fori(0, KC // 2) as i:
                for s in range(2):
                    sp.wait_ge(sem(f"evac{s}"), primed(i + (base + 1)))
                    sp.dma_start(out[:, bass.ds(i * (2 * S) + s * S, S)], chunk(h, i * 2 + s)).then_inc(sem("stored"), 16)
            sp.wait_ge(sem("stored"), 16 * KC)

        @block.gpsimd
        def _(pool):
            def low_loop(n0, count, width):
                with pool.Fori(0, count // 2) as i:
                    for s in range(2):
                        pool.wait_ge(sem("w_hi"), i * 2 + (n0 + s + 1))
                        nc.gpsimd.tensor_tensor(wlo[:, s, 0:width], raw[:, s, 0:width], whi[:, s, 0:width].bitcast(F32),
                                                ALU.subtract).then_inc(sem("w_lo"), 1)

            def norm_lows(r):
                for c in range(1, KC, 2):
                    pool.wait_ge(sem("x_hi"), KC * r + c + 1)
                    nc.gpsimd.tensor_tensor(xl[:, c, :], tmp[c % 3], xh[:, c, :].bitcast(F32), ALU.subtract).then_inc(sem("x_lo1"), 1)

            low_loop(0, 2, WC)
            norm_lows(0)
            low_loop(2, SLAB["ff0"], WC)
            norm_lows(1)
            low_loop(SLAB["ff0"] + 2, N_FF - 2, WC)
            low_loop(SLAB["down0"], N_DOWN, DC)
            low_loop(SLAB["ff1"], 2, WC)
            norm_lows(2)
            low_loop(SLAB["ff1"] + 2, N_FF - 2, WC)
            low_loop(SLAB["down1"], N_DOWN, DC)
            low_loop(SLAB["mlstm"], 2, WC)
            norm_lows(3)
            low_loop(SLAB["mlstm"] + 2, SLAB["ff2"] - SLAB["mlstm"], WC)
            norm_lows(4)
            low_loop(SLAB["ff2"] + 2, N_FF - 2, WC)
            low_loop(SLAB["down2"], N_DOWN, DC)

        @block.tensor
        def _(pe):
            def slab(n, s, b, uses, ih, il, chunks, first=True, last=True, ready=None, part=None):
                lo, hi = part or (0, len(chunks))
                if lo == 0:
                    pe.wait_ge(sem("w_lo"), primed(n + 1))
                if lo == 0 and first:
                    pe.wait_ge(sem(f"evac{b}"), primed(uses))
                for j in range(lo, hi):
                    k = chunks[j]
                    if ready and ready[0] == "x_lo":
                        pe.wait_ge(sem(f"x_lo{k % 2}"), primed(ready[1] * (KC // 2) + k // 2 + 1))
                    elif ready:
                        pe.wait_ge(sem(ready[0]), primed(ready[1] + k + 1))
                    W = slice(j * P, j * P + P)
                    for a, (w, v) in enumerate(((whi, ih), (whi, il), (wlo, ih))):
                        mm = nc.tensor.matmul(proj[b][:], w[:, s, W], v[:, k, :], start=first and j == 0 and a == 0,
                                              stop=last and j == len(chunks) - 1 and a == 2, skip_group_check=True)
                if hi == len(chunks):
                    mm.then_inc(sem("mm_done"), 1)

            def wide(name, i, per, s, ready=None, ih=xh, il=xl, part=None):
                slab(i * per + (SLAB[name] + s), s % 2, s % 2, i * (per // 2) + (TILE[name] + s) // 2, ih, il,
                     range(KC), ready=ready, part=part)

            def norm_sum(r):
                pe.wait_ge(sem("ssum"), primed(KC * (r + 1)))
                nc.tensor.matmul(bank[4][:], ones[:], ssum[:], start=True, stop=True).then_inc(sem("norm_sum"), 1)

            def down(run):
                with pe.Fori(0, KC // 2) as i:
                    for s in range(2):
                        for f in range(2):
                            n = i * 4 + (SLAB[f"down{run}"] + 2 * s + f)
                            slab(n, f, s, i + (TILE[f"down{run}"] + s) // 2, acth, actl,
                                 range(f * HALF, f * HALF + HALF), first=f == 0, last=f == 1,
                                 ready=("act_lo", run * FC))

            def transpose_values(src, dst_bank, done):
                for b in range(NB):
                    tr = nc.tensor.transpose(dst_bank[:, b * P:(b + 1) * P], src[:, b * P:(b + 1) * P], ident[:])
                tr.then_inc(sem(done), 1)

            pe.wait_ge(sem("ones"), 1)
            norm_sum(0)

            def sums_and_turn(p):
                pe.wait_ge(sem(f"evac{p % 2}"), primed(p // 2 + 1))
                pe.wait_ge(sem("rope_out"), primed(p))
                nc.tensor.matmul(bank[5][:], blk[:], rsq[:], start=True, stop=True).then_inc(sem("rope_ss"), 1)
                nc.tensor.matmul(bank[6][:], rot[:], rraw[:, p % 2, :], start=True, stop=True).then_inc(sem("rope_rot"), 1)

            def win_scores(t, k):
                e, b = k // NB, k % NB
                lo, hi = keys(b)
                H = slice(e * DH, e * DH + DH)
                if k == 0:
                    pe.wait_ge(sem("q_cur"), t + 1)
                if k >= 2:
                    pe.wait_ge(sem("probs"), t * 8 + (k - 1))
                elif not isinstance(t, int) or t > 0:
                    pe.wait_ge(sem("ret_decayed"), t * 8 + (k - 1))
                dst = bank[2 + k % 2]
                W = window(k)
                mm = nc.tensor.matmul(dst[:, 0:W], qf[H, b * P:(b + 1) * P], kf[H, lo * P:(hi + 1) * P], start=True, stop=False,
                                      skip_group_check=True)
                if b > 0:
                    mm = nc.tensor.matmul(dst[:, 0:P], identb[:], geb[:], start=False, stop=b == NB - 1, skip_group_check=True)
                if b < NB - 1:
                    mm = nc.tensor.matmul(dst[:, W - P:W], identb[:], leb[:], start=False, stop=True, skip_group_check=True)
                mm.then_inc(sem("scores"), 1)

            def win_turn(t, k):
                pe.wait_ge(sem("probs_scaled"), primed(t * 8 + (k + 1)))
                if k >= 2:
                    pe.wait_ge(sem("pT_copied"), t * 8 + (k - 1))
                else:
                    pe.wait_ge(sem("rope_out"), primed(t * 2 + QT))
                for j in range(window(k) // P):
                    tr = nc.tensor.transpose(bank[5 + k % 2][:, j * P:(j + 1) * P], prob[:, k % 2, j * P:(j + 1) * P], ident[:])
                tr.then_inc(sem("pT_ready"), 1)

            def win_values(t, k):
                e, b = k // NB, k % NB
                lo, hi = keys(b)
                H = slice(e * DH, e * DH + DH)
                pe.wait_ge(sem("pT_copied"), t * 8 + (k + 1))
                if k == 0:
                    pe.wait_ge(sem("y_lo"), primed(t * 2))
                    pe.wait_ge(sem("vtok"), t + 1)
                for j in range(hi - lo + 1):
                    mm = nc.tensor.matmul(bank[7][H, b * P:(b + 1) * P], vtok[:, lo + j, H], pT[:, k % 2, j * P:(j + 1) * P],
                                          start=j == 0, stop=j == hi - lo, skip_group_check=True)
                mm.then_inc(sem("values"), 1)

            def ret_turn(t, j):
                pe.wait_ge(sem(f"evac{j}"), primed(t * 2 + (TILE["ret"] // 2 + 1)))
                pe.wait_ge(sem("rope_out"), primed(t * 2 + (QT + j)))
                nc.tensor.matmul(bank[4][:], rot[:], rraw[:, j, :], start=True, stop=True).then_inc(sem("rope_rot"), 1)

            def ret_scores(t, k):
                e, b = k // NB, k % NB
                H = slice(e * DH, e * DH + DH)
                if k >= 2:
                    pe.wait_ge(sem("ret_decayed"), t * 8 + (k - 1))
                nc.tensor.matmul(bank[2 + k % 2][:], rkf[H, b * P:(b + 1) * P], rqf[H, :], start=True, stop=True,
                                 skip_group_check=True).then_inc(sem("ret_scores"), 1)

            def ret_values(t, k):
                e, b = k // NB, k % NB
                H = slice(e * DH, e * DH + DH)
                pe.wait_ge(sem("ret_decayed"), t * 8 + (k + 1))
                if k == 0:
                    pe.wait_ge(sem("vtok"), t + 2)
                nc.tensor.matmul(bank[4][H, :], rvtok[:, b, H], prob[:, k % 2, :], start=b == 0, stop=b == NB - 1,
                                 skip_group_check=True).then_inc(sem("ret_values"), 1)

            def mixing_step(t, more=True):
                for k in range(8):
                    win_turn(t, k)
                    if k + 2 < 8:
                        win_scores(t, k + 2)
                    if k == 3:
                        ret_turn(t, 0)
                    j, lo, hi = BESIDE[k]
                    wide("ret", t, 4, j, part=(lo, hi))
                    if k == 7:
                        ret_turn(t, 1)
                    win_values(t, k)
                wide("ret", t, 4, 3, part=(0, 6))
                pe.wait_ge(sem("evac0"), primed(t * 2 + (TILE["ret"] // 2 + 2)))
                pe.wait_ge(sem("rope_out"), primed(t * 2 + (QT + 2)))
                transpose_values(vraw, bank[4], "vT")
                wide("ret", t, 4, 3, part=(6, KC))
                ret_scores(t, 0)
                ret_scores(t, 1)
                for k in range(8):
                    ret_values(t, k)
                    if k + 2 < 8:
                        ret_scores(t, k + 2)
                    elif more:
                        win_scores(t + 1, k - 6)
                pe.wait_ge(sem("ret_sq"), t + 1)
                nc.tensor.matmul(bank[7][:], blk[:], rsq[:], start=True, stop=True).then_inc(sem("ret_ss"), 1)

            for p in range(N_ATT):
                wide("att", 0, 2, p, ready=("x_lo", 0) if p == 0 else None, part=(0, KC // 2))
                if p == 1:
                    pe.wait_ge(sem("const_ready"), 1)
                if p > 0:
                    sums_and_turn(p - 1)
                if p == N_ATT - 1:
                    win_scores(0, 0)
                    win_scores(0, 1)
                wide("att", 0, 2, p, ready=("x_lo", 0) if p == 0 else None, part=(KC // 2, KC))
            pe.wait_ge(sem("evac1"), primed(N_ATT // 2))
            transpose_values(vraw, bank[4], "vT")
            with pe.Fori(0, AH // 2 - 1) as t:
                mixing_step(t)
            mixing_step(AH // 2 - 1, more=False)

            for s, lo, hi in ((0, 0, KC - 1), (1, 0, KC // 2), (0, KC - 1, KC), (1, KC // 2, KC)):
                wide("out", 0, 2, s, ready=("y_lo", 0), ih=yh, il=yl, part=(lo, hi))
            with pe.Fori(0, N_OUT // 2 - 1) as i:
                for s in range(2):
                    wide("out", i, 2, s + 2, ih=yh, il=yl)
            norm_sum(1)

            def mod_sum(i):
                pe.wait_ge(sem("ada_acc"), primed(i * KC + KC))
                for c in range(KC):
                    mm = nc.tensor.matmul(bank[2][:, c:c + 1], adac[:, c * P:(c + 1) * P], ones[:, 0:1], start=True, stop=True,
                                          skip_group_check=True)
                mm.then_inc(sem("mod_sum"), 1)

            def ff_step(run, i, i0, mod=None):
                for s in range(4):
                    if s == 2 and mod is not None:
                        mod_sum(mod)
                    n = SLAB[f"ff{run}"] + 4 * i0 + s
                    slab(i * 4 + n, s % 2, s % 2, i * 2 + (TILE[f"ff{run}"] + 4 * i0 + s) // 2, xh, xl, range(KC),
                         ready=("x_lo", NORM[run]) if s == 0 else None)

            NORM = (1, 2, 4)
            ff_step(0, 0, 0)
            with pe.Fori(0, NMOD) as i:
                ff_step(0, i, 1, mod=i)
            ff_step(0, 0, NMOD + 1)
            down(0)

            norm_sum(2)
            with pe.Fori(0, FC // 2) as i:
                ff_step(1, i, 0)
            down(1)
            norm_sum(3)

            pe.wait_ge(sem("gates_split"), 2)
            for k in range(KC):
                pe.wait_ge(sem(f"x_lo{k % 2}"), primed(3 * (KC // 2) + k // 2 + 1))
                for a, (w, v) in enumerate(((ghi, xh), (ghi, xl), (glo, xh))):
                    mm = nc.tensor.matmul(bank[4][0:96, :], w[:, k * 96:(k + 1) * 96], v[:, k, :], start=k == 0 and a == 0,
                                          stop=k == KC - 1 and a == 2)
            mm.then_inc(sem("gates"), 1)

            def mlstm_scores(hd, b):
                pe.wait_ge(sem("m_weighted"), primed(hd * NB + max(b - 1, 0)))
                nc.tensor.matmul(bank[2 + b % 2][:, 0:S - b * P], qk[:, 1, b * P:(b + 1) * P], qk[:, 0, b * P:S],
                                 start=True, stop=True).then_inc(sem("m_scores"), 1)

            def mlstm_values(hd, b):
                pe.wait_ge(sem("m_weighted"), primed(hd * NB + (b + 1)))
                if b == 0:
                    pe.wait_ge(sem("m_emm"), hd + 1)
                    pe.wait_ge(sem("m_out"), primed(hd * 2))
                for j in range(3):
                    w = mv[:, b, j * P:(j + 1) * P] if j < 2 else ones[:]
                    mm = nc.tensor.matmul(bank[5 + j][:, b * P:S], w, sT[:, b % 2, 0:S - b * P], start=b == 0, stop=b == NB - 1,
                                          skip_group_check=True)
                mm.then_inc(sem("m_values"), 1)

            def mlstm_head(hd):
                head = sel[:, bass.ds(hd, 1), :].rearrange("p a n -> p (a n)")
                for s in range(2, 5):
                    wide("mlstm", hd, 6, s)
                for j in range(2):
                    pe.wait_ge(sem(f"evac{j}"), primed(hd * 3 + (TILE["mlstm"] // 2 + 2)))
                    transpose_values(mvT[:, j, :], bank[2 + j], "m_turned")
                wide("mlstm", hd, 6, 5, part=(0, KC // 2))
                pe.wait_ge(sem("sel_ready"), FH)
                pe.wait_ge(sem("m_rows"), 6)
                nc.tensor.matmul(bank[4][:], head, msM[:], start=True, stop=True).then_inc(sem("m_bcast"), 1)
                nc.tensor.matmul(bank[5][:], head, msm[:], start=True, stop=True).then_inc(sem("m_bcast"), 1)
                for b in range(NB):
                    tr = nc.tensor.transpose(bank[6][:, b * MH:(b + 1) * MH], arow[:, b * P:(b + 1) * P], ident[0:MH, 0:MH])
                tr.then_inc(sem("m_acol"), 1)
                wide("mlstm", hd, 6, 5, part=(KC // 2, KC))
                pe.wait_ge(sem("m_qk"), primed(hd * 2 + 2))
                pe.wait_ge(sem("m_v"), hd * 2 + 2)
                mlstm_scores(hd, 0)
                mlstm_scores(hd, 1)
                pe.wait_ge(sem("m_acols"), hd + 1)
                for b in range(NB):
                    mlstm_values(hd, b)
                    if b + 2 < NB:
                        mlstm_scores(hd, b + 2)
                wide("mlstm", hd, 6, 6)
                wide("mlstm", hd, 6, 7, part=(0, 6))
                pe.wait_ge(sem("m_sq"), hd + 1)
                nc.tensor.matmul(bank[4][:], ones[:], hsq[:, 0, :], start=True, stop=False)
                nc.tensor.matmul(bank[4][:], ones[:], hsq[:, 1, :], start=False, stop=True).then_inc(sem("m_ss"), 1)
                wide("mlstm", hd, 6, 7, part=(6, KC))

            for s in range(2):
                wide("mlstm", 0, 6, s)
            with pe.Fori(0, MH) as hd:
                mlstm_head(hd)

            UA = AH * NB

            def fox_scores(t, tt, k):
                e, b = k // NB, k % NB
                H = slice(e * DH, e * DH + DH)
                W = (b + 1) * P
                pe.wait_ge(sem("probs"), t * 8 + (UA + k - 1))
                if k == 0:
                    pe.wait_ge(sem("f_qk"), primed(t * 2 + 2))
                dst = bank[2 + k % 2]
                nc.tensor.matmul(dst[:, 0:W], fq[H, tt, b * P:W], fk[H, tt, 0:W], start=True, stop=False, skip_group_check=True)
                nc.tensor.matmul(dst[:, 0:W], sel[:, bass.ds(t * 2 + e, 1), :].rearrange("p a n -> p (a n)"), fsp[:, 0:W],
                                 start=False, stop=False, skip_group_check=True)
                nc.tensor.matmul(dst[:, W - P:W], identb[:], leb[:], start=False, stop=True,
                                 skip_group_check=True).then_inc(sem("scores"), 1)

            def fox_turn(t, k):
                b = k % NB
                pe.wait_ge(sem("probs_scaled"), primed(t * 8 + (UA + k + 1)))
                pe.wait_ge(sem("pT_copied"), t * 8 + (UA + k - 1))
                for j in range(b + 1):
                    tr = nc.tensor.transpose(bank[5 + k % 2][:, j * P:(j + 1) * P], fprob[:, k % 2, j * P:(j + 1) * P], ident[:])
                tr.then_inc(sem("pT_ready"), 1)

            def fox_values(t, k):
                e, b = k // NB, k % NB
                H = slice(e * DH, e * DH + DH)
                pe.wait_ge(sem("pT_copied"), t * 8 + (UA + k + 1))
                if k == 0:
                    pe.wait_ge(sem("f_v"), t + 1)
                    pe.wait_ge(sem("yb_lo"), primed(t))
                for j in range(b + 1):
                    mm = nc.tensor.matmul(bank[7][H, b * P:(b + 1) * P], fv[:, j, H], fpT[:, k % 2, j * P:(j + 1) * P],
                                          start=j == 0, stop=j == b, skip_group_check=True)
                mm.then_inc(sem("values"), 1)

            def fox_sums(p, i, s, j):
                pe.wait_ge(sem(f"evac{s % 2}"), primed(i * 3 + (TILE["fox"] + s) // 2 + 1))
                if j == 1:
                    pe.wait_ge(sem("f_ln"), p * 2 + 1)
                nc.tensor.matmul(bank[4][:], blk[:], fsq[:, j, :], start=True, stop=True).then_inc(sem("f_ss"), 1)

            def fox_turn_values(t, i, s):
                pe.wait_ge(sem(f"evac{s % 2}"), primed(i * 3 + (TILE["fox"] + s) // 2 + 1))
                transpose_values(fvraw, bank[4], "f_vT")

            def fox_pair(i, tt, more=True):
                t = i * 2 + tt
                for k in range(8):
                    fox_turn(t, k)
                    if k + 2 < 8:
                        fox_scores(t, tt, k + 2)
                    if k == 0:
                        fox_turn_values(t, i, 3 * tt + 2)
                    if more:
                        s = 3 * tt + 3
                        if k == 3:
                            fox_sums(t + 1, i, s, 0)
                        j, lo, hi = BESIDE[k]
                        wide("fox", i, 6, s + j, part=(lo, hi))
                        if k == 5:
                            fox_sums(t + 1, i, s + 1, 1)
                    fox_values(t, k)
                    if more and k >= 6:
                        fox_scores(t + 1, 1 - tt, k - 6)

            pe.wait_ge(sem("m_ln"), MH)
            fox_sums(0, 0, 0, 0)
            wide("fox", 0, 6, 2)
            fox_sums(0, 0, 1, 1)
            pe.wait_ge(sem("f_rows"), 3)
            fox_scores(0, 0, 0)
            fox_scores(0, 0, 1)
            with pe.Fori(0, FH // 4 - 1) as i:
                for tt in range(2):
                    fox_pair(i, tt)
            fox_pair(FH // 4 - 1, 0)
            fox_pair(FH // 4 - 1, 1, more=False)

            with pe.Fori(0, KC) as m:
                wide("merge", m, 4, 0)
                wide("merge", m, 4, 1, ih=yah, il=yal, ready=("m_y", 0))
                wide("merge", m, 4, 2)
                wide("merge", m, 4, 3, ih=ybh, il=ybl, ready=("yb_lo", 0))
            with pe.Fori(0, N_OUT // 2) as i:
                for s in range(2):
                    wide("out2", i, 2, s, ih=mgh, il=mgl, ready=("mg_lo", 0))
            norm_sum(4)
            with pe.Fori(0, FC // 2) as i:
                ff_step(2, i, 0)
            down(2)

        @block.scalar
        def _(act):
            def split(i, per, n0, k, width):
                s = (n0 + k) % 2
                act.wait_ge(sem(f"raw_in{s}"), i * (8 * per) + ((n0 + k) // 2 * 16 + 16))
                if not isinstance(i, int) or i * per + n0 + k >= 2:
                    act.wait_ge(sem("mm_done"), i * per + (n0 + k - 1))
                nc.scalar.activation(whi[:, s, 0:width], raw[:, s, 0:width], ACT.Copy).then_inc(sem("w_hi"), 1)

            def width(name):
                return DC if name.startswith("down") else WC

            def steps(name, per, count, body, after=None, i0=0):
                def ahead_in(i, last):
                    def ahead(k):
                        if last and k >= per - 2:
                            if after:
                                split(0, 2, SLAB[after], k - (per - 2), width(after))
                        else:
                            split(i, per, SLAB[name] + i0 * per + 2, k, width(name))
                    return ahead

                with act.Fori(0, count - 1) as i:
                    body(i, ahead_in(i, False))
                body(count - 1, ahead_in(count - 1, True))

            def matmuls(n):
                act.wait_ge(sem("mm_done"), n)

            def square_chunk(r, m, k):
                if r > 0 or m > 0:
                    act.wait_ge(sem("ssum"), primed(m + (KC * r - 1)))
                nc.scalar.activation(sqn[:, k, :], chunk(h, m), ACT.Square).then_inc(sem("sq"), 1)

            def inverse_root(name, i, src, dst, width):
                nc.scalar.activation(dst, src, ACT.Ln, scale=1.0 / width, bias=epsc[:]).then_inc(sem(name + "_ln"), 1)
                act.wait_ge(sem(name + "_ln"), i + 1)
                nc.scalar.activation(dst, dst, ACT.Exp, scale=-0.5).then_inc(sem(name + "_rstd"), 1)

            def norm(r, shift=None):
                if r > 0:
                    act.preload_act_table_set("natural_log_exp_and_others")
                act.wait_ge(sem("norm_sum"), primed(r + 1))
                inverse_root("norm", r, bank[4][:], rstd[:], D)
                for c in range(KC):
                    act.wait_ge(sem("x_scaled"), KC * r + c + 1)
                    if shift is None:
                        nc.scalar.activation(xh[:, c, :], tmp[c % 3], ACT.Copy).then_inc(sem("x_hi"), 1)
                        continue
                    sh = modc[:, shift * KC + c:shift * KC + c + 1]
                    if c % 2:
                        nc.scalar.activation(tmp[c % 3], tmp[c % 3], ACT.Identity, bias=sh).then_inc(sem("x_shifted"), 1)
                        act.wait_ge(sem("x_shifted"), (r - 2) * (KC // 2) + c // 2 + 1)
                        nc.scalar.activation(xh[:, c, :], tmp[c % 3], ACT.Copy).then_inc(sem("x_hi"), 1)
                    else:
                        nc.scalar.activation(xh[:, c, :], tmp[c % 3], ACT.Identity, bias=sh).then_inc(sem("x_hi"), 1)

            act.preload_act_table_set("natural_log_exp_and_others")
            act.wait_ge(sem("ones"), 1)
            for c in range(KC):
                if c % 2 == 0:
                    act.wait_ge(sem(f"x_in{c // 2}"), 16)
                square_chunk(0, c, c % 2)
            for dst, at, n in ((ident, 0, P), (blk, P, P), (rot, 2 * P, P), (ge, 3 * P, P), (leconst, 4 * P, P),
                               (cos, 5 * P, S), (sin, 5 * P + S, S)):
                act.dma_start(dst[:], const_in[:, at:at + n]).then_inc(sem("const_in"), 16)
            act.dma_start(rel[:], rel_in).then_inc(sem("rel_in"), 16)
            for k in range(2):
                split(0, 2, 0, k, WC)
            norm(0)

            def rope_tile(p):
                matmuls(p + 1)
                act.wait_ge(sem("rope_out"), primed(max(p - 1, 0)))
                nc.scalar.activation(rsq[:], proj[p % 2][:], ACT.Square)
                nc.scalar.activation(rraw[:, p % 2, :], proj[p % 2][:], ACT.Identity,
                                     scale=c1("q_norm" if p else "k_norm")).then_inc(sem(f"evac{p % 2}"), 1)
                split(0, 2, 0, p + 2, WC)

            def rope_roots(p):
                act.wait_ge(sem("rope_ss"), p + 1)
                if p > 0:
                    act.wait_ge(sem("rope_out"), primed(p))
                inverse_root("rope", p, bank[5][:], rr[:], DH)

            def win_exps(t, k):
                e = k // NB
                act.wait_ge(sem("negmax"), t * 8 + (k + 1))
                if k >= 2:
                    act.wait_ge(sem("pT_ready"), t * 8 + (k - 1))
                st = stat[:, k % 2, :]
                nc.scalar.activation(prob[:, k % 2, 0:window(k)], bank[2 + k % 2][:, 0:window(k)], ACT.Exp, bias=st[:, 1:2],
                                     accum_out=st[:, 2:3]).then_inc(sem("probs"), 1)
                nc.scalar.activation(st[:, 3:4], c1("sink", t + e * (AH // 2)), ACT.Exp, bias=st[:, 1:2]).then_inc(sem("sink_exp"), 1)

            def win_copy(t, k):
                act.wait_ge(sem("pT_ready"), t * 8 + (k + 1))
                if k >= 2:
                    act.wait_ge(sem("values"), t * 8 + (k - 1))
                nc.scalar.activation(pT[:, k % 2, 0:window(k)], bank[5 + k % 2][:, 0:window(k)], ACT.Copy).then_inc(sem("pT_copied"), 1)

            def ret_decays(t):
                act.wait_ge(sem("decay_log"), t * 4 + 4)
                for e in range(2):
                    at, lo, hi = e * REL, S - P, S
                    fwd = lg[:, bass.ds(t * 2 + e, 1)]
                    bwd = lg[:, bass.ds(t * 2 + (RH + e), 1)]
                    nc.scalar.activation(decay[:, at:at + lo], rel[:, REL:REL + lo], ACT.Exp, scale=bwd)
                    nc.scalar.activation(decay[:, at + hi:at + REL], rel[:, hi:REL], ACT.Exp, scale=fwd)
                    nc.scalar.activation(decay[:, at + lo:at + hi], decay[:, at + lo:at + hi], ACT.Exp).then_inc(sem("decay"), 1)

            def ret_tile(t, j):
                matmuls(t * 4 + (SLAB["ret"] + j + 1))
                act.wait_ge(sem("rope_out"), primed(t * 2 + QT))
                nc.scalar.activation(rraw[:, j, :], proj[j][:], ACT.Copy, scale=DH ** -0.5 if j else 1.0).then_inc(sem(f"evac{j}"), 1)
                split(t, 4, SLAB["ret"], j + 2, WC)

            def mixing_step(t, more=True):
                n = SLAB["ret"]
                for k in range(8):
                    win_copy(t, k)
                    if k + 2 < 8:
                        win_exps(t, k + 2)
                    if k == 1:
                        ret_tile(t, 0)
                    if k == 4:
                        ret_tile(t, 1)
                act.wait_ge(sem("values"), t * 8 + 8)
                nc.scalar.activation(chunk(yh, t * 2), bank[7][:], ACT.Copy).then_inc(sem("y_hi"), 1)
                matmuls(t * 4 + (n + 3))
                nc.scalar.activation(vraw[:], proj[0][:], ACT.Copy).then_inc(sem("evac0"), 1)
                split(t, 4, n, 4, WC)
                ret_decays(t)
                act.preload_act_table(ACT.Silu)
                act.wait_ge(sem("vT"), t + 2)
                nc.scalar.activation(rvtok[:].rearrange("p b n -> p (b n)"), bank[4][:], ACT.Copy).then_inc(sem("vtok"), 1)
                matmuls(t * 4 + (n + 4))
                nc.scalar.activation(rsil[:], proj[1][:], ACT.Silu).then_inc(sem("evac1"), 1)
                split(t, 4, n, 5, WC)
                act.preload_act_table_set("natural_log_exp_and_others")
                if more:
                    win_exps(t + 1, 0)
                act.wait_ge(sem("ret_values"), t * 8 + 8)
                nc.scalar.activation(rsq[:], bank[4][:], ACT.Square).then_inc(sem("ret_sq"), 1)
                if more:
                    win_exps(t + 1, 1)
                act.wait_ge(sem("ret_ss"), t + 1)
                inverse_root("ret", t, bank[7][:], rr[:], DH)

            for p in range(QT):
                rope_tile(p)
                if p == QT - 1:
                    win_exps(0, 0)
                rope_roots(p)
            matmuls(N_ATT)
            nc.scalar.activation(vraw[:], proj[1][:], ACT.Copy).then_inc(sem("evac1"), 1)
            split(0, 2, 0, N_ATT + 1, WC)
            win_exps(0, 1)
            act.wait_ge(sem("vT"), 1)
            nc.scalar.activation(vtok[:].rearrange("p b n -> p (b n)"), bank[4][:], ACT.Copy).then_inc(sem("vtok"), 1)
            act.wait_ge(sem("rel_in"), 16)
            with act.Fori(0, AH // 2 - 1) as t:
                mixing_step(t)
            mixing_step(AH // 2 - 1, more=False)

            def square_added(r, name, q, i, s):
                act.wait_ge(sem(f"evac{s}"), primed(i + ((TILE[name] + s) // 2 + 1)))
                square_chunk(r, i * 2 + s, s)

            def out_step(r, name):
                def step(i, ahead):
                    for s in range(2):
                        ahead(s)
                        square_added(r, name, 0, i, s)
                return step

            def down_step(r, name):
                def step(i, ahead):
                    for s in range(2):
                        ahead(2 * s)
                        ahead(2 * s + 1)
                        if r is not None:
                            square_added(r, name, 0, i, s)
                return step

            def ff_step(run, i0):
                def step(i, ahead):
                    for jj in range(2):
                        matmuls(i * 4 + (SLAB[f"ff{run}"] + 4 * i0 + 2 * jj + 1))
                        nc.scalar.activation(gsil[:, jj, :], proj[0][:], ACT.Silu).then_inc(sem("evac0"), 1)
                        ahead(2 * jj)
                        ahead(2 * jj + 1)
                        j = i * 2 + (2 * i0 + jj)
                        act.wait_ge(sem("evac1"), primed(i * 2 + (TILE[f"ff{run}"] // 2 + 2 * i0 + jj + 1)))
                        nc.scalar.activation(chunk(acth, j), aprod[:, jj, :], ACT.Copy).then_inc(sem("act_hi"), 1)
                return step

            steps("out", 2, N_OUT // 2, out_step(1, "out"), "ff0")
            norm(1)
            act.preload_act_table(ACT.Silu)
            nc.scalar.activation(csil[:], col[:, COL["c"]:COL["c"] + KC], ACT.Silu).then_inc(sem("c_silu"), 1)
            steps("ff0", 4, FC // 2, ff_step(0, 0), "down0")
            steps("down0", 4, N_DOWN // 4, down_step(2, "down0"), "ff1")

            norm(2, shift=0)
            act.preload_act_table(ACT.Silu)
            steps("ff1", 4, FC // 2, ff_step(1, 0), "down1")
            steps("down1", 4, N_DOWN // 4, down_step(3, "down1"), "mlstm")
            norm(3, shift=3)

            act.wait_ge(sem("gates"), 1)
            nc.scalar.activation(zg[:], bank[4][0:96, :], ACT.Identity, bias=c1("b_gates", rows=slice(0, 96))).then_inc(sem("gates_out"), 1)
            nc.scalar.activation(zi[:], bank[4][64:64 + MH, :], ACT.Identity,
                                 bias=c1("b_gates", rows=slice(64, 64 + MH))).then_inc(sem("gates_out"), 1)
            act.wait_ge(sem("g_abs"), 1)
            nc.scalar.activation(zt[0:48, :], zt[0:48, :], ACT.Exp, scale=-1.0).then_inc(sem("g_exp"), 1)
            act.wait_ge(sem("g_exp"), 1)
            nc.scalar.activation(zt[0:48, :], zt[0:48, :], ACT.Ln, bias=ones[0:48, 0:1]).then_inc(sem("g_ln"), 1)

            def place_rows(which, dst, rows, done):
                act.wait_ge(sem("row_split"), primed(3 * which + 3))
                for j in range(3):
                    n = rows.stop - rows.start
                    nc.scalar.activation(dst[32 * j:32 * j + n, :], gsp[rows, j, :], ACT.Copy).then_inc(sem(done), 1)

            def conv_tile(hd, j, i, s):
                matmuls(i * 6 + (SLAB["mlstm"] + s + 1))
                act.wait_ge(sem("m_conv"), primed(hd * 2))
                nc.scalar.activation(qz[:, j, CONV - 1:], proj[j][:], ACT.Identity, bias=c1("b_mlstm", i * 6 + s)).then_inc(sem(f"evac{j}"), 1)
                split(i, 6, SLAB["mlstm"], s + 2, WC)

            def mlstm_weight(hd, b):
                act.wait_ge(sem("m_weighted"), primed(hd * NB + max(b - 1, 0)))
                a = acol[:, bass.ds(hd + b * MH, 1)]
                if b < NB - 1:
                    nc.scalar.activation(Dm[:, b % 2, P:S - b * P], nM[:, (b + 1) * P:S], ACT.Exp, bias=a)
                nc.scalar.activation(Dm[:, b % 2, 0:P], nMd[:, b * P:(b + 1) * P], ACT.Exp, bias=a).then_inc(sem("m_D"), 1)

            def mlstm_head(hd, more=True):
                n = SLAB["mlstm"]
                for j in range(2):
                    matmuls(hd * 6 + (n + j + 3))
                    act.wait_ge(sem("m_turned"), primed(hd * 2))
                    nc.scalar.activation(mvT[:, j, :], proj[j][:], ACT.Identity, bias=c1("b_mlstm", hd * 6 + (j + 2))).then_inc(sem(f"evac{j}"), 1)
                    split(hd, 6, n, j + 4, WC)
                act.preload_act_table(ACT.Silu)
                for j in range(2):
                    act.wait_ge(sem("m_conv"), primed(hd * 2 + (j + 1)))
                    act.wait_ge(sem("m_values"), primed(hd * NB))
                    nc.scalar.activation(qk[:, j, :], cv[:, j, :], ACT.Silu).then_inc(sem("m_qk"), 1)
                act.preload_act_table_set("natural_log_exp_and_others")
                matmuls(hd * 6 + (n + 5))
                act.wait_ge(sem("m_gated"), primed(hd * 2))
                nc.scalar.activation(so[:, 0, :], proj[0][:], ACT.Identity, bias=c1("b_mlstm", hd * 6 + 4)).then_inc(sem("evac0"), 1)
                split(hd, 6, n, 6, WC)
                for j in range(2):
                    act.wait_ge(sem("m_turned"), primed(hd * 2 + (j + 1)))
                    nc.scalar.activation(mv[:, :, j * P:(j + 1) * P], bank[2 + j][:].rearrange("p (b n) -> p b n", b=NB),
                                         ACT.Copy).then_inc(sem("m_v"), 1)
                act.wait_ge(sem("m_bcast"), hd * 2 + 1)
                act.wait_ge(sem("m_nMd"), primed(hd))
                nc.scalar.activation(nM[:], bank[4][:], ACT.Copy).then_inc(sem("m_nM"), 1)
                act.wait_ge(sem("m_acol"), hd + 1)
                nc.scalar.activation(acol[:], bank[6][:, 0:NB * MH], ACT.Copy).then_inc(sem("m_acols"), 1)
                act.wait_ge(sem("m_bcast"), hd * 2 + 2)
                act.wait_ge(sem("m_normed"), primed(hd * 2))
                nc.scalar.activation(emm[:], bank[5][:], ACT.Exp).then_inc(sem("m_emm"), 1)
                act.wait_ge(sem("m_nMd"), primed(hd + 1))
                act.wait_ge(sem("m_acols"), hd + 1)
                mlstm_weight(hd, 0)
                mlstm_weight(hd, 1)
                matmuls(hd * 6 + (n + 6))
                nc.scalar.activation(so[:, 1, :], proj[1][:], ACT.Identity, bias=c1("b_mlstm", hd * 6 + 5)).then_inc(sem("evac1"), 1)
                split(hd, 6, n, 7, WC)
                mlstm_weight(hd, 2)
                mlstm_weight(hd, 3)
                act.preload_act_table(ACT.Sigmoid)
                act.wait_ge(sem("evac1"), primed(hd * 3 + (TILE["mlstm"] // 2 + 3)))
                for j in range(2):
                    nc.scalar.activation(so[:, j, :], so[:, j, :], ACT.Sigmoid).then_inc(sem("m_sig"), 1)
                act.preload_act_table_set("natural_log_exp_and_others")
                if more:
                    conv_tile(hd + 1, 0, hd, 6)
                else:
                    fox_tile(0, 0, 0, 0)
                act.wait_ge(sem("m_out"), primed(hd * 2 + 2))
                nc.scalar.activation(hsq[:, 0, :], hm[:, 0, :], ACT.Square)
                nc.scalar.activation(hsq[:, 1, :], hm[:, 1, :], ACT.Square).then_inc(sem("m_sq"), 1)
                act.wait_ge(sem("m_ss"), hd + 1)
                inverse_root("m", hd, bank[4][:], hrs[:], DV)
                if more:
                    conv_tile(hd + 1, 1, hd, 7)
                else:
                    fox_tile(0, 0, 1, 1)
                for j in range(2):
                    act.wait_ge(sem("m_gated"), primed(hd * 2 + (j + 1)))
                    nc.scalar.activation(chunk(yah, hd * 2 + j), hn[:, j, :], ACT.Copy).then_inc(sem("m_yhi"), 1)

            def fox_tile(p, i, s, j):
                matmuls(i * 6 + (SLAB["fox"] + s + 1))
                act.wait_ge(sem("f_qk"), primed(p * 2))
                bias = c1("b_fox", i * 6 + s)
                nc.scalar.activation(fsq[:, j, :], proj[s % 2][:], ACT.Square, bias=bias)
                nc.scalar.activation(fraw[:, j, :], proj[s % 2][:], ACT.Identity, bias=bias).then_inc(sem(f"evac{s % 2}"), 1)
                split(i, 6, SLAB["fox"], s + 2, WC)
            act.wait_ge(sem("pads"), 1)
            conv_tile(0, 0, 0, 0)
            act.wait_ge(sem("rows_clear"), 3)
            place_rows(0, msM, slice(0, MH), "m_rows")
            conv_tile(0, 1, 0, 1)
            place_rows(1, msm, slice(0, MH), "m_rows")
            with act.Fori(0, MH - 1) as hd:
                mlstm_head(hd)
            mlstm_head(MH - 1, more=False)
            place_rows(2, fsp, slice(32, 48), "f_rows")

            UA = AH * NB

            def fox_exps(t, k):
                W = (k % NB + 1) * P
                act.wait_ge(sem("negmax"), t * 8 + (UA + k + 1))
                act.wait_ge(sem("pT_ready"), t * 8 + (UA + k - 1))
                st = stat[:, k % 2, :]
                nc.scalar.activation(fprob[:, k % 2, 0:W], bank[2 + k % 2][:, 0:W], ACT.Exp, bias=st[:, 1:2],
                                     accum_out=st[:, 2:3]).then_inc(sem("probs"), 1)

            def fox_copy(t, k):
                W = (k % NB + 1) * P
                act.wait_ge(sem("pT_ready"), t * 8 + (UA + k + 1))
                act.wait_ge(sem("values"), t * 8 + (UA + k - 1))
                nc.scalar.activation(fpT[:, k % 2, 0:W], bank[5 + k % 2][:, 0:W], ACT.Copy).then_inc(sem("pT_copied"), 1)

            def fox_values(i, s):
                matmuls(i * 6 + (SLAB["fox"] + s + 1))
                nc.scalar.activation(fvraw[:], proj[s % 2][:], ACT.Identity, bias=c1("b_fox", i * 6 + s)).then_inc(sem(f"evac{s % 2}"), 1)

            def fox_roots(p, j):
                act.wait_ge(sem("f_ss"), p * 2 + (j + 1))
                nc.scalar.activation(frs[:, j, :], bank[4][:], ACT.Ln, scale=1.0 / DH, bias=epsc[:]).then_inc(sem("f_ln"), 1)
                act.wait_ge(sem("f_ln"), p * 2 + (j + 1))
                nc.scalar.activation(frs[:, j, :], frs[:, j, :], ACT.Exp, scale=-0.5).then_inc(sem("f_rstd"), 1)

            def fox_pair(i, tt, more=True):
                t = i * 2 + tt
                s = 3 * tt + 3
                for k in range(8):
                    fox_copy(t, k)
                    if k == 0:
                        act.wait_ge(sem("f_vT"), t + 1)
                        nc.scalar.activation(fv[:].rearrange("p b n -> p (b n)"), bank[4][:], ACT.Copy).then_inc(sem("f_v"), 1)
                    if k + 2 < 8:
                        fox_exps(t, k + 2)
                    if more:
                        if k == 1:
                            fox_tile(t + 1, i, s, 0)
                        if k == 3:
                            fox_roots(t + 1, 0)
                        if k == 4:
                            fox_tile(t + 1, i, s + 1, 1)
                        if k == 5:
                            fox_roots(t + 1, 1)
                        if k == 7:
                            fox_exps(t + 1, 0)
                            fox_values(i, s + 2)
                act.wait_ge(sem("values"), t * 8 + (UA + 8))
                nc.scalar.activation(chunk(ybh, t), bank[7][:], ACT.Copy).then_inc(sem("yb_hi"), 1)
                if more:
                    fox_exps(t + 1, 1)
                    split(i, 6, SLAB["fox"], s + 4, WC)

            fox_roots(0, 0)
            fox_values(0, 2)
            fox_roots(0, 1)
            split(0, 6, SLAB["fox"], 4, WC)
            fox_exps(0, 0)
            fox_exps(0, 1)
            with act.Fori(0, FH // 4 - 1) as i:
                for tt in range(2):
                    fox_pair(i, tt)
            fox_pair(FH // 4 - 1, 0)
            fox_pair(FH // 4 - 1, 1, more=False)

            def merge_step(m, ahead):
                n = SLAB["merge"]
                for j in range(2):
                    matmuls(m * 4 + (n + 2 * j + 1))
                    nc.scalar.activation(sg[:, j, :], proj[0][:], ACT.Sigmoid, bias=c1("b_merge", m * 2 + j)).then_inc(sem("evac0"), 1)
                    ahead(2 * j)
                    ahead(2 * j + 1)
                act.wait_ge(sem("mg"), primed(m + 1))
                nc.scalar.activation(chunk(mgh, m), mg[:, 0, :], ACT.Copy).then_inc(sem("mg_hi"), 1)

            act.preload_act_table(ACT.Sigmoid)
            steps("merge", 4, KC, merge_step, "out2")
            steps("out2", 2, N_OUT // 2, out_step(4, "out2"), "ff2")
            norm(4, shift=6)
            act.preload_act_table(ACT.Silu)
            steps("ff2", 4, FC // 2, ff_step(2, 0), "down2")
            steps("down2", 4, N_DOWN // 4, down_step(None, "down2"))

        @block.vector
        def _(dve):
            V = nc.vector

            def matmuls(n):
                dve.wait_ge(sem("mm_done"), n)

            def add_square(r, m, k):
                dve.wait_ge(sem("sq"), m + (KC * r + 1))
                dve.wait_ge(sem("ssum"), primed(m + KC * r))
                V.tensor_tensor(ssum[:], ssum[:], sqn[:, k, :], ALU.add).then_inc(sem("ssum"), 1)

            def clear_sum(r):
                dve.wait_ge(sem("norm_sum"), primed(r))
                V.memset(ssum[:], 0.0).then_inc(sem("ssum_clear"), 1)
                dve.wait_ge(sem("ssum_clear"), r + 1)

            def norm(r, weight, shift=None):
                def scaled(c):
                    if c >= 3:
                        dve.wait_ge(sem(f"x_lo{(c - 3) % 2}"), primed(r * (KC // 2) + (c - 3) // 2 + 1))
                    V.scalar_tensor_tensor(tmp[c % 3], chunk(h, c), weight(c), rstd[:], ALU.mult, ALU.mult).then_inc(sem("x_scaled"), 1)

                def low(c):
                    dve.wait_ge(sem("x_hi"), KC * r + c + 1)
                    sh = 0.0 if shift is None else modc[:, shift * KC + c:shift * KC + c + 1]
                    V.scalar_tensor_tensor(xl[:, c, :], tmp[c % 3], sh, xh[:, c, :].bitcast(F32), ALU.add,
                                           ALU.subtract).then_inc(sem("x_lo0"), 1)

                dve.wait_ge(sem("norm_rstd"), r + 1)
                for c in range(3):
                    scaled(c)
                for c in range(0, KC, 2):
                    low(c)
                    for d in (c + 3, c + 4):
                        if d < KC:
                            scaled(d)

            V.memset(epsc[:], EPS)
            V.memset(ones[:], 1.0).then_inc(sem("ones"), 1)
            clear_sum(0)
            for c in range(KC):
                add_square(0, c, c % 2)
            dve.wait_ge(sem("cols_in"), 16)
            V.tensor_scalar(lg[:], col[:, COL["decay_f"]:COL["decay_f"] + 2 * RH], -1.0, None, ALU.mult).then_inc(sem("lg"), 1)
            dve.wait_ge(sem("lg"), 1)
            V.tensor_tensor(lg[:], lg[:], col[:, COL["decay_f"]:COL["decay_f"] + 2 * RH], ALU.min).then_inc(sem("lg"), 1)
            V.tensor_scalar(c1("q_norm"), c1("q_norm"), DH ** -0.5, None, ALU.mult).then_inc(sem("q_scale"), 1)
            V.tensor_scalar(col[:, COL["fox_q"]:COL["fox_q"] + FH // 2], col[:, COL["fox_q"]:COL["fox_q"] + FH // 2], DH ** -0.5, None,
                            ALU.mult).then_inc(sem("q_scale"), 1)
            norm(0, lambda c: c1("attn_norm", c))
            dve.wait_ge(sem("const_in"), 16 * 7)
            V.tensor_copy(identb[:], ident[:])
            V.tensor_copy(geb[:], ge[:])
            V.tensor_copy(leb[:], leconst[:]).then_inc(sem("const_ready"), 1)

            def rope_part(p, slot, turned, part):
                if part == 0:
                    dve.wait_ge(sem("rope_rot"), p + 1)
                    dve.wait_ge(sem("rope_out"), primed(p))
                    V.tensor_tensor(rt[:, 0, :], bank[turned][:], sin[:], ALU.mult).then_inc(sem("rope_part"), 1)
                else:
                    V.tensor_tensor(rt[:, 1, :], rraw[:, slot, :], cos[:], ALU.mult).then_inc(sem("rope_part"), 1)

            def normed_rope(p, dst):
                for part in range(2):
                    rope_part(p, p % 2, 6, part)
                dve.wait_ge(sem("rope_part"), p * 2 + 2)
                V.tensor_tensor(rt[:, 0, :], rt[:, 0, :], rt[:, 1, :], ALU.add).then_inc(sem("rope_sum"), 1)
                dve.wait_ge(sem("rope_sum"), p + 1)
                dve.wait_ge(sem("rope_rstd"), p + 1)
                V.tensor_tensor(dst, rt[:, 0, :], rr[:], ALU.mult).then_inc(sem("rope_out"), 1)

            def ret_rope(t, j, part):
                p = t * 2 + (QT + j)
                if part < 2:
                    rope_part(p, j, 4, part)
                else:
                    dve.wait_ge(sem("rope_part"), p * 2 + 2)
                    V.tensor_tensor((rqf, rkf)[j][:], rt[:, 0, :], rt[:, 1, :], ALU.add).then_inc(sem("rope_out"), 1)

            def queries(t):
                V.tensor_copy(qf[:], chunk(qall, t)).then_inc(sem("q_cur"), 1)

            def maxima(u, k, width, sink=None):
                st = stat[:, k % 2, :]
                dve.wait_ge(sem("scores"), u + (k + 1))
                if not isinstance(u, int) or u + k > 0:
                    dve.wait_ge(sem("probs_scaled"), primed(u + (k - 1)))
                V.tensor_reduce(st[:, 0:1], bank[2 + k % 2][:, 0:width], AX.X, ALU.max).then_inc(sem("rowmax"), 1)
                dve.wait_ge(sem("rowmax"), u + (k + 1))
                if sink is not None:
                    V.tensor_scalar(st[:, 1:2], st[:, 0:1], sink, -1.0, ALU.max, ALU.mult).then_inc(sem("negmax"), 1)
                else:
                    V.tensor_scalar(st[:, 1:2], st[:, 0:1], -1.0, None, ALU.mult).then_inc(sem("negmax"), 1)

            def win_maxima(t, k):
                maxima(t * 8, k, window(k), c1("sink", t + (k // NB) * (AH // 2)))

            def win_scale(t, k):
                st = stat[:, k % 2, :]
                W = window(k)
                dve.wait_ge(sem("sink_exp"), t * 8 + (k + 1))
                V.tensor_tensor(st[:, 4:5], st[:, 2:3], st[:, 3:4], ALU.add).then_inc(sem("den"), 1)
                dve.wait_ge(sem("den"), t * 8 + (k + 1))
                V.reciprocal(st[:, 5:6], st[:, 4:5]).then_inc(sem("rden"), 1)
                dve.wait_ge(sem("rden"), t * 8 + (k + 1))
                V.tensor_scalar(prob[:, k % 2, 0:W], prob[:, k % 2, 0:W], st[:, 5:6], None, ALU.mult).then_inc(sem("probs_scaled"), 1)

            def ret_decay_logs(t):
                bands = [decay[:, e * REL + S - P:e * REL + S] for e in range(2)]
                for e in range(2):
                    V.tensor_scalar(bands[e], rel[:, S - P:S], lg[:, bass.ds(t * 2 + e, 1)], None, ALU.mult).then_inc(sem("decay_log"), 1)
                for e in range(2):
                    dve.wait_ge(sem("decay_log"), t * 4 + 2)
                    V.scalar_tensor_tensor(bands[e], rel[:, REL + S - P:REL + S], lg[:, bass.ds(t * 2 + (RH + e), 1)], bands[e], ALU.mult,
                                           ALU.add).then_inc(sem("decay_log"), 1)

            def mixing_step(t, more=True):
                for k in range(8):
                    if k > 1:
                        win_scale(t, k)
                    if k + 2 < 8:
                        win_maxima(t, k + 2)
                    if 4 <= k < 7:
                        ret_rope(t, 0, k - 4)
                ret_decay_logs(t)
                for part in range(3):
                    ret_rope(t, 1, part)
                if more:
                    queries(t + 1)
                dve.wait_ge(sem("y_hi"), t + 1)
                V.tensor_tensor(chunk(yl, t * 2), bank[7][:], chunk(yh, t * 2).bitcast(F32), ALU.subtract).then_inc(sem("y_lo"), 1)
                dve.wait_ge(sem("decay"), t * 2 + 2)
                for k in range(8):
                    e, b = k // NB, k % NB
                    at = e * REL + S - P - b * P
                    dve.wait_ge(sem("ret_scores"), t * 8 + (k + 1))
                    if k >= 2:
                        dve.wait_ge(sem("ret_values"), t * 8 + (k - 1))
                    V.tensor_tensor(prob[:, k % 2, :], bank[2 + k % 2][:], decay[:, at:at + S], ALU.mult).then_inc(sem("ret_decayed"), 1)
                if more:
                    win_maxima(t + 1, 0)
                    win_scale(t + 1, 0)
                    win_maxima(t + 1, 1)
                    win_scale(t + 1, 1)
                dve.wait_ge(sem("ret_rstd"), t + 1)
                V.tensor_tensor(ry[:], bank[4][:], rr[:], ALU.mult).then_inc(sem("ret_normed"), 1)
                dve.wait_ge(sem("ret_normed"), t + 1)
                V.scalar_tensor_tensor(ry[:], ry[:], c1("ret_norm", t), rsil[:], ALU.mult, ALU.mult).then_inc(sem("ret_y"), 1)
                dve.wait_ge(sem("ret_y"), t + 1)
                V.tensor_copy(chunk(yh, t * 2 + 1), ry[:]).then_inc(sem("ret_y_hi"), 1)
                dve.wait_ge(sem("ret_y_hi"), t + 1)
                V.tensor_tensor(chunk(yl, t * 2 + 1), ry[:], chunk(yh, t * 2 + 1).bitcast(F32), ALU.subtract).then_inc(sem("y_lo"), 1)

            dve.wait_ge(sem("lg"), 2)
            for p in range(QT):
                if p == QT - 1:
                    win_maxima(0, 0)
                    win_maxima(0, 1)
                    win_scale(0, 0)
                normed_rope(p, qall[:, p - 1, :] if p else kf[:])
                if p == QT - 1:
                    win_scale(0, 1)
                if p == 1:
                    dve.wait_ge(sem("rope_out"), primed(2))
                    queries(0)
            dve.wait_ge(sem("rel_in"), 16)
            with dve.Fori(0, AH // 2 - 1) as t:
                mixing_step(t)
            mixing_step(AH // 2 - 1, more=False)

            def add_tile(name, per, r, gate, i, s):
                m = i * 2 + s
                matmuls(i * (2 * per) + (SLAB[name] + per * (s + 1)))
                V.scalar_tensor_tensor(chunk(h, m), proj[s][:], gate(m), chunk(h, m), ALU.mult, ALU.add).then_inc(sem(f"evac{s}"), 1)
                if r is not None:
                    add_square(r, m, s)

            def add_tiles(name, per, r, gate):
                if r is not None:
                    clear_sum(r)
                with dve.Fori(0, KC // 2) as i:
                    for s in range(2):
                        add_tile(name, per, r, gate, i, s)

            def ff_product(run, i, i0, jj):
                j = i * 2 + (2 * i0 + jj)
                matmuls(i * 4 + (SLAB[f"ff{run}"] + 4 * i0 + 2 * jj + 2))
                dve.wait_ge(sem("evac0"), primed(i * 2 + (TILE[f"ff{run}"] // 2 + 2 * i0 + jj + 1)))
                dve.wait_ge(sem("act_lo"), primed(j + run * FC))
                V.tensor_tensor(aprod[:, jj, :], proj[1][:], gsil[:, jj, :], ALU.mult).then_inc(sem("evac1"), 1)

            def ff_low(run, i, i0, jj):
                j = i * 2 + (2 * i0 + jj)
                dve.wait_ge(sem("act_hi"), j + (run * FC + 1))
                V.tensor_tensor(chunk(actl, j), aprod[:, jj, :], chunk(acth, j).bitcast(F32), ALU.subtract).then_inc(sem("act_lo"), 1)

            def ada_parts(i, ks):
                for k in ks:
                    dve.wait_ge(sem(f"ada_in{k % 2}"), i * (KC * 8) + (k // 2 * 16 + 16))
                    if k == 0:
                        V.tensor_scalar(adac[:], adaw[:, 0, :], csil[:, 0:1], None, ALU.mult).then_inc(sem("ada_acc"), 1)
                    else:
                        dve.wait_ge(sem("ada_acc"), primed(i * KC + k))
                        V.scalar_tensor_tensor(adac[:], adaw[:, k % 2, :], csil[:, k:k + 1], adac[:], ALU.mult,
                                               ALU.add).then_inc(sem("ada_acc"), 1)

            def mod_column(v):
                dve.wait_ge(sem("mod_sum"), primed(v + 1))
                V.tensor_tensor(modc[:, bass.ds(v * KC, KC)], bank[2][:, 0:KC], col[:, bass.ds(v * KC + COL["b_ada"], KC)],
                                ALU.add).then_inc(sem("mod"), 1)

            def ff_beside_ada(i, i0, v):
                for jj in range(2):
                    ff_product(0, i, i0, jj)
                    if jj == 0 and i0 > 0:
                        mod_column(i)
                    ada_parts(v, range(4 * jj, 4 * jj + 2))
                    ff_low(0, i, i0, jj)
                    ada_parts(v, range(4 * jj + 2, 4 * jj + 4))

            add_tiles("out", 1, 1, lambda m: 1.0)
            norm(1, lambda c: c1("ffn_norm", c))
            dve.wait_ge(sem("c_silu"), 1)
            ff_beside_ada(0, 0, 0)
            with dve.Fori(0, NMOD - 1) as i:
                ff_beside_ada(i, 1, i + 1)
            for i0 in (NMOD, NMOD + 1):
                for jj in range(2):
                    ff_product(0, 0, i0, jj)
                    if i0 == NMOD and jj == 0:
                        mod_column(NMOD - 1)
                    ff_low(0, 0, i0, jj)
            dve.wait_ge(sem("mod"), NMOD)
            for r, name in enumerate(("ffn1_norm", "mix_norm", "ffn2_norm")):
                sc = modc[:, (3 * r + 1) * KC:(3 * r + 2) * KC]
                V.scalar_tensor_tensor(scl[:, r * KC:(r + 1) * KC], sc, 1.0, col[:, COL[name]:COL[name] + KC], ALU.add,
                                       ALU.mult).then_inc(sem("mod_cols"), 1)
                V.tensor_scalar(gat[:, r * KC:(r + 1) * KC], modc[:, (3 * r + 2) * KC:(3 * r + 3) * KC], 1.0 if r == 1 else 0.5, None,
                                ALU.mult).then_inc(sem("mod_cols"), 1)
            dve.wait_ge(sem("mod_cols"), 6)
            add_tiles("down0", 2, 2, lambda m: 1.0)

            def ff_products(run):
                with dve.Fori(0, FC // 2) as i:
                    for jj in range(2):
                        ff_product(run, i, 0, jj)
                        ff_low(run, i, 0, jj)

            def gate(r):
                return lambda m: gat[:, bass.ds(m + r * KC, 1)]

            norm(2, lambda c: scl[:, c:c + 1], shift=0)
            ff_products(1)
            add_tiles("down1", 2, 3, gate(0))

            dve.wait_ge(sem("gates_in"), 16)
            V.tensor_copy(ghi[:], gates_raw[:]).then_inc(sem("gates_split"), 1)
            dve.wait_ge(sem("gates_split"), 1)
            V.tensor_tensor(glo[:], gates_raw[:], ghi[:].bitcast(F32), ALU.subtract).then_inc(sem("gates_split"), 1)
            V.memset(qz[:, :, 0:CONV - 1], 0.0).then_inc(sem("pads"), 1)
            norm(3, lambda c: scl[:, KC + c:KC + c + 1], shift=3)

            dve.wait_ge(sem("gates_out"), 2)
            V.scalar_tensor_tensor(zt[0:48, :], zg[0:48, :], -1.0, zg[0:48, :], ALU.mult, ALU.max).then_inc(sem("g_abs"), 1)
            V.memset(zrow[:], 0.0).then_inc(sem("zeros"), 1)
            for t_ in (msM, msm, fsp):
                V.memset(t_[:], 0.0).then_inc(sem("rows_clear"), 1)
            dve.wait_ge(sem("g_ln"), 1)
            V.scalar_tensor_tensor(lf[:], zg[0:48, :], 0.0, zt[0:48, :], ALU.min, ALU.subtract).then_inc(sem("log_f"), 1)
            dve.wait_ge(sem("zeros"), 1)
            dve.wait_ge(sem("log_f"), 1)
            V.tensor_tensor_scan(cs[:], zrow[:], lf[:], 0.0, ALU.add, ALU.add).then_inc(sem("cum_f"), 1)

            def split_rows(which, rows, src):
                rest = [src, zt[rows, :], zg[rows, :]]
                for j in range(3):
                    V.tensor_copy(gsp[rows, j, :], rest[j]).then_inc(sem("row_split"), 1)
                    if j < 2:
                        dve.wait_ge(sem("row_split"), primed(3 * which + j + 1))
                        V.tensor_tensor(rest[j + 1], rest[j], gsp[rows, j, :], ALU.subtract).then_inc(sem("row_rest"), 1)
                        dve.wait_ge(sem("row_rest"), 2 * which + j + 1)

            H4 = slice(0, MH)
            dve.wait_ge(sem("cum_f"), 1)
            V.tensor_tensor(arow[:], zi[:], cs[H4, :], ALU.subtract).then_inc(sem("arow"), 1)
            dve.wait_ge(sem("arow"), 1)
            mrow, frow = lf[H4, :], zi[:]
            V.tensor_tensor_scan(mrow, arow[:], arow[:], 0.0, ALU.max, ALU.max).then_inc(sem("mrow"), 1)
            dve.wait_ge(sem("mrow"), 1)
            split_rows(0, H4, mrow)
            V.tensor_tensor(frow, cs[H4, :], mrow, ALU.add).then_inc(sem("frow"), 1)
            for g in range(FH):
                V.tensor_scalar(sel[:, g, :], ones[0:96, :], c1("sel", g, rows=slice(0, 96)), None, ALU.mult).then_inc(sem("sel_ready"), 1)
            dve.wait_ge(sem("frow"), 1)
            dve.wait_ge(sem("m_rows"), 3)
            split_rows(1, H4, frow)

            def convolve(hd):
                for j in range(2):
                    dve.wait_ge(sem(f"evac{j}"), primed(hd * 3 + (TILE["mlstm"] // 2 + 1)))
                    dve.wait_ge(sem("m_qk"), primed(hd * 2))
                    cw = lambda tap: c1("conv_w", hd * (2 * CONV) + (j * CONV + tap))
                    V.tensor_scalar(cv[:, j, :], qz[:, j, 0:S], cw(0), c1("conv_b", hd * 2 + j), ALU.mult, ALU.add).then_inc(sem("m_tap"), 1)
                    for tap in range(1, CONV):
                        dve.wait_ge(sem("m_tap"), hd * (2 * (CONV - 1)) + (j * (CONV - 1) + tap))
                        V.scalar_tensor_tensor(cv[:, j, :], qz[:, j, tap:tap + S], cw(tap), cv[:, j, :], ALU.mult,
                                               ALU.add).then_inc(sem("m_tap" if tap < CONV - 1 else "m_conv"), 1)

            def mlstm_head(hd, more=True):
                dve.wait_ge(sem("m_nM"), hd + 1)
                for b in range(NB):
                    ins = V.tensor_tensor(nMd[:, b * P:(b + 1) * P], nM[:, b * P:(b + 1) * P], ge[:], ALU.add)
                ins.then_inc(sem("m_nMd"), 1)
                for b in range(NB):
                    W = S - b * P
                    dve.wait_ge(sem("m_D"), hd * NB + (b + 1))
                    dve.wait_ge(sem("m_scores"), hd * NB + (b + 1))
                    dve.wait_ge(sem("m_values"), primed(hd * NB + max(b - 1, 0)))
                    V.scalar_tensor_tensor(sT[:, b % 2, 0:W], bank[2 + b % 2][:, 0:W], DQK ** -0.5, Dm[:, b % 2, 0:W], ALU.mult,
                                           ALU.mult).then_inc(sem("m_weighted"), 1)
                dve.wait_ge(sem("m_values"), primed(hd * NB + NB))
                dve.wait_ge(sem("m_emm"), hd + 1)
                dve.wait_ge(sem("m_y"), primed(hd * 2))
                V.tensor_scalar(mxr[:, 0, :], bank[7][:], -1.0, None, ALU.mult).then_inc(sem("m_den"), 1)
                dve.wait_ge(sem("m_den"), hd * 4 + 1)
                V.tensor_tensor(mxr[:, 0, :], mxr[:, 0, :], bank[7][:], ALU.max).then_inc(sem("m_den"), 1)
                dve.wait_ge(sem("m_den"), hd * 4 + 2)
                V.tensor_tensor(mxr[:, 0, :], mxr[:, 0, :], emm[:], ALU.max).then_inc(sem("m_den"), 1)
                dve.wait_ge(sem("m_den"), hd * 4 + 3)
                V.reciprocal(mxr[:, 1, :], mxr[:, 0, :]).then_inc(sem("m_den"), 1)
                dve.wait_ge(sem("m_den"), hd * 4 + 4)
                for j in range(2):
                    V.tensor_tensor(hm[:, j, :], bank[5 + j][:], mxr[:, 1, :], ALU.mult).then_inc(sem("m_out"), 1)
                dve.wait_ge(sem("m_rstd"), hd + 1)
                for j in range(2):
                    V.scalar_tensor_tensor(hn[:, j, :], hm[:, j, :], c1("mlstm_norm", hd * 2 + j), hrs[:], ALU.mult, ALU.mult).then_inc(sem("m_normed"), 1)
                dve.wait_ge(sem("m_sig"), hd * 2 + 2)
                dve.wait_ge(sem("m_normed"), primed(hd * 2 + 2))
                for j in range(2):
                    V.tensor_tensor(hn[:, j, :], hn[:, j, :], so[:, j, :], ALU.mult).then_inc(sem("m_gated"), 1)
                if more:
                    convolve(hd + 1)
                for j in range(2):
                    dve.wait_ge(sem("m_yhi"), hd * 2 + (j + 1))
                    V.tensor_tensor(chunk(yal, hd * 2 + j), hn[:, j, :], chunk(yah, hd * 2 + j).bitcast(F32), ALU.subtract).then_inc(sem("m_y"), 1)

            convolve(0)
            split_rows(2, slice(32, 48), cs[32:48, :])
            with dve.Fori(0, MH - 1) as hd:
                mlstm_head(hd)
            mlstm_head(MH - 1, more=False)

            UA = AH * NB

            def fox_maxima(t, k):
                maxima(t * 8 + UA, k, (k % NB + 1) * P)

            def fox_scale(t, k):
                st = stat[:, k % 2, :]
                W = (k % NB + 1) * P
                dve.wait_ge(sem("probs"), t * 8 + (UA + k + 1))
                V.reciprocal(st[:, 5:6], st[:, 2:3]).then_inc(sem("rden"), 1)
                dve.wait_ge(sem("rden"), t * 8 + (UA + k + 1))
                V.tensor_scalar(fprob[:, k % 2, 0:W], fprob[:, k % 2, 0:W], st[:, 5:6], None, ALU.mult).then_inc(sem("probs_scaled"), 1)

            def fox_normed(p, par, j):
                dve.wait_ge(sem("f_rstd"), p * 2 + (j + 1))
                V.scalar_tensor_tensor((fq, fk)[j][:, par, :], fraw[:, j, :], c1(("fox_q", "fox_k")[j], p), frs[:, j, :], ALU.mult,
                                       ALU.mult).then_inc(sem("f_qk"), 1)

            def fox_pair(i, tt, more=True):
                t = i * 2 + tt
                for k in range(8):
                    if k > 0:
                        fox_scale(t, k)
                    if k + 2 < 8:
                        fox_maxima(t, k + 2)
                    if more and k >= 5 and k < 7:
                        fox_normed(t + 1, 1 - tt, k - 5)
                if more:
                    fox_maxima(t + 1, 0)
                    fox_scale(t + 1, 0)
                    fox_maxima(t + 1, 1)
                dve.wait_ge(sem("yb_hi"), t + 1)
                V.tensor_tensor(chunk(ybl, t), bank[7][:], chunk(ybh, t).bitcast(F32), ALU.subtract).then_inc(sem("yb_lo"), 1)

            for j in range(2):
                fox_normed(0, 0, j)
            fox_maxima(0, 0)
            fox_maxima(0, 1)
            fox_scale(0, 0)
            with dve.Fori(0, FH // 4 - 1) as i:
                for tt in range(2):
                    fox_pair(i, tt)
            fox_pair(FH // 4 - 1, 0)
            fox_pair(FH // 4 - 1, 1, more=False)

            with dve.Fori(0, KC) as m:
                for j in range(2):
                    matmuls(m * 4 + (SLAB["merge"] + 2 * j + 2))
                    dve.wait_ge(sem("mg"), primed(m))
                    dve.wait_ge(sem("evac0"), primed(m * 2 + (TILE["merge"] // 2 + j + 1)))
                    V.tensor_tensor(br[:, j, :], proj[1][:], sg[:, j, :], ALU.mult).then_inc(sem("evac1"), 1)
                dve.wait_ge(sem("evac1"), primed(m * 2 + (TILE["merge"] // 2 + 2)))
                dve.wait_ge(sem("mg_lo"), primed(m))
                V.tensor_tensor(mg[:, 0, :], br[:, 0, :], br[:, 1, :], ALU.add).then_inc(sem("mg"), 1)
                dve.wait_ge(sem("mg_hi"), m + 1)
                V.tensor_tensor(chunk(mgl, m), mg[:, 0, :], chunk(mgh, m).bitcast(F32), ALU.subtract).then_inc(sem("mg_lo"), 1)
            add_tiles("out2", 1, 4, gate(1))
            norm(4, lambda c: scl[:, 2 * KC + c:2 * KC + c + 1], shift=6)
            ff_products(2)
            add_tiles("down2", 2, None, gate(2))


def constants():
    p = np.arange(P)
    ident = np.eye(P, dtype=np.float32)
    blk = (p[:, None] // DH == p[None, :] // DH).astype(np.float32)
    rot = np.zeros((P, P), np.float32)
    for o in range(P):
        if o % DH < DH // 2:
            rot[o + DH // 2, o] = -1.0
        else:
            rot[o - DH // 2, o] = 1.0
    ge = np.where(p[None, :] >= p[:, None], 0.0, NEG).astype(np.float32)
    le = np.where(p[None, :] <= p[:, None], 0.0, NEG).astype(np.float32)
    inv = (np.float32(10000.0) ** (-np.arange(0, DH, 2, dtype=np.float32) / np.float32(DH))).astype(np.float32)
    ang = inv[p % (DH // 2)][:, None] * np.arange(S, dtype=np.float32)[None, :]
    const = np.concatenate([ident, blk, rot, ge, le, np.cos(ang), np.sin(ang)], 1).astype(np.float32)
    diff = np.arange(REL)[None, :] - (REL - S) - p[:, None]
    rel = np.concatenate([np.maximum(diff, 0), np.maximum(-diff, 0)], 1).astype(np.float32)
    sel = np.zeros((P, FH), np.float32)
    for g in range(FH):
        sel[[g, 32 + g, 64 + g], g] = -1.0
    return const, rel, sel


def kernel(**inputs):
    import concourse.bacc as bacc
    from concourse.bass_utils import run_bass_kernel_spmd

    a = {k: np.asarray(v) for k, v in inputs.items()}

    def tile(w, cols):
        w = w[:, cols]
        return w.reshape(-1, P, w.shape[1]).transpose(1, 0, 2).reshape(P, -1)

    def tiles(w):
        return [tile(w, slice(m * P, (m + 1) * P)) for m in range(w.shape[1] // P)]

    def pairs(w, v):
        return [t for both in zip(tiles(w), tiles(v)) for t in both]

    w_in, w_mix, b_mix = a["w_in"][0], a["w_mix_2"][0], a["b_mix_2"][0]
    pair = [np.r_[t * DH:(t + 1) * DH, (t + 4) * DH:(t + 5) * DH] for t in range(AH // 2)]
    kv0 = AH * DH
    att = [tile(w_in, c) for c in (slice(kv0, kv0 + P), *pair, slice(kv0 + P, kv0 + 2 * P))]
    r0 = kv0 + 2 * P
    RW = RH * DH
    ret = [tile(w_in, slice(r0 + j * RW + t * P, r0 + j * RW + (t + 1) * P)) for t in range(RH // 2) for j in range(4)]
    order = np.concatenate([c for t in range(AH // 2) for c in (pair[t], np.arange(AH * DH + t * P, AH * DH + (t + 1) * P))])
    out1 = tiles(a["w_out"][0][order])
    o = np.cumsum([0, 512, 512, 1024, 1024, MH, MH, D, D, D, FH, D, D])
    m_at = [s for hd in range(MH) for s in (o[0] + hd * P, o[1] + hd * P, o[2] + hd * DV, o[2] + hd * DV + P,
                                            o[3] + hd * DV, o[3] + hd * DV + P)]
    f_at = [o[j] + t * P for t in range(FH // 2) for j in (6, 7, 8)]
    g_at = [o[j] + m * P for m in range(KC) for j in (10, 11)]
    gates = tiles(np.ascontiguousarray(w_mix[:, o[10]:o[12]]))
    wa, wb = tiles(a["w_branch_a_2"][0]), tiles(a["w_branch_b_2"][0])
    merge = [t for m in range(KC) for t in (gates[m], wa[m], gates[KC + m], wb[m])]
    f1, f2 = a["ffn1_w_in_2"][0], a["ffn2_w_in_2"][0]
    w_all = np.stack(att + ret + out1 + pairs(a["w_gate"][0], a["w_up"][0]) + pairs(f1[:, :FF], f1[:, FF:])
                     + [tile(w_mix, slice(c, c + P)) for c in m_at + f_at] + merge + tiles(a["w_out_2"][0])
                     + pairs(f2[:, :FF], f2[:, FF:]))
    wd_all = np.stack([tile(w[f * DC:(f + 1) * DC], slice(m * P, (m + 1) * P))
                       for w in (a["w_down"][0], a["ffn1_w_out_2"][0], a["ffn2_w_out_2"][0]) for m in range(KC) for f in range(2)])
    ada = a["w_ada_2"][0].reshape(KC, P, NMOD, D).transpose(2, 0, 1, 3).reshape(NMOD * KC, P, D)

    gate_rows = ((0, slice(o[5], o[6])), (32, slice(o[9], o[10])), (64, slice(o[4], o[5])))
    gw = np.zeros((D, 96), np.float32)
    gb = np.zeros((P, 1), np.float32)
    for at, c in gate_rows:
        gw[:, at:at + c.stop - c.start] = w_mix[:, c]
        gb[at:at + c.stop - c.start, 0] = b_mix[c]

    def columns(v):
        return v.reshape(-1, P).T

    def everywhere(v):
        return np.broadcast_to(v[None, :], (P, v.size))

    const, rel, sel = constants()
    conv = a["conv_w_2"][0].reshape(CONV, 2, MH, P).transpose(3, 2, 1, 0).reshape(P, -1)
    convb = a["conv_b_2"][0].reshape(2, MH, P).transpose(2, 1, 0).reshape(P, -1)
    at_cols = lambda starts: np.stack([b_mix[c:c + P] for c in starts], 1)
    cols = np.concatenate([
        columns(a["attn_norm_w"][0]), columns(a["ffn_norm_w"][0]), columns(a["ffn1_norm_g_2"][0]), columns(a["mix_norm_g_2"][0]),
        columns(a["ffn2_norm_g_2"][0]), np.tile(a["q_norm_w"][0], 2)[:, None], np.tile(a["k_norm_w"][0], 2)[:, None],
        columns(a["ret_norm_w"][0]), everywhere(a["attn_sink"][0]), everywhere(a["ret_log_decay_fwd"][0]),
        everywhere(a["ret_log_decay_bwd"][0]), columns(a["c_2"][0]), columns(a["b_ada_2"][0]), gb, at_cols(m_at), conv, convb,
        columns(a["mlstm_norm_g_2"][0].reshape(-1)), at_cols(f_at), columns(a["fox_q_norm_g_2"][0].reshape(-1)),
        columns(a["fox_k_norm_g_2"][0].reshape(-1)), at_cols(g_at), sel], 1)
    assert cols.shape == (P, NCOL)
    x = a["x"][0].reshape(S, KC, P).transpose(2, 1, 0).reshape(P, KC * S)

    arrays = {"x": x, "cols": cols, "const": const, "rel": rel, "w": w_all, "wd": wd_all, "ada": ada, "gates": tile(gw, slice(0, 96))}
    arrays = {k: np.ascontiguousarray(v) for k, v in arrays.items()}
    nc = bacc.Bacc("TRN2", target_bir_lowering=False, num_devices=1)
    args = [nc.dram_tensor(k + "_dram", v.shape, F32, kind="ExternalInput").ap() for k, v in arrays.items()]
    out = nc.dram_tensor("out_dram", (P, KC * S), F32, kind="ExternalOutput").ap()
    arrays = {k + "_dram": v for k, v in arrays.items()}
    build(nc, *args, out)
    r = run_bass_kernel_spmd(nc, [arrays], core_ids=[0])
    got = r.results[0]["out_dram"]
    return np.ascontiguousarray(got.reshape(P, KC, S).transpose(2, 1, 0).reshape(1, S, D))
```

```python
from contextlib import ExitStack

import numpy as np
import concourse.bass as bass
from concourse import mybir

F32 = mybir.dt.float32
F32R = mybir.dt.float32r
BF16 = mybir.dt.bfloat16
ALU = mybir.AluOpType
ACT = mybir.ActivationFunctionType
AX = mybir.AxisListType

P = 128
S = 512
D = 1024
KC = D // P
NB = S // P
DH = 64
FF = 2816
FC = FF // P
HALF = FC // 2
WC = KC * P
DC = HALF * P
EPS = 1e-6
NEG = -1e30
AH = 8
RH = 8
MH = 4
DQK = 128
DV = 256
FH = 16
CONV = 4
NMOD = 9
REL = S + (NB - 1) * P

N_ATT, N_RET, N_OUT, N_FF, N_DOWN = 6, 16, 8, 2 * FC, 16
N_MLSTM, N_FOX, N_MERGE = 6 * MH, 24, 32
SLAB = {}
TILE = {}
_n = _q = 0
for _name, _count in (("att", N_ATT), ("ret", N_RET), ("out", N_OUT), ("ff0", N_FF), ("down0", N_DOWN),
                      ("ff1", N_FF), ("down1", N_DOWN), ("mlstm", N_MLSTM), ("fox", N_FOX),
                      ("merge", N_MERGE), ("out2", N_OUT), ("ff2", N_FF), ("down2", N_DOWN)):
    SLAB[_name], TILE[_name] = _n, _q
    _n += _count
    _q += _count // 2 if _name.startswith("down") else _count

COL = {}
_c = 0
for _name, _count in (("attn_norm", KC), ("ffn_norm", KC), ("ffn1_norm", KC), ("mix_norm", KC), ("ffn2_norm", KC),
                      ("q_norm", 1), ("k_norm", 1), ("ret_norm", RH // 2), ("sink", AH), ("decay_f", RH),
                      ("decay_b", RH), ("b_ada", NMOD * KC), ("b_gates", 1), ("b_mlstm", 6 * MH),
                      ("conv_w", 2 * MH * CONV), ("conv_b", 2 * MH), ("mlstm_norm", 2 * MH), ("b_fox", 24),
                      ("fox_q", FH // 2), ("fox_k", FH // 2), ("b_merge", 16), ("sel", FH)):
    COL[_name] = _c
    _c += _count
NCOL = _c


PRIMED = ("act_lo", "ada_acc", "evac0", "evac1", "f_qk", "m_conv", "m_nMd", "m_out", "m_qk", "m_turned", "m_values",
          "m_weighted", "m_gated", "m_normed", "m_y", "mg", "mg_lo", "norm_sum", "probs_scaled", "rope_out", "row_split", "ssum",
          "w_lo", "x_lo0", "x_lo1", "y_lo", "yb_lo")


def build(nc, x_in, cols_in, const_in, rel_in, w_in, wd_in, ada_in, c_in, gates_in, out):
    ctx = ExitStack()
    with ctx:
        def sb(name, shape, dt=F32, scope=ctx):
            return scope.enter_context(nc.sbuf_tensor(name, shape, dt))

        sems = {}

        def sem(name):
            if name not in sems:
                sems[name] = ctx.enter_context(nc.semaphore(name))
            return sems[name]

        def primed(count):
            return count + 1

        h = sb("h", [P, KC * S])
        xh = sb("xh", [P, KC, S], F32R)
        xl = sb("xl", [P, KC, S], F32R)
        raw = sb("raw", [P, 2, DC])
        whi = sb("whi", [P, 2, DC], F32R)
        wlo = sb("wlo", [P, 2, DC], F32R)
        col = sb("col", [P, NCOL])
        modc = sb("modc", [P, NMOD * KC])
        scl = sb("scl", [P, 3 * KC])
        gat = sb("gat", [P, 3 * KC])
        ident = sb("ident", [P, P])
        ones = sb("ones", [P, P])
        blk = sb("blk", [P, P])
        identb = sb("identb", [P, P], BF16)
        ge = sb("ge", [P, P])
        geb = sb("geb", [P, P], BF16)
        leb = sb("leb", [P, P], BF16)
        ssum = sb("ssum", [P, S])
        sqn = sb("sqn", [P, 2, S])
        rstd = sb("rstd", [P, S])
        tmp = (sqn[:, 0, :], sqn[:, 1, :], ssum[:])
        gates_raw = sb("gates_raw", [P, KC * 96])
        stat = sb("stat", [P, 2, 8])
        lg = sb("lg", [P, 2 * RH])
        epsc = sb("epsc", [P, 1])

        ffs = ExitStack()
        acth = sb("acth", [P, FC, S], F32R, ffs)
        actl = sb("actl", [P, FC, S], F32R, ffs)
        gsil = sb("gsil", [P, 2, S], F32, ffs)
        aprod = sb("aprod", [P, 2, S], F32, ffs)
        adaw = sb("adaw", [P, 2, D], F32, ffs)
        crow = sb("crow", [P, D], F32, ffs)
        ffs.close()

        abs_ = ExitStack()
        yh = sb("yh", [P, KC, S], F32R, abs_)
        yl = sb("yl", [P, KC, S], F32R, abs_)
        decay = sb("decay", [P, 2 * REL], F32, abs_)
        rel = sb("rel", [P, 2 * S], F32, abs_)
        cos = sb("cos", [P, S], F32, abs_)
        sin = sb("sin", [P, S], F32, abs_)
        rot = sb("rot", [P, P], F32, abs_)
        leconst = sb("leconst", [P, P], F32, abs_)
        rraw = sb("rraw", [P, 2, S], F32, abs_)
        rsq = sb("rsq", [P, S], F32, abs_)
        rr = sb("rr", [P, S], F32, abs_)
        rt = sb("rt", [P, 2, S], F32, abs_)
        qall = sb("qall", [P, AH // 2, S], F32, abs_)
        wqs = sb("wqs", [P, 2, S], F32R, abs_)
        wks = sb("wks", [P, 2, S], F32R, abs_)
        wkl = sb("wkl", [P, S], F32R, abs_)
        rqf = sb("rqf", [P, S], F32, abs_)
        rkf = sb("rkf", [P, S], F32, abs_)
        rks = sb("rks", [P, 2, S], F32R, abs_)
        rqs = sb("rqs", [P, 2, S], F32R, abs_)
        rql = sb("rql", [P, S], F32R, abs_)
        rvtok = sb("rvtok", [P, NB, P], F32, abs_)
        vraw = sb("vraw", [P, S], F32, abs_)
        vtok = sb("vtok", [P, NB, P], F32, abs_)
        prob = sb("prob", [P, 2, S], F32, abs_)
        pT = sb("pT", [P, 2, S], F32, abs_)
        rsil = sb("rsil", [P, S], F32, abs_)
        ry = sb("ry", [P, S], F32, abs_)
        kf = ry
        abs_.close()

        mix = ExitStack()
        yah = sb("yah", [P, KC, S], F32R, mix)
        yal = sb("yal", [P, KC, S], F32R, mix)
        sel = sb("sel", [96, FH, P], BF16, mix)
        fsp = sb("fsp", [96, S], BF16, mix)
        mls = ExitStack()
        ghi = sb("ghi", [P, KC * 96], F32R, mls)
        glo = sb("glo", [P, KC * 96], F32R, mls)
        zg = sb("zg", [96, S], F32, mls)
        zt = sb("zt", [96, S], F32, mls)
        zi = sb("zi", [MH, S], F32, mls)
        zrow = sb("zrow", [48, S], F32, mls)
        lf = sb("lf", [48, S], F32, mls)
        cs = sb("cs", [48, S], F32, mls)
        gsp = sb("gsp", [48, 3, S], BF16, mls)
        msM = sb("msM", [96, S], BF16, mls)
        msm = sb("msm", [96, S], BF16, mls)
        arow = sb("arow", [MH, S], F32, mls)
        acol = sb("acol", [P, NB * MH], F32, mls)
        qz = sb("qz", [P, 2, S + CONV - 1], F32, mls)
        cv = sb("cv", [P, 2, S], F32, mls)
        qk = sb("qk", [P, 2, S], F32, mls)
        mvT = sb("mvT", [P, 2, S], F32, mls)
        mv = sb("mv", [P, NB, DV], F32, mls)
        nM = sb("nM", [P, S], F32, mls)
        nMd = sb("nMd", [P, S], F32, mls)
        emm = sb("emm", [P, S], F32, mls)
        Dm = sb("Dm", [P, 2, S], F32, mls)
        sT = sb("sT", [P, 2, S], F32, mls)
        hm = sb("hm", [P, 2, S], F32, mls)
        hsq = cv
        so = sb("so", [P, 2, S], F32, mls)
        mxr = sb("mxr", [P, 2, S], F32, mls)
        hn = mxr
        hrs = emm
        mls.close()
        fox = ExitStack()
        fraw = sb("fraw", [P, 2, S], F32, fox)
        fsq = sb("fsq", [P, 2, S], F32, fox)
        frs = sb("frs", [P, 2, S], F32, fox)
        fq = sb("fq", [P, 2, S], F32, fox)
        fk = sb("fk", [P, 2, S], F32, fox)
        fvraw = sb("fvraw", [P, S], F32, fox)
        fv = sb("fv", [P, NB, P], F32, fox)
        fprob = sb("fprob", [P, 2, S], F32, fox)
        fpT = sb("fpT", [P, 2, S], F32, fox)
        ybh = sb("ybh", [P, KC, S], F32R, fox)
        ybl = sb("ybl", [P, KC, S], F32R, fox)
        fox.close()
        mgh = sb("mgh", [P, KC, S], F32R, mix)
        mgl = sb("mgl", [P, KC, S], F32R, mix)
        sb("yb_kept", [P, 2, KC, S], F32R, mix)
        sg = sb("sg", [P, 2, S], F32, mix)
        br = sb("br", [P, 2, S], F32, mix)
        mg = sb("mg", [P, 1, S], F32, mix)
        mix.close()

        bank = [ctx.enter_context(nc.psum_tensor(f"bank{i}", [P, S], F32)) for i in range(8)]
        proj = bank[0:2]

        def c1(name, i=0, rows=slice(0, P)):
            if isinstance(i, int):
                return col[rows, COL[name] + i:COL[name] + i + 1]
            return col[rows, bass.ds(i + COL[name], 1)]

        def chunk(t, m):
            flat = t[:].rearrange("p c s -> p (c s)") if len(t.shape) == 3 else t
            return flat[:, m * S:m * S + S] if isinstance(m, int) else flat[:, bass.ds(m * S, S)]

        BESIDE = ((0, 0, 4), (0, 4, 8), (1, 0, 3), (1, 3, 6), (1, 6, 8), (2, 0, 2), (2, 2, 4), (2, 4, 8))
        RET_BESIDE = ((0, 0, 4), (0, 4, 8), (1, 0, 4), (1, 4, 8), (2, 0, 2), (2, 2, 4), (2, 4, 6), (2, 6, 8))
        QT = 1 + AH // 2

        def keys(b):
            return max(0, b - 1), min(NB - 1, b + 1)

        def halves(e):
            return slice(e * DH, e * DH + DH), slice(DH - e * DH, P - e * DH)

        def window(k):
            lo, hi = keys(k % NB)
            return (hi - lo + 1) * P

        block = ctx.enter_context(nc.Block())

        @block.sync
        def _(sp):
            for name in PRIMED:
                sp.sem_inc(sem(name), 1)
            for c in range(4):
                sp.dma_start(h[:, c * 2 * S:(c + 1) * 2 * S], x_in[:, c * 2 * S:(c + 1) * 2 * S]).then_inc(sem(f"x_in{c}"), 16)
            sp.dma_start(col[:], cols_in).then_inc(sem("cols_in"), 16)

            def load(n, s, src, width):
                if not isinstance(n, int) or n >= 2:
                    sp.wait_ge(sem("w_lo"), primed(n - 1))
                sp.dma_start(raw[:, s, 0:width], src).then_inc(sem(f"raw_in{s}"), 16)

            def downs_before(n0):
                return sum(N_DOWN for d in ("down0", "down1", "down2") if SLAB[d] < n0)

            def load_wide(i, per, n0, k):
                n = n0 - downs_before(n0) + k
                src = w_in[n] if i is None else w_in[bass.ds(i * per + n, 1)].rearrange("a p n -> (a p) n")
                load(n0 + k if i is None else i * per + (n0 + k), (n0 + k) % 2, src, WC)

            def wide_loop(n0, pairs):
                with sp.Fori(0, pairs) as i:
                    for k in range(2):
                        load_wide(i, 2, n0, k)

            def down_loop(run):
                n0 = SLAB[f"down{run}"]
                with sp.Fori(0, N_DOWN // 2) as i:
                    for k in range(2):
                        load(i * 2 + (n0 + k), k,
                             wd_in[bass.ds(i * 2 + (run * N_DOWN + k), 1)].rearrange("a p n -> (a p) n"), DC)

            for k in range(2):
                load_wide(None, 2, 0, k)
            sp.dma_start(gates_raw[:], gates_in).then_inc(sem("gates_in"), 16)
            wide_loop(2, (SLAB["ff0"] - 2) // 2)

            for s in range(4):
                if s == 2:
                    sp.wait_ge(sem("mm_done"), SLAB["ff0"])
                    sp.dma_start(crow[:], c_in).then_inc(sem("c_in"), 16)
                load_wide(None, 4, SLAB["ff0"], s)
            with sp.Fori(0, NMOD) as i:
                for s in range(4):
                    load_wide(i, 4, SLAB["ff0"] + 4, s)
                    for k in range(2 * s, 2 * s + 2):
                        sp.wait_ge(sem("ada_acc"), primed(i * KC + max(k - 1, 0)))
                        sp.dma_start(adaw[:, k % 2, :], ada_in[bass.ds(i * KC + k, 1)].rearrange("a p n -> (a p) n")
                                     ).then_inc(sem(f"ada_in{k % 2}"), 16)
            wide_loop(SLAB["ff0"] + 4 * (NMOD + 1), (N_FF - 4 * (NMOD + 1)) // 2)
            down_loop(0)
            wide_loop(SLAB["ff1"], N_FF // 2)
            down_loop(1)
            wide_loop(SLAB["mlstm"], (SLAB["down2"] - SLAB["mlstm"]) // 2)
            down_loop(2)
            base = TILE["down2"] // 2
            with sp.Fori(0, KC // 2) as i:
                for s in range(2):
                    sp.wait_ge(sem(f"evac{s}"), primed(i + (base + 1)))
                    sp.dma_start(out[:, bass.ds(i * (2 * S) + s * S, S)], chunk(h, i * 2 + s)).then_inc(sem("stored"), 16)
            sp.wait_ge(sem("stored"), 16 * KC)

        @block.gpsimd
        def _(pool):
            def low_loop(n0, count, width):
                with pool.Fori(0, count // 2) as i:
                    for s in range(2):
                        pool.wait_ge(sem("w_hi"), i * 2 + (n0 + s + 1))
                        nc.gpsimd.tensor_tensor(wlo[:, s, 0:width], raw[:, s, 0:width], whi[:, s, 0:width].bitcast(F32),
                                                ALU.subtract).then_inc(sem("w_lo"), 1)

            def norm_lows(r):
                for c in range(1, KC, 2):
                    pool.wait_ge(sem("x_hi"), KC * r + c + 1)
                    nc.gpsimd.tensor_tensor(xl[:, c, :], tmp[c % 3], xh[:, c, :].bitcast(F32),
                                            ALU.subtract).then_inc(sem("x_lo1"), 1)

            low_loop(0, 2, WC)
            norm_lows(0)
            low_loop(2, SLAB["ff0"], WC)
            norm_lows(1)
            low_loop(SLAB["ff0"] + 2, N_FF - 2, WC)
            low_loop(SLAB["down0"], N_DOWN, DC)
            low_loop(SLAB["ff1"], 2, WC)
            norm_lows(2)
            low_loop(SLAB["ff1"] + 2, N_FF - 2, WC)
            low_loop(SLAB["down1"], N_DOWN, DC)
            low_loop(SLAB["mlstm"], 2, WC)
            norm_lows(3)
            low_loop(SLAB["mlstm"] + 2, SLAB["ff2"] - SLAB["mlstm"], WC)
            norm_lows(4)
            low_loop(SLAB["ff2"] + 2, N_FF - 2, WC)
            low_loop(SLAB["down2"], N_DOWN, DC)

        @block.tensor
        def _(pe):
            def slab(n, s, b, uses, ih, il, chunks, first=True, last=True, ready=None, part=None):
                lo, hi = part or (0, len(chunks))
                if lo == 0:
                    pe.wait_ge(sem("w_lo"), primed(n + 1))
                if lo == 0 and first:
                    pe.wait_ge(sem(f"evac{b}"), primed(uses))
                for j in range(lo, hi):
                    k = chunks[j]
                    if ready and ready[0] == "x_lo":
                        pe.wait_ge(sem(f"x_lo{k % 2}"), primed(ready[1] * (KC // 2) + k // 2 + 1))
                    elif ready:
                        pe.wait_ge(sem(ready[0]), primed(ready[1] + k + 1))
                    W = slice(j * P, j * P + P)
                    for a, (w, v) in enumerate(((whi, ih), (whi, il), (wlo, ih))):
                        mm = nc.tensor.matmul(proj[b][:], w[:, s, W], v[:, k, :], start=first and j == 0 and a == 0,
                                              stop=last and j == len(chunks) - 1 and a == 2, skip_group_check=True)
                if hi == len(chunks):
                    mm.then_inc(sem("mm_done"), 1)

            def wide(name, i, per, s, ready=None, ih=xh, il=xl, part=None):
                slab(i * per + (SLAB[name] + s), s % 2, s % 2, i * (per // 2) + (TILE[name] + s) // 2, ih, il,
                     range(KC), ready=ready, part=part)

            def norm_sum(r):
                pe.wait_ge(sem("ssum"), primed(KC * (r + 1)))
                nc.tensor.matmul(bank[4][:], ones[:], ssum[:], start=True, stop=True).then_inc(sem("norm_sum"), 1)

            def down(run):
                with pe.Fori(0, KC // 2) as i:
                    for s in range(2):
                        for f in range(2):
                            n = i * 4 + (SLAB[f"down{run}"] + 2 * s + f)
                            slab(n, f, s, i + (TILE[f"down{run}"] + s) // 2, acth, actl,
                                 range(f * HALF, f * HALF + HALF), first=f == 0, last=f == 1,
                                 ready=("act_lo", run * FC))

            def transpose_values(src, dst_bank, done):
                for b in range(NB):
                    tr = nc.tensor.transpose(dst_bank[:, b * P:(b + 1) * P], src[:, b * P:(b + 1) * P], ident[:])
                tr.then_inc(sem(done), 1)

            pe.wait_ge(sem("ones"), 1)
            norm_sum(0)

            def sums_and_turn(p):
                pe.wait_ge(sem(f"evac{p % 2}"), primed(p // 2 + 1))
                pe.wait_ge(sem("rope_out"), primed(p))
                nc.tensor.matmul(bank[5][:], blk[:], rsq[:], start=True, stop=True).then_inc(sem("rope_ss"), 1)
                nc.tensor.matmul(bank[6][:], rot[:], rraw[:, p % 2, :], start=True, stop=True).then_inc(sem("rope_rot"), 1)

            def win_scores(t, k):
                e, b = k // NB, k % NB
                lo, hi = keys(b)
                H = slice(e * DH, e * DH + DH)
                if k == 0:
                    pe.wait_ge(sem("q_low"), t * 2 + 2)
                if k >= 2:
                    pe.wait_ge(sem("probs"), t * 8 + (k - 1))
                elif not isinstance(t, int) or t > 0:
                    pe.wait_ge(sem("ret_decayed"), t * 8 + (k - 1))
                dst = bank[2 + k % 2]
                W = window(k)
                B, C = slice(b * P, (b + 1) * P), slice(lo * P, (hi + 1) * P)
                nc.tensor.matmul(dst[:, 0:W], wqs[:, e, B], wks[:, e, C], start=True, stop=False, skip_group_check=True)
                mm = nc.tensor.matmul(dst[:, 0:W], wqs[H, e, B], wkl[H, C], start=False, stop=False, skip_group_check=True)
                if b > 0:
                    mm = nc.tensor.matmul(dst[:, 0:P], identb[:], geb[:], start=False, stop=b == NB - 1, skip_group_check=True)
                if b < NB - 1:
                    mm = nc.tensor.matmul(dst[:, W - P:W], identb[:], leb[:], start=False, stop=True, skip_group_check=True)
                mm.then_inc(sem("scores"), 1)

            def win_turn(t, k):
                pe.wait_ge(sem("probs_scaled"), primed(t * 8 + (k + 1)))
                if k >= 2:
                    pe.wait_ge(sem("pT_copied"), t * 8 + (k - 1))
                else:
                    pe.wait_ge(sem("rope_out"), primed(t * 2 + QT))
                for j in range(window(k) // P):
                    tr = nc.tensor.transpose(bank[5 + k % 2][:, j * P:(j + 1) * P], prob[:, k % 2, j * P:(j + 1) * P], ident[:])
                tr.then_inc(sem("pT_ready"), 1)

            def win_values(t, k):
                e, b = k // NB, k % NB
                lo, hi = keys(b)
                H = slice(e * DH, e * DH + DH)
                pe.wait_ge(sem("pT_copied"), t * 8 + (k + 1))
                if k == 0:
                    pe.wait_ge(sem("y_lo"), primed(t * 2))
                    pe.wait_ge(sem("vtok"), t + 1)
                for j in range(hi - lo + 1):
                    mm = nc.tensor.matmul(bank[7][H, b * P:(b + 1) * P], vtok[:, lo + j, H], pT[:, k % 2, j * P:(j + 1) * P],
                                          start=j == 0, stop=j == hi - lo, skip_group_check=True)
                mm.then_inc(sem("values"), 1)

            def ret_turn(t, j):
                pe.wait_ge(sem(f"evac{j}"), primed(t * 2 + (TILE["ret"] // 2 + 1)))
                if j == 0:
                    pe.wait_ge(sem("rope_out"), primed(t * 2 + QT))
                else:
                    pe.wait_ge(sem("rope_part"), t * 4 + (2 * QT + 1))
                nc.tensor.matmul(bank[4][:], rot[:], rraw[:, j, :], start=True, stop=True).then_inc(sem("rope_rot"), 1)

            def ret_scores(t, k):
                e, b = k // NB, k % NB
                H = slice(e * DH, e * DH + DH)
                if k >= 2:
                    pe.wait_ge(sem("ret_decayed"), t * 8 + (k - 1))
                B = slice(b * P, (b + 1) * P)
                nc.tensor.matmul(bank[2 + k % 2][:], rks[:, e, B], rqs[:, e, :], start=True, stop=False, skip_group_check=True)
                nc.tensor.matmul(bank[2 + k % 2][:], rks[H, e, B], rql[H, :], start=False, stop=True,
                                 skip_group_check=True).then_inc(sem("ret_scores"), 1)

            def ret_values(t, k):
                e, b = k // NB, k % NB
                H = slice(e * DH, e * DH + DH)
                pe.wait_ge(sem("ret_decayed"), t * 8 + (k + 1))
                if k == 0:
                    pe.wait_ge(sem("vtok"), t + 2)
                nc.tensor.matmul(bank[4][H, :], rvtok[:, b, H], prob[:, k % 2, :], start=b == 0, stop=b == NB - 1,
                                 skip_group_check=True).then_inc(sem("ret_values"), 1)

            def mixing_step(t, more=True):
                for k in range(8):
                    win_turn(t, k)
                    if k + 2 < 8:
                        win_scores(t, k + 2)
                    if k in (3, 6):
                        ret_turn(t, k // 6)
                    j, lo, hi = RET_BESIDE[k]
                    wide("ret", t, 4, j, part=(lo, hi))
                    win_values(t, k)
                wide("ret", t, 4, 3, part=(0, 6))
                pe.wait_ge(sem("evac0"), primed(t * 2 + (TILE["ret"] // 2 + 2)))
                pe.wait_ge(sem("rope_out"), primed(t * 2 + (QT + 2)))
                transpose_values(vraw, bank[4], "vT")
                wide("ret", t, 4, 3, part=(6, KC))
                pe.wait_ge(sem("ret_low"), t * 4 + 4)
                ret_scores(t, 0)
                ret_scores(t, 1)
                for k in range(8):
                    ret_values(t, k)
                    if k + 2 < 8:
                        ret_scores(t, k + 2)
                    elif more:
                        win_scores(t + 1, k - 6)
                pe.wait_ge(sem("ret_sq"), t + 1)
                nc.tensor.matmul(bank[7][:], blk[:], rsq[:], start=True, stop=True).then_inc(sem("ret_ss"), 1)

            for p in range(N_ATT):
                wide("att", 0, 2, p, ready=("x_lo", 0) if p == 0 else None, part=(0, KC // 2))
                if p == 1:
                    pe.wait_ge(sem("const_ready"), 1)
                if p > 0:
                    sums_and_turn(p - 1)
                if p == N_ATT - 1:
                    win_scores(0, 0)
                    win_scores(0, 1)
                wide("att", 0, 2, p, ready=("x_lo", 0) if p == 0 else None, part=(KC // 2, KC))
            pe.wait_ge(sem("evac1"), primed(N_ATT // 2))
            transpose_values(vraw, bank[4], "vT")
            with pe.Fori(0, AH // 2 - 1) as t:
                mixing_step(t)
            mixing_step(AH // 2 - 1, more=False)

            for s, lo, hi in ((0, 0, KC - 1), (1, 0, KC // 2), (0, KC - 1, KC), (1, KC // 2, KC)):
                wide("out", 0, 2, s, ready=("y_lo", 0), ih=yh, il=yl, part=(lo, hi))
            with pe.Fori(0, N_OUT // 2 - 1) as i:
                for s in range(2):
                    wide("out", i, 2, s + 2, ih=yh, il=yl)
            norm_sum(1)

            def ff_step(run, i):
                for s in range(4):
                    n = SLAB[f"ff{run}"] + s
                    slab(i * 4 + n, s % 2, s % 2, i * 2 + (TILE[f"ff{run}"] + s) // 2, xh, xl, range(KC),
                         ready=("x_lo", NORM[run]) if s == 0 else None)

            NORM = (1, 2, 4)
            with pe.Fori(0, FC // 2) as i:
                ff_step(0, i)
            down(0)

            norm_sum(2)
            with pe.Fori(0, FC // 2) as i:
                ff_step(1, i)
            down(1)
            norm_sum(3)

            pe.wait_ge(sem("gates_split"), 2)
            for k in range(KC):
                pe.wait_ge(sem(f"x_lo{k % 2}"), primed(3 * (KC // 2) + k // 2 + 1))
                for a, (w, v) in enumerate(((ghi, xh), (ghi, xl), (glo, xh))):
                    mm = nc.tensor.matmul(bank[4][0:96, :], w[:, k * 96:(k + 1) * 96], v[:, k, :], start=k == 0 and a == 0,
                                          stop=k == KC - 1 and a == 2)
            mm.then_inc(sem("gates"), 1)

            def mlstm_scores(hd, b):
                pe.wait_ge(sem("m_weighted"), primed(hd * NB + max(b - 1, 0)))
                nc.tensor.matmul(bank[2 + b % 2][:, 0:S - b * P], qk[:, 1, b * P:(b + 1) * P], qk[:, 0, b * P:S],
                                 start=True, stop=True).then_inc(sem("m_scores"), 1)

            def mlstm_values(hd, b):
                pe.wait_ge(sem("m_weighted"), primed(hd * NB + (b + 1)))
                if b == 0:
                    pe.wait_ge(sem("m_emm"), hd + 1)
                    pe.wait_ge(sem("m_out"), primed(hd * 2))
                for j in range(3):
                    w = mv[:, b, j * P:(j + 1) * P] if j < 2 else ones[:]
                    mm = nc.tensor.matmul(bank[5 + j][:, b * P:S], w, sT[:, b % 2, 0:S - b * P], start=b == 0, stop=b == NB - 1,
                                          skip_group_check=True)
                mm.then_inc(sem("m_values"), 1)

            def mlstm_head(hd):
                head = sel[:, bass.ds(hd, 1), :].rearrange("p a n -> p (a n)")
                for s in range(2, 5):
                    wide("mlstm", hd, 6, s)
                for j in range(2):
                    pe.wait_ge(sem(f"evac{j}"), primed(hd * 3 + (TILE["mlstm"] // 2 + 2)))
                    transpose_values(mvT[:, j, :], bank[2 + j], "m_turned")
                wide("mlstm", hd, 6, 5, part=(0, KC // 2))
                pe.wait_ge(sem("sel_ready"), FH)
                pe.wait_ge(sem("m_rows"), 6)
                nc.tensor.matmul(bank[4][:], head, msM[:], start=True, stop=True).then_inc(sem("m_bcast"), 1)
                nc.tensor.matmul(bank[5][:], head, msm[:], start=True, stop=True).then_inc(sem("m_bcast"), 1)
                for b in range(NB):
                    tr = nc.tensor.transpose(bank[6][:, b * MH:(b + 1) * MH], arow[:, b * P:(b + 1) * P], ident[0:MH, 0:MH])
                tr.then_inc(sem("m_acol"), 1)
                wide("mlstm", hd, 6, 5, part=(KC // 2, KC))
                pe.wait_ge(sem("m_qk"), primed(hd * 2 + 2))
                pe.wait_ge(sem("m_v"), hd * 2 + 2)
                mlstm_scores(hd, 0)
                mlstm_scores(hd, 1)
                pe.wait_ge(sem("m_acols"), hd + 1)
                for b in range(NB):
                    mlstm_values(hd, b)
                    if b + 2 < NB:
                        mlstm_scores(hd, b + 2)
                wide("mlstm", hd, 6, 6)
                wide("mlstm", hd, 6, 7, part=(0, 6))
                pe.wait_ge(sem("m_sq"), hd + 1)
                nc.tensor.matmul(bank[4][:], ones[:], hsq[:, 0, :], start=True, stop=False)
                nc.tensor.matmul(bank[4][:], ones[:], hsq[:, 1, :], start=False, stop=True).then_inc(sem("m_ss"), 1)
                wide("mlstm", hd, 6, 7, part=(6, KC))

            for s in range(2):
                wide("mlstm", 0, 6, s)
            with pe.Fori(0, MH) as hd:
                mlstm_head(hd)

            UA = AH * NB

            def fox_scores(t, tt, k):
                e, b = k // NB, k % NB
                H = slice(e * DH, e * DH + DH)
                W = (b + 1) * P
                pe.wait_ge(sem("probs"), t * 8 + (UA + k - 1))
                if k == 0:
                    pe.wait_ge(sem("f_qk"), primed(t * 2 + 2))
                dst = bank[2 + k % 2]
                nc.tensor.matmul(dst[:, 0:W], fq[H, tt, b * P:W], fk[H, tt, 0:W], start=True, stop=False, skip_group_check=True)
                nc.tensor.matmul(dst[:, 0:W], sel[:, bass.ds(t * 2 + e, 1), :].rearrange("p a n -> p (a n)"), fsp[:, 0:W],
                                 start=False, stop=False, skip_group_check=True)
                nc.tensor.matmul(dst[:, W - P:W], identb[:], leb[:], start=False, stop=True,
                                 skip_group_check=True).then_inc(sem("scores"), 1)

            def fox_turn(t, k):
                b = k % NB
                pe.wait_ge(sem("probs_scaled"), primed(t * 8 + (UA + k + 1)))
                pe.wait_ge(sem("pT_copied"), t * 8 + (UA + k - 1))
                for j in range(b + 1):
                    tr = nc.tensor.transpose(bank[5 + k % 2][:, j * P:(j + 1) * P], fprob[:, k % 2, j * P:(j + 1) * P], ident[:])
                tr.then_inc(sem("pT_ready"), 1)

            def fox_values(t, k):
                e, b = k // NB, k % NB
                H = slice(e * DH, e * DH + DH)
                pe.wait_ge(sem("pT_copied"), t * 8 + (UA + k + 1))
                if k == 0:
                    pe.wait_ge(sem("f_v"), t + 1)
                    pe.wait_ge(sem("yb_lo"), primed(t))
                for j in range(b + 1):
                    mm = nc.tensor.matmul(bank[7][H, b * P:(b + 1) * P], fv[:, j, H], fpT[:, k % 2, j * P:(j + 1) * P],
                                          start=j == 0, stop=j == b, skip_group_check=True)
                mm.then_inc(sem("values"), 1)

            def fox_sums(p, i, s, j):
                pe.wait_ge(sem(f"evac{s % 2}"), primed(i * 3 + (TILE["fox"] + s) // 2 + 1))
                if j == 1:
                    pe.wait_ge(sem("f_ln"), p * 2 + 1)
                nc.tensor.matmul(bank[4][:], blk[:], fsq[:, j, :], start=True, stop=True).then_inc(sem("f_ss"), 1)

            def fox_turn_values(t, i, s):
                pe.wait_ge(sem(f"evac{s % 2}"), primed(i * 3 + (TILE["fox"] + s) // 2 + 1))
                transpose_values(fvraw, bank[4], "f_vT")

            def fox_pair(i, tt, more=True):
                t = i * 2 + tt
                for k in range(8):
                    fox_turn(t, k)
                    if k + 2 < 8:
                        fox_scores(t, tt, k + 2)
                    if k == 0:
                        fox_turn_values(t, i, 3 * tt + 2)
                    j, lo, hi = BESIDE[k]
                    if not more:
                        ih, il = (yah, yal) if j == 1 else (xh, xl)
                        wide("merge", 0, 4, j, ih=ih, il=il, ready=("m_y", 0) if j == 1 else None, part=(lo, hi))
                    if more:
                        s = 3 * tt + 3
                        if k == 3:
                            fox_sums(t + 1, i, s, 0)
                        wide("fox", i, 6, s + j, part=(lo, hi))
                        if k == 5:
                            fox_sums(t + 1, i, s + 1, 1)
                    fox_values(t, k)
                    if more and k >= 6:
                        fox_scores(t + 1, 1 - tt, k - 6)

            pe.wait_ge(sem("m_ln"), MH)
            fox_sums(0, 0, 0, 0)
            wide("fox", 0, 6, 2)
            fox_sums(0, 0, 1, 1)
            pe.wait_ge(sem("f_rows"), 3)
            fox_scores(0, 0, 0)
            fox_scores(0, 0, 1)
            with pe.Fori(0, FH // 4 - 1) as i:
                for tt in range(2):
                    fox_pair(i, tt)
            fox_pair(FH // 4 - 1, 0)
            fox_pair(FH // 4 - 1, 1, more=False)

            wide("merge", 0, 4, 3, ih=ybh, il=ybl, ready=("yb_lo", 0))
            with pe.Fori(0, KC - 1) as m:
                wide("merge", m, 4, 4)
                wide("merge", m, 4, 5, ih=yah, il=yal)
                wide("merge", m, 4, 6)
                wide("merge", m, 4, 7, ih=ybh, il=ybl)
            with pe.Fori(0, N_OUT // 2) as i:
                for s in range(2):
                    wide("out2", i, 2, s, ih=mgh, il=mgl, ready=("mg_lo", 0))
            norm_sum(4)
            with pe.Fori(0, FC // 2) as i:
                ff_step(2, i)
            down(2)

        @block.scalar
        def _(act):
            def split(i, per, n0, k, width):
                s = (n0 + k) % 2
                act.wait_ge(sem(f"raw_in{s}"), i * (8 * per) + ((n0 + k) // 2 * 16 + 16))
                if not isinstance(i, int) or i * per + n0 + k >= 2:
                    act.wait_ge(sem("mm_done"), i * per + (n0 + k - 1))
                nc.scalar.activation(whi[:, s, 0:width], raw[:, s, 0:width], ACT.Copy).then_inc(sem("w_hi"), 1)

            def width(name):
                return DC if name.startswith("down") else WC

            def steps(name, per, count, body, after=None, i0=0):
                def ahead_in(i, last):
                    def ahead(k):
                        if last and k >= per - 2:
                            if after:
                                split(0, 2, SLAB[after], k - (per - 2), width(after))
                        else:
                            split(i, per, SLAB[name] + i0 * per + 2, k, width(name))
                    return ahead

                with act.Fori(0, count - 1) as i:
                    body(i, ahead_in(i, False))
                body(count - 1, ahead_in(count - 1, True))

            def matmuls(n):
                act.wait_ge(sem("mm_done"), n)

            def square_chunk(r, m, k):
                if r > 0 or m > 0:
                    act.wait_ge(sem("ssum"), primed(m + (KC * r - 1)))
                nc.scalar.activation(sqn[:, k, :], chunk(h, m), ACT.Square).then_inc(sem("sq"), 1)

            def inverse_root(name, i, src, dst, width):
                nc.scalar.activation(dst, src, ACT.Ln, scale=1.0 / width, bias=epsc[:]).then_inc(sem(name + "_ln"), 1)
                act.wait_ge(sem(name + "_ln"), i + 1)
                nc.scalar.activation(dst, dst, ACT.Exp, scale=-0.5).then_inc(sem(name + "_rstd"), 1)

            def norm(r, shift=None):
                if r > 0:
                    act.preload_act_table_set("natural_log_exp_and_others")
                act.wait_ge(sem("norm_sum"), primed(r + 1))
                inverse_root("norm", r, bank[4][:], rstd[:], D)
                for c in range(KC):
                    act.wait_ge(sem("x_scaled"), KC * r + c + 1)
                    if shift is None:
                        nc.scalar.activation(xh[:, c, :], tmp[c % 3], ACT.Copy).then_inc(sem("x_hi"), 1)
                        continue
                    sh = modc[:, shift * KC + c:shift * KC + c + 1]
                    if c % 2:
                        nc.scalar.activation(tmp[c % 3], tmp[c % 3], ACT.Identity, bias=sh).then_inc(sem("x_shifted"), 1)
                        act.wait_ge(sem("x_shifted"), (r - 2) * (KC // 2) + c // 2 + 1)
                        nc.scalar.activation(xh[:, c, :], tmp[c % 3], ACT.Copy).then_inc(sem("x_hi"), 1)
                    else:
                        nc.scalar.activation(xh[:, c, :], tmp[c % 3], ACT.Identity, bias=sh).then_inc(sem("x_hi"), 1)

            act.preload_act_table_set("natural_log_exp_and_others")
            act.wait_ge(sem("ones"), 1)
            for c in range(KC):
                if c % 2 == 0:
                    act.wait_ge(sem(f"x_in{c // 2}"), 16)
                square_chunk(0, c, c % 2)
            for dst, at, n in ((ident, 0, P), (blk, P, P), (rot, 2 * P, P), (ge, 3 * P, P), (leconst, 4 * P, P),
                               (cos, 5 * P, S), (sin, 5 * P + S, S)):
                act.dma_start(dst[:], const_in[:, at:at + n]).then_inc(sem("const_in"), 16)
            act.dma_start(rel[:], rel_in).then_inc(sem("rel_in"), 16)
            for k in range(2):
                split(0, 2, 0, k, WC)
            norm(0)

            def rope_tile(p):
                matmuls(p + 1)
                act.wait_ge(sem("rope_out"), primed(max(p - 1, 0)))
                nc.scalar.activation(rsq[:], proj[p % 2][:], ACT.Square)
                nc.scalar.activation(rraw[:, p % 2, :], proj[p % 2][:], ACT.Identity,
                                     scale=c1("q_norm" if p else "k_norm")).then_inc(sem(f"evac{p % 2}"), 1)
                split(0, 2, 0, p + 2, WC)

            def rope_roots(p):
                act.wait_ge(sem("rope_ss"), p + 1)
                if p > 0:
                    act.wait_ge(sem("rope_out"), primed(p))
                inverse_root("rope", p, bank[5][:], rr[:], DH)

            def win_exps(t, k):
                e = k // NB
                act.wait_ge(sem("negmax"), t * 8 + (k + 1))
                if k >= 2:
                    act.wait_ge(sem("pT_ready"), t * 8 + (k - 1))
                st = stat[:, k % 2, :]
                nc.scalar.activation(prob[:, k % 2, 0:window(k)], bank[2 + k % 2][:, 0:window(k)], ACT.Exp, bias=st[:, 1:2],
                                     accum_out=st[:, 2:3]).then_inc(sem("probs"), 1)
                nc.scalar.activation(st[:, 3:4], c1("sink", t + e * (AH // 2)), ACT.Exp,
                                     bias=st[:, 1:2]).then_inc(sem("sink_exp"), 1)

            def win_copy(t, k):
                act.wait_ge(sem("pT_ready"), t * 8 + (k + 1))
                if k >= 2:
                    act.wait_ge(sem("values"), t * 8 + (k - 1))
                nc.scalar.activation(pT[:, k % 2, 0:window(k)], bank[5 + k % 2][:, 0:window(k)],
                                     ACT.Copy).then_inc(sem("pT_copied"), 1)

            def ret_decays(t, e):
                act.wait_ge(sem("decay_log"), t * 4 + 4)
                at, lo, hi = e * REL, S - P, S
                fwd = lg[:, bass.ds(t * 2 + e, 1)]
                bwd = lg[:, bass.ds(t * 2 + (RH + e), 1)]
                nc.scalar.activation(decay[:, at:at + lo], rel[:, S:S + lo], ACT.Exp, scale=bwd)
                nc.scalar.activation(decay[:, at + hi:at + REL], rel[:, P:S], ACT.Exp, scale=fwd)
                nc.scalar.activation(decay[:, at + lo:at + hi], decay[:, at + lo:at + hi], ACT.Exp).then_inc(sem("decay"), 1)

            def ret_tile(t, j):
                matmuls(t * 4 + (SLAB["ret"] + j + 1))
                act.wait_ge(sem("rope_out"), primed(t * 2 + QT))
                nc.scalar.activation(rraw[:, j, :], proj[j][:], ACT.Copy,
                                     scale=DH ** -0.5 if j else 1.0).then_inc(sem(f"evac{j}"), 1)
                split(t, 4, SLAB["ret"], j + 2, WC)

            def ret_highs(t, j):
                act.wait_ge(sem("rope_out"), primed(t * 2 + (QT + j + 1)))
                for e in range(2):
                    H, other = halves(e)
                    if j == 0:
                        nc.scalar.activation(rqs[other, e, :], rqf[H, :], ACT.Copy)
                        nc.scalar.activation(rqs[H, e, :], rqf[H, :], ACT.Copy).then_inc(sem("ret_high"), 1)
                    else:
                        nc.scalar.activation(rks[H, e, :], rkf[H, :], ACT.Copy).then_inc(sem("ret_high"), 1)

            def mixing_step(t, more=True):
                n = SLAB["ret"]
                for k in range(8):
                    win_copy(t, k)
                    if k + 2 < 8:
                        win_exps(t, k + 2)
                    if k == 1:
                        ret_tile(t, 0)
                    if k == 3:
                        ret_tile(t, 1)
                    if k in (4, 5):
                        ret_decays(t, k - 4)
                ret_highs(t, 0)
                act.wait_ge(sem("values"), t * 8 + 8)
                nc.scalar.activation(chunk(yh, t * 2), bank[7][:], ACT.Copy).then_inc(sem("y_hi"), 1)
                matmuls(t * 4 + (n + 3))
                nc.scalar.activation(vraw[:], proj[0][:], ACT.Copy).then_inc(sem("evac0"), 1)
                ret_highs(t, 1)
                split(t, 4, n, 4, WC)
                act.wait_ge(sem("vT"), t + 2)
                nc.scalar.activation(rvtok[:].rearrange("p b n -> p (b n)"), bank[4][:], ACT.Copy).then_inc(sem("vtok"), 1)
                act.preload_act_table(ACT.Silu)
                matmuls(t * 4 + (n + 4))
                nc.scalar.activation(rsil[:], proj[1][:], ACT.Silu).then_inc(sem("evac1"), 1)
                split(t, 4, n, 5, WC)
                act.preload_act_table_set("natural_log_exp_and_others")
                if more:
                    win_exps(t + 1, 0)
                act.wait_ge(sem("ret_values"), t * 8 + 8)
                nc.scalar.activation(rsq[:], bank[4][:], ACT.Square).then_inc(sem("ret_sq"), 1)
                if more:
                    win_exps(t + 1, 1)
                act.wait_ge(sem("ret_ss"), t + 1)
                inverse_root("ret", t, bank[7][:], rr[:], DH)

            act.wait_ge(sem("q_scale"), 1)
            for p in range(QT):
                rope_tile(p)
                if p == QT - 1:
                    win_exps(0, 0)
                rope_roots(p)
            matmuls(N_ATT)
            nc.scalar.activation(vraw[:], proj[1][:], ACT.Copy).then_inc(sem("evac1"), 1)
            split(0, 2, 0, N_ATT + 1, WC)
            win_exps(0, 1)
            act.wait_ge(sem("vT"), 1)
            nc.scalar.activation(vtok[:].rearrange("p b n -> p (b n)"), bank[4][:], ACT.Copy).then_inc(sem("vtok"), 1)
            act.wait_ge(sem("rel_in"), 16)
            with act.Fori(0, AH // 2 - 1) as t:
                mixing_step(t)
            mixing_step(AH // 2 - 1, more=False)

            def square_added(r, name, i, s):
                act.wait_ge(sem(f"evac{s}"), primed(i + ((TILE[name] + s) // 2 + 1)))
                square_chunk(r, i * 2 + s, s)

            def out_step(r, name):
                def step(i, ahead):
                    for s in range(2):
                        ahead(s)
                        square_added(r, name, i, s)
                return step

            def down_step(r, name):
                def step(i, ahead):
                    for s in range(2):
                        ahead(2 * s)
                        ahead(2 * s + 1)
                        if r is not None:
                            square_added(r, name, i, s)
                return step

            def ff_step(run, i0):
                def step(i, ahead):
                    for jj in range(2):
                        matmuls(i * 4 + (SLAB[f"ff{run}"] + 4 * i0 + 2 * jj + 1))
                        nc.scalar.activation(gsil[:, jj, :], proj[0][:], ACT.Silu).then_inc(sem("evac0"), 1)
                        ahead(2 * jj)
                        ahead(2 * jj + 1)
                        j = i * 2 + (2 * i0 + jj)
                        act.wait_ge(sem("evac1"), primed(i * 2 + (TILE[f"ff{run}"] // 2 + 2 * i0 + jj + 1)))
                        nc.scalar.activation(chunk(acth, j), aprod[:, jj, :], ACT.Copy).then_inc(sem("act_hi"), 1)
                return step

            steps("out", 2, N_OUT // 2, out_step(1, "out"), "ff0")
            norm(1)
            act.preload_act_table(ACT.Silu)
            act.wait_ge(sem("c_in"), 16)
            nc.scalar.activation(crow[:], crow[:], ACT.Silu).then_inc(sem("c_silu"), 1)
            steps("ff0", 4, FC // 2, ff_step(0, 0), "down0")
            steps("down0", 4, N_DOWN // 4, down_step(2, "down0"), "ff1")

            norm(2, shift=0)
            act.preload_act_table(ACT.Silu)
            steps("ff1", 4, FC // 2, ff_step(1, 0), "down1")
            steps("down1", 4, N_DOWN // 4, down_step(3, "down1"), "mlstm")
            norm(3, shift=3)

            act.wait_ge(sem("gates"), 1)
            nc.scalar.activation(zg[:], bank[4][0:96, :], ACT.Identity, bias=c1("b_gates", rows=slice(0, 96))).then_inc(sem("gates_out"), 1)
            nc.scalar.activation(zi[:], bank[4][64:64 + MH, :], ACT.Identity,
                                 bias=c1("b_gates", rows=slice(64, 64 + MH))).then_inc(sem("gates_out"), 1)
            act.wait_ge(sem("g_abs"), 1)
            nc.scalar.activation(zt[0:48, :], zt[0:48, :], ACT.Exp, scale=-1.0).then_inc(sem("g_exp"), 1)
            act.wait_ge(sem("g_exp"), 1)
            nc.scalar.activation(zt[0:48, :], zt[0:48, :], ACT.Ln, bias=ones[0:48, 0:1]).then_inc(sem("g_ln"), 1)

            def place_rows(which, dst, rows, done):
                act.wait_ge(sem("row_split"), primed(3 * which + 3))
                for j in range(3):
                    n = rows.stop - rows.start
                    nc.scalar.activation(dst[32 * j:32 * j + n, :], gsp[rows, j, :], ACT.Copy).then_inc(sem(done), 1)

            def conv_tile(hd, j, i, s):
                matmuls(i * 6 + (SLAB["mlstm"] + s + 1))
                act.wait_ge(sem("m_conv"), primed(hd * 2))
                nc.scalar.activation(qz[:, j, CONV - 1:], proj[j][:], ACT.Identity,
                                     bias=c1("b_mlstm", i * 6 + s)).then_inc(sem(f"evac{j}"), 1)
                split(i, 6, SLAB["mlstm"], s + 2, WC)

            def mlstm_weight(hd, b):
                act.wait_ge(sem("m_weighted"), primed(hd * NB + max(b - 1, 0)))
                a = acol[:, bass.ds(hd + b * MH, 1)]
                if b < NB - 1:
                    nc.scalar.activation(Dm[:, b % 2, P:S - b * P], nM[:, (b + 1) * P:S], ACT.Exp, bias=a)
                nc.scalar.activation(Dm[:, b % 2, 0:P], nMd[:, b * P:(b + 1) * P], ACT.Exp, bias=a).then_inc(sem("m_D"), 1)

            def mlstm_head(hd, more=True):
                n = SLAB["mlstm"]
                for j in range(2):
                    matmuls(hd * 6 + (n + j + 3))
                    act.wait_ge(sem("m_turned"), primed(hd * 2))
                    nc.scalar.activation(mvT[:, j, :], proj[j][:], ACT.Identity,
                                         bias=c1("b_mlstm", hd * 6 + (j + 2))).then_inc(sem(f"evac{j}"), 1)
                    split(hd, 6, n, j + 4, WC)
                act.preload_act_table(ACT.Silu)
                for j in range(2):
                    act.wait_ge(sem("m_conv"), primed(hd * 2 + (j + 1)))
                    act.wait_ge(sem("m_values"), primed(hd * NB))
                    nc.scalar.activation(qk[:, j, :], cv[:, j, :], ACT.Silu).then_inc(sem("m_qk"), 1)
                act.preload_act_table_set("natural_log_exp_and_others")
                matmuls(hd * 6 + (n + 5))
                act.wait_ge(sem("m_gated"), primed(hd * 2))
                nc.scalar.activation(so[:, 0, :], proj[0][:], ACT.Identity,
                                     bias=c1("b_mlstm", hd * 6 + 4)).then_inc(sem("evac0"), 1)
                split(hd, 6, n, 6, WC)
                for j in range(2):
                    act.wait_ge(sem("m_turned"), primed(hd * 2 + (j + 1)))
                    nc.scalar.activation(mv[:, :, j * P:(j + 1) * P], bank[2 + j][:].rearrange("p (b n) -> p b n", b=NB),
                                         ACT.Copy).then_inc(sem("m_v"), 1)
                act.wait_ge(sem("m_bcast"), hd * 2 + 1)
                act.wait_ge(sem("m_nMd"), primed(hd))
                nc.scalar.activation(nM[:], bank[4][:], ACT.Copy).then_inc(sem("m_nM"), 1)
                act.wait_ge(sem("m_acol"), hd + 1)
                nc.scalar.activation(acol[:], bank[6][:, 0:NB * MH], ACT.Copy).then_inc(sem("m_acols"), 1)
                act.wait_ge(sem("m_bcast"), hd * 2 + 2)
                act.wait_ge(sem("m_normed"), primed(hd * 2))
                nc.scalar.activation(emm[:], bank[5][:], ACT.Exp).then_inc(sem("m_emm"), 1)
                act.wait_ge(sem("m_nMd"), primed(hd + 1))
                act.wait_ge(sem("m_acols"), hd + 1)
                mlstm_weight(hd, 0)
                mlstm_weight(hd, 1)
                matmuls(hd * 6 + (n + 6))
                nc.scalar.activation(so[:, 1, :], proj[1][:], ACT.Identity,
                                     bias=c1("b_mlstm", hd * 6 + 5)).then_inc(sem("evac1"), 1)
                split(hd, 6, n, 7, WC)
                mlstm_weight(hd, 2)
                mlstm_weight(hd, 3)
                act.preload_act_table(ACT.Sigmoid)
                act.wait_ge(sem("evac1"), primed(hd * 3 + (TILE["mlstm"] // 2 + 3)))
                for j in range(2):
                    nc.scalar.activation(so[:, j, :], so[:, j, :], ACT.Sigmoid).then_inc(sem("m_sig"), 1)
                act.preload_act_table_set("natural_log_exp_and_others")
                if more:
                    conv_tile(hd + 1, 0, hd, 6)
                else:
                    fox_tile(0, 0, 0, 0)
                act.wait_ge(sem("m_out"), primed(hd * 2 + 2))
                nc.scalar.activation(hsq[:, 0, :], hm[:, 0, :], ACT.Square)
                nc.scalar.activation(hsq[:, 1, :], hm[:, 1, :], ACT.Square).then_inc(sem("m_sq"), 1)
                act.wait_ge(sem("m_ss"), hd + 1)
                inverse_root("m", hd, bank[4][:], hrs[:], DV)
                if more:
                    conv_tile(hd + 1, 1, hd, 7)
                else:
                    fox_tile(0, 0, 1, 1)
                for j in range(2):
                    act.wait_ge(sem("m_gated"), primed(hd * 2 + (j + 1)))
                    nc.scalar.activation(chunk(yah, hd * 2 + j), hn[:, j, :], ACT.Copy).then_inc(sem("m_yhi"), 1)

            def fox_tile(p, i, s, j):
                matmuls(i * 6 + (SLAB["fox"] + s + 1))
                act.wait_ge(sem("f_qk"), primed(p * 2))
                bias = c1("b_fox", i * 6 + s)
                nc.scalar.activation(fsq[:, j, :], proj[s % 2][:], ACT.Square, bias=bias)
                nc.scalar.activation(fraw[:, j, :], proj[s % 2][:], ACT.Identity, bias=bias).then_inc(sem(f"evac{s % 2}"), 1)
                split(i, 6, SLAB["fox"], s + 2, WC)
            act.wait_ge(sem("pads"), 1)
            conv_tile(0, 0, 0, 0)
            act.wait_ge(sem("rows_clear"), 3)
            place_rows(0, msM, slice(0, MH), "m_rows")
            conv_tile(0, 1, 0, 1)
            place_rows(1, msm, slice(0, MH), "m_rows")
            with act.Fori(0, MH - 1) as hd:
                mlstm_head(hd)
            mlstm_head(MH - 1, more=False)
            place_rows(2, fsp, slice(32, 48), "f_rows")

            UA = AH * NB

            def fox_exps(t, k):
                W = (k % NB + 1) * P
                act.wait_ge(sem("negmax"), t * 8 + (UA + k + 1))
                act.wait_ge(sem("pT_ready"), t * 8 + (UA + k - 1))
                st = stat[:, k % 2, :]
                nc.scalar.activation(fprob[:, k % 2, 0:W], bank[2 + k % 2][:, 0:W], ACT.Exp, bias=st[:, 1:2],
                                     accum_out=st[:, 2:3]).then_inc(sem("probs"), 1)

            def fox_copy(t, k):
                W = (k % NB + 1) * P
                act.wait_ge(sem("pT_ready"), t * 8 + (UA + k + 1))
                act.wait_ge(sem("values"), t * 8 + (UA + k - 1))
                nc.scalar.activation(fpT[:, k % 2, 0:W], bank[5 + k % 2][:, 0:W], ACT.Copy).then_inc(sem("pT_copied"), 1)

            def fox_values(i, s):
                matmuls(i * 6 + (SLAB["fox"] + s + 1))
                nc.scalar.activation(fvraw[:], proj[s % 2][:], ACT.Identity,
                                     bias=c1("b_fox", i * 6 + s)).then_inc(sem(f"evac{s % 2}"), 1)

            def fox_roots(p, j):
                act.wait_ge(sem("f_ss"), p * 2 + (j + 1))
                nc.scalar.activation(frs[:, j, :], bank[4][:], ACT.Ln, scale=1.0 / DH, bias=epsc[:]).then_inc(sem("f_ln"), 1)
                act.wait_ge(sem("f_ln"), p * 2 + (j + 1))
                nc.scalar.activation(frs[:, j, :], frs[:, j, :], ACT.Exp, scale=-0.5).then_inc(sem("f_rstd"), 1)

            def merge_tile(j):
                matmuls(SLAB["merge"] + j + 1)
                if j == 1:
                    nc.scalar.activation(br[:, 0, :], proj[1][:], ACT.Copy).then_inc(sem("evac1"), 1)
                else:
                    nc.scalar.activation(sg[:, j // 2, :], proj[0][:], ACT.Identity,
                                         bias=c1("b_merge", j // 2)).then_inc(sem("evac0"), 1)
                split(0, 4, SLAB["merge"], j + 2, WC)

            def fox_pair(i, tt, more=True):
                t = i * 2 + tt
                s = 3 * tt + 3
                for k in range(8):
                    fox_copy(t, k)
                    if k == 0:
                        act.wait_ge(sem("f_vT"), t + 1)
                        nc.scalar.activation(fv[:].rearrange("p b n -> p (b n)"), bank[4][:], ACT.Copy).then_inc(sem("f_v"), 1)
                    if k + 2 < 8:
                        fox_exps(t, k + 2)
                    if not more and k in (1, 4, 7):
                        merge_tile((k - 1) // 3)
                    if more:
                        if k == 1:
                            fox_tile(t + 1, i, s, 0)
                        if k == 3:
                            fox_roots(t + 1, 0)
                        if k == 4:
                            fox_tile(t + 1, i, s + 1, 1)
                        if k == 5:
                            fox_roots(t + 1, 1)
                        if k == 7:
                            fox_exps(t + 1, 0)
                            fox_values(i, s + 2)
                act.wait_ge(sem("values"), t * 8 + (UA + 8))
                nc.scalar.activation(chunk(ybh, t), bank[7][:], ACT.Copy).then_inc(sem("yb_hi"), 1)
                if more:
                    fox_exps(t + 1, 1)
                    split(i, 6, SLAB["fox"], s + 4, WC)

            fox_roots(0, 0)
            fox_values(0, 2)
            fox_roots(0, 1)
            split(0, 6, SLAB["fox"], 4, WC)
            fox_exps(0, 0)
            fox_exps(0, 1)
            with act.Fori(0, FH // 4 - 1) as i:
                for tt in range(2):
                    fox_pair(i, tt)
            fox_pair(FH // 4 - 1, 0)
            fox_pair(FH // 4 - 1, 1, more=False)

            def merge_high(m):
                act.wait_ge(sem("mg"), primed(m + 1))
                nc.scalar.activation(chunk(mgh, m), mg[:, 0, :], ACT.Copy).then_inc(sem("mg_hi"), 1)

            def merge_step(i, ahead):
                n = SLAB["merge"] + 4
                for j in range(2):
                    matmuls(i * 4 + (n + 2 * j + 1))
                    act.wait_ge(sem("evac1"), primed(i * 2 + (TILE["merge"] // 2 + j + 1)))
                    nc.scalar.activation(sg[:, j, :], proj[0][:], ACT.Sigmoid,
                                         bias=c1("b_merge", i * 2 + (j + 2))).then_inc(sem("evac0"), 1)
                    ahead(2 * j)
                    ahead(2 * j + 1)
                merge_high(i + 1)

            act.preload_act_table(ACT.Sigmoid)
            act.wait_ge(sem("evac0"), primed(TILE["merge"] // 2 + 2))
            for j in range(2):
                nc.scalar.activation(sg[:, j, :], sg[:, j, :], ACT.Sigmoid).then_inc(sem("mg_sig"), 1)
            matmuls(SLAB["merge"] + 4)
            split(0, 4, SLAB["merge"], 5, WC)
            merge_high(0)
            steps("merge", 4, KC - 1, merge_step, "out2", i0=1)
            steps("out2", 2, N_OUT // 2, out_step(4, "out2"), "ff2")
            norm(4, shift=6)
            act.preload_act_table(ACT.Silu)
            steps("ff2", 4, FC // 2, ff_step(2, 0), "down2")
            steps("down2", 4, N_DOWN // 4, down_step(None, "down2"))

        @block.vector
        def _(dve):
            V = nc.vector

            def matmuls(n):
                dve.wait_ge(sem("mm_done"), n)

            def add_square(r, m, k):
                dve.wait_ge(sem("sq"), m + (KC * r + 1))
                dve.wait_ge(sem("ssum"), primed(m + KC * r))
                V.tensor_tensor(ssum[:], ssum[:], sqn[:, k, :], ALU.add).then_inc(sem("ssum"), 1)

            def clear_sum(r):
                dve.wait_ge(sem("norm_sum"), primed(r))
                V.memset(ssum[:], 0.0).then_inc(sem("ssum_clear"), 1)
                dve.wait_ge(sem("ssum_clear"), r + 1)

            def norm(r, weight, shift=None):
                def scaled(c):
                    if c >= 3:
                        dve.wait_ge(sem(f"x_lo{(c - 3) % 2}"), primed(r * (KC // 2) + (c - 3) // 2 + 1))
                    V.scalar_tensor_tensor(tmp[c % 3], chunk(h, c), weight(c), rstd[:], ALU.mult,
                                           ALU.mult).then_inc(sem("x_scaled"), 1)

                def low(c):
                    dve.wait_ge(sem("x_hi"), KC * r + c + 1)
                    sh = 0.0 if shift is None else modc[:, shift * KC + c:shift * KC + c + 1]
                    V.scalar_tensor_tensor(xl[:, c, :], tmp[c % 3], sh, xh[:, c, :].bitcast(F32), ALU.add,
                                           ALU.subtract).then_inc(sem("x_lo0"), 1)

                dve.wait_ge(sem("norm_rstd"), r + 1)
                for c in range(3):
                    scaled(c)
                for c in range(0, KC, 2):
                    low(c)
                    for d in (c + 3, c + 4):
                        if d < KC:
                            scaled(d)

            V.memset(epsc[:], EPS)
            V.memset(ones[:], 1.0).then_inc(sem("ones"), 1)
            clear_sum(0)
            for c in range(KC):
                add_square(0, c, c % 2)
            dve.wait_ge(sem("cols_in"), 16)
            V.tensor_scalar(lg[:], col[:, COL["decay_f"]:COL["decay_f"] + 2 * RH], -1.0, None, ALU.mult).then_inc(sem("lg"), 1)
            dve.wait_ge(sem("lg"), 1)
            V.tensor_tensor(lg[:], lg[:], col[:, COL["decay_f"]:COL["decay_f"] + 2 * RH], ALU.min).then_inc(sem("lg"), 1)
            V.tensor_scalar(c1("q_norm"), c1("q_norm"), DH ** -0.5, None, ALU.mult).then_inc(sem("q_scale"), 1)
            V.tensor_scalar(col[:, COL["fox_q"]:COL["fox_q"] + FH // 2], col[:, COL["fox_q"]:COL["fox_q"] + FH // 2], DH ** -0.5, None,
                            ALU.mult).then_inc(sem("q_scale"), 1)
            norm(0, lambda c: c1("attn_norm", c))
            dve.wait_ge(sem("const_in"), 16 * 7)
            V.tensor_copy(identb[:], ident[:])
            V.tensor_copy(geb[:], ge[:])
            V.tensor_copy(leb[:], leconst[:]).then_inc(sem("const_ready"), 1)

            def rope_part(p, slot, turned, part):
                if part == 0:
                    dve.wait_ge(sem("rope_rot"), p + 1)
                    dve.wait_ge(sem("rope_out"), primed(p))
                    V.tensor_tensor(rt[:, 0, :], bank[turned][:], sin[:], ALU.mult).then_inc(sem("rope_part"), 1)
                else:
                    V.tensor_tensor(rt[:, 1, :], rraw[:, slot, :], cos[:], ALU.mult).then_inc(sem("rope_part"), 1)

            def normed_rope(p, dst):
                for part in range(2):
                    rope_part(p, p % 2, 6, part)
                dve.wait_ge(sem("rope_part"), p * 2 + 2)
                V.tensor_tensor(rt[:, 0, :], rt[:, 0, :], rt[:, 1, :], ALU.add).then_inc(sem("rope_sum"), 1)
                dve.wait_ge(sem("rope_sum"), p + 1)
                dve.wait_ge(sem("rope_rstd"), p + 1)
                V.tensor_tensor(dst, rt[:, 0, :], rr[:], ALU.mult).then_inc(sem("rope_out"), 1)

            def ret_rope(t, j, part):
                p = t * 2 + (QT + j)
                if part < 2:
                    rope_part(p, j, 4, part)
                else:
                    dve.wait_ge(sem("rope_part"), p * 2 + 2)
                    V.tensor_tensor((rqf, rkf)[j][:], rt[:, 0, :], rt[:, 1, :], ALU.add).then_inc(sem("rope_out"), 1)

            def ret_lows(t, j):
                for e in range(2):
                    H, other = halves(e)
                    dve.wait_ge(sem("ret_high"), t * 4 + (2 * j + e + 1))
                    src, high, dst = ((rqf, rqs, rql[H, :]), (rkf, rks, rks[other, e, :]))[j]
                    V.tensor_tensor(dst, src[H, :], high[H, e, :].bitcast(F32), ALU.subtract).then_inc(sem("ret_low"), 1)

            def queries(t):
                for e in range(2):
                    H, other = halves(e)
                    V.tensor_copy(wqs[H, e, :], chunk(qall, t)[H]).then_inc(sem("q_high"), 1)
                for e in range(2):
                    H, other = halves(e)
                    dve.wait_ge(sem("q_high"), t * 2 + (e + 1))
                    V.tensor_tensor(wqs[other, e, :], chunk(qall, t)[H], wqs[H, e, :].bitcast(F32),
                                    ALU.subtract).then_inc(sem("q_low"), 1)

            def window_keys():
                dve.wait_ge(sem("rope_out"), primed(1))
                for e in range(2):
                    H, other = halves(e)
                    V.tensor_copy(wks[other, e, :], kf[H, :])
                    V.tensor_copy(wks[H, e, :], kf[H, :]).then_inc(sem("k_high"), 1)
                for e in range(2):
                    H, other = halves(e)
                    dve.wait_ge(sem("k_high"), e + 1)
                    V.tensor_tensor(wkl[H, :], kf[H, :], wks[H, e, :].bitcast(F32), ALU.subtract)

            def maxima(u, k, width, sink=None):
                st = stat[:, k % 2, :]
                dve.wait_ge(sem("scores"), u + (k + 1))
                if not isinstance(u, int) or u + k > 0:
                    dve.wait_ge(sem("probs_scaled"), primed(u + (k - 1)))
                V.tensor_reduce(st[:, 0:1], bank[2 + k % 2][:, 0:width], AX.X, ALU.max).then_inc(sem("rowmax"), 1)
                dve.wait_ge(sem("rowmax"), u + (k + 1))
                if sink is not None:
                    V.tensor_scalar(st[:, 1:2], st[:, 0:1], sink, -1.0, ALU.max, ALU.mult).then_inc(sem("negmax"), 1)
                else:
                    V.tensor_scalar(st[:, 1:2], st[:, 0:1], -1.0, None, ALU.mult).then_inc(sem("negmax"), 1)

            def win_maxima(t, k):
                maxima(t * 8, k, window(k), c1("sink", t + (k // NB) * (AH // 2)))

            def win_scale(t, k):
                st = stat[:, k % 2, :]
                W = window(k)
                dve.wait_ge(sem("sink_exp"), t * 8 + (k + 1))
                V.tensor_tensor(st[:, 4:5], st[:, 2:3], st[:, 3:4], ALU.add).then_inc(sem("den"), 1)
                dve.wait_ge(sem("den"), t * 8 + (k + 1))
                V.reciprocal(st[:, 5:6], st[:, 4:5]).then_inc(sem("rden"), 1)
                dve.wait_ge(sem("rden"), t * 8 + (k + 1))
                V.tensor_scalar(prob[:, k % 2, 0:W], prob[:, k % 2, 0:W], st[:, 5:6], None,
                                ALU.mult).then_inc(sem("probs_scaled"), 1)

            def ret_decay_logs(t):
                bands = [decay[:, e * REL + S - P:e * REL + S] for e in range(2)]
                for e in range(2):
                    V.tensor_scalar(bands[e], rel[:, 0:P], lg[:, bass.ds(t * 2 + e, 1)], None,
                                    ALU.mult).then_inc(sem("decay_log"), 1)
                for e in range(2):
                    dve.wait_ge(sem("decay_log"), t * 4 + 2)
                    V.scalar_tensor_tensor(bands[e], rel[:, 2 * S - P:2 * S], lg[:, bass.ds(t * 2 + (RH + e), 1)], bands[e], ALU.mult,
                                           ALU.add).then_inc(sem("decay_log"), 1)

            def mixing_step(t, more=True):
                for k in range(8):
                    if k > 1:
                        win_scale(t, k)
                    if k + 2 < 8:
                        win_maxima(t, k + 2)
                    if k == 2:
                        ret_decay_logs(t)
                    if 4 <= k < 7:
                        ret_rope(t, 0, k - 4)
                    if k == 7:
                        ret_rope(t, 1, 0)
                for part in (1, 2):
                    ret_rope(t, 1, part)
                ret_lows(t, 0)
                dve.wait_ge(sem("y_hi"), t + 1)
                V.tensor_tensor(chunk(yl, t * 2), bank[7][:], chunk(yh, t * 2).bitcast(F32), ALU.subtract).then_inc(sem("y_lo"), 1)
                ret_lows(t, 1)
                if more:
                    queries(t + 1)
                dve.wait_ge(sem("decay"), t * 2 + 2)
                for k in range(8):
                    e, b = k // NB, k % NB
                    at = e * REL + S - P - b * P
                    dve.wait_ge(sem("ret_scores"), t * 8 + (k + 1))
                    if k >= 2:
                        dve.wait_ge(sem("ret_values"), t * 8 + (k - 1))
                    V.tensor_tensor(prob[:, k % 2, :], bank[2 + k % 2][:], decay[:, at:at + S],
                                    ALU.mult).then_inc(sem("ret_decayed"), 1)
                if more:
                    win_maxima(t + 1, 0)
                    win_scale(t + 1, 0)
                    win_maxima(t + 1, 1)
                    win_scale(t + 1, 1)
                dve.wait_ge(sem("ret_rstd"), t + 1)
                V.tensor_tensor(ry[:], bank[4][:], rr[:], ALU.mult).then_inc(sem("ret_normed"), 1)
                dve.wait_ge(sem("ret_normed"), t + 1)
                V.scalar_tensor_tensor(ry[:], ry[:], c1("ret_norm", t), rsil[:], ALU.mult, ALU.mult).then_inc(sem("ret_y"), 1)
                dve.wait_ge(sem("ret_y"), t + 1)
                V.tensor_copy(chunk(yh, t * 2 + 1), ry[:]).then_inc(sem("ret_y_hi"), 1)
                dve.wait_ge(sem("ret_y_hi"), t + 1)
                V.tensor_tensor(chunk(yl, t * 2 + 1), ry[:], chunk(yh, t * 2 + 1).bitcast(F32),
                                ALU.subtract).then_inc(sem("y_lo"), 1)

            dve.wait_ge(sem("lg"), 2)
            for p in range(QT):
                if p == QT - 1:
                    win_maxima(0, 0)
                    win_maxima(0, 1)
                    win_scale(0, 0)
                normed_rope(p, qall[:, p - 1, :] if p else kf[:])
                if p == QT - 1:
                    win_scale(0, 1)
                if p == 0:
                    window_keys()
                if p == 1:
                    dve.wait_ge(sem("rope_out"), primed(2))
                    queries(0)
            dve.wait_ge(sem("rel_in"), 16)
            with dve.Fori(0, AH // 2 - 1) as t:
                mixing_step(t)
            mixing_step(AH // 2 - 1, more=False)

            def add_tile(name, per, r, gate, i, s):
                m = i * 2 + s
                matmuls(i * (2 * per) + (SLAB[name] + per * (s + 1)))
                V.scalar_tensor_tensor(chunk(h, m), proj[s][:], gate(m), chunk(h, m), ALU.mult,
                                       ALU.add).then_inc(sem(f"evac{s}"), 1)
                if r is not None:
                    add_square(r, m, s)

            def add_tiles(name, per, r, gate):
                if r is not None:
                    clear_sum(r)
                with dve.Fori(0, KC // 2) as i:
                    for s in range(2):
                        add_tile(name, per, r, gate, i, s)

            def ff_product(run, i, i0, jj):
                j = i * 2 + (2 * i0 + jj)
                matmuls(i * 4 + (SLAB[f"ff{run}"] + 4 * i0 + 2 * jj + 2))
                dve.wait_ge(sem("evac0"), primed(i * 2 + (TILE[f"ff{run}"] // 2 + 2 * i0 + jj + 1)))
                dve.wait_ge(sem("act_lo"), primed(j + run * FC))
                V.tensor_tensor(aprod[:, jj, :], proj[1][:], gsil[:, jj, :], ALU.mult).then_inc(sem("evac1"), 1)

            def ff_low(run, i, i0, jj):
                j = i * 2 + (2 * i0 + jj)
                dve.wait_ge(sem("act_hi"), j + (run * FC + 1))
                V.tensor_tensor(chunk(actl, j), aprod[:, jj, :], chunk(acth, j).bitcast(F32),
                                ALU.subtract).then_inc(sem("act_lo"), 1)

            def ada_parts(v, ks):
                for k in ks:
                    dve.wait_ge(sem(f"ada_in{k % 2}"), v * (KC * 8) + (k // 2 * 16 + 16))
                    W = adaw[:, k % 2, :]
                    V.scalar_tensor_tensor(W, W, 1.0, crow[:], ALU.mult, ALU.mult,
                                           accum_out=modc[:, bass.ds(v * KC + k, 1)]).then_inc(sem("ada_acc"), 1)

            def ff_beside_ada(i, i0, v):
                for jj in range(2):
                    ff_product(0, i, i0, jj)
                    ada_parts(v, range(4 * jj, 4 * jj + 2))
                    ff_low(0, i, i0, jj)
                    ada_parts(v, range(4 * jj + 2, 4 * jj + 4))

            add_tiles("out", 1, 1, lambda m: 1.0)
            norm(1, lambda c: c1("ffn_norm", c))
            dve.wait_ge(sem("c_silu"), 1)
            with dve.Fori(0, NMOD) as i:
                ff_beside_ada(i, 0, i)
            with dve.Fori(0, FC // 2 - NMOD) as i:
                for jj in range(2):
                    ff_product(0, i, NMOD, jj)
                    ff_low(0, i, NMOD, jj)
            dve.wait_ge(sem("ada_acc"), primed(NMOD * KC))
            V.tensor_tensor(modc[:], modc[:], col[:, COL["b_ada"]:COL["b_ada"] + NMOD * KC], ALU.add).then_inc(sem("mod"), 1)
            dve.wait_ge(sem("mod"), 1)
            for r, name in enumerate(("ffn1_norm", "mix_norm", "ffn2_norm")):
                sc = modc[:, (3 * r + 1) * KC:(3 * r + 2) * KC]
                V.scalar_tensor_tensor(scl[:, r * KC:(r + 1) * KC], sc, 1.0, col[:, COL[name]:COL[name] + KC], ALU.add,
                                       ALU.mult).then_inc(sem("mod_cols"), 1)
                V.tensor_scalar(gat[:, r * KC:(r + 1) * KC], modc[:, (3 * r + 2) * KC:(3 * r + 3) * KC], 1.0 if r == 1 else 0.5, None,
                                ALU.mult).then_inc(sem("mod_cols"), 1)
            dve.wait_ge(sem("mod_cols"), 6)
            add_tiles("down0", 2, 2, lambda m: 1.0)

            def ff_products(run):
                with dve.Fori(0, FC // 2) as i:
                    for jj in range(2):
                        ff_product(run, i, 0, jj)
                        ff_low(run, i, 0, jj)

            def gate(r):
                return lambda m: gat[:, bass.ds(m + r * KC, 1)]

            norm(2, lambda c: scl[:, c:c + 1], shift=0)
            ff_products(1)
            add_tiles("down1", 2, 3, gate(0))

            dve.wait_ge(sem("gates_in"), 16)
            V.tensor_copy(ghi[:], gates_raw[:]).then_inc(sem("gates_split"), 1)
            dve.wait_ge(sem("gates_split"), 1)
            V.tensor_tensor(glo[:], gates_raw[:], ghi[:].bitcast(F32), ALU.subtract).then_inc(sem("gates_split"), 1)
            V.memset(qz[:, :, 0:CONV - 1], 0.0).then_inc(sem("pads"), 1)
            norm(3, lambda c: scl[:, KC + c:KC + c + 1], shift=3)

            dve.wait_ge(sem("gates_out"), 2)
            V.scalar_tensor_tensor(zt[0:48, :], zg[0:48, :], -1.0, zg[0:48, :], ALU.mult, ALU.max).then_inc(sem("g_abs"), 1)
            V.memset(zrow[:], 0.0).then_inc(sem("zeros"), 1)
            for t_ in (msM, msm, fsp):
                V.memset(t_[:], 0.0).then_inc(sem("rows_clear"), 1)
            dve.wait_ge(sem("g_ln"), 1)
            V.scalar_tensor_tensor(lf[:], zg[0:48, :], 0.0, zt[0:48, :], ALU.min, ALU.subtract).then_inc(sem("log_f"), 1)
            dve.wait_ge(sem("zeros"), 1)
            dve.wait_ge(sem("log_f"), 1)
            V.tensor_tensor_scan(cs[:], zrow[:], lf[:], 0.0, ALU.add, ALU.add).then_inc(sem("cum_f"), 1)

            def split_rows(which, rows, src):
                rest = [src, zt[rows, :], zg[rows, :]]
                for j in range(3):
                    V.tensor_copy(gsp[rows, j, :], rest[j]).then_inc(sem("row_split"), 1)
                    if j < 2:
                        dve.wait_ge(sem("row_split"), primed(3 * which + j + 1))
                        V.tensor_tensor(rest[j + 1], rest[j], gsp[rows, j, :], ALU.subtract).then_inc(sem("row_rest"), 1)
                        dve.wait_ge(sem("row_rest"), 2 * which + j + 1)

            H4 = slice(0, MH)
            dve.wait_ge(sem("cum_f"), 1)
            V.tensor_tensor(arow[:], zi[:], cs[H4, :], ALU.subtract).then_inc(sem("arow"), 1)
            dve.wait_ge(sem("arow"), 1)
            mrow, frow = lf[H4, :], zi[:]
            V.tensor_tensor_scan(mrow, arow[:], arow[:], 0.0, ALU.max, ALU.max).then_inc(sem("mrow"), 1)
            dve.wait_ge(sem("mrow"), 1)
            split_rows(0, H4, mrow)
            V.tensor_tensor(frow, cs[H4, :], mrow, ALU.add).then_inc(sem("frow"), 1)
            for g in range(FH):
                V.tensor_scalar(sel[:, g, :], ones[0:96, :], c1("sel", g, rows=slice(0, 96)), None,
                                ALU.mult).then_inc(sem("sel_ready"), 1)
            dve.wait_ge(sem("frow"), 1)
            dve.wait_ge(sem("m_rows"), 3)
            split_rows(1, H4, frow)

            def convolve(hd):
                for j in range(2):
                    dve.wait_ge(sem(f"evac{j}"), primed(hd * 3 + (TILE["mlstm"] // 2 + 1)))
                    dve.wait_ge(sem("m_qk"), primed(hd * 2))
                    cw = lambda tap: c1("conv_w", hd * (2 * CONV) + (j * CONV + tap))
                    V.tensor_scalar(cv[:, j, :], qz[:, j, 0:S], cw(0), c1("conv_b", hd * 2 + j), ALU.mult,
                                    ALU.add).then_inc(sem("m_tap"), 1)
                    for tap in range(1, CONV):
                        dve.wait_ge(sem("m_tap"), hd * (2 * (CONV - 1)) + (j * (CONV - 1) + tap))
                        V.scalar_tensor_tensor(cv[:, j, :], qz[:, j, tap:tap + S], cw(tap), cv[:, j, :], ALU.mult,
                                               ALU.add).then_inc(sem("m_tap" if tap < CONV - 1 else "m_conv"), 1)

            def mlstm_head(hd, more=True):
                dve.wait_ge(sem("m_nM"), hd + 1)
                for b in range(NB):
                    ins = V.tensor_tensor(nMd[:, b * P:(b + 1) * P], nM[:, b * P:(b + 1) * P], ge[:], ALU.add)
                ins.then_inc(sem("m_nMd"), 1)
                for b in range(NB):
                    W = S - b * P
                    dve.wait_ge(sem("m_D"), hd * NB + (b + 1))
                    dve.wait_ge(sem("m_scores"), hd * NB + (b + 1))
                    dve.wait_ge(sem("m_values"), primed(hd * NB + max(b - 1, 0)))
                    V.scalar_tensor_tensor(sT[:, b % 2, 0:W], bank[2 + b % 2][:, 0:W], DQK ** -0.5, Dm[:, b % 2, 0:W], ALU.mult,
                                           ALU.mult).then_inc(sem("m_weighted"), 1)
                dve.wait_ge(sem("m_values"), primed(hd * NB + NB))
                dve.wait_ge(sem("m_emm"), hd + 1)
                dve.wait_ge(sem("m_y"), primed(hd * 2))
                V.tensor_scalar(mxr[:, 0, :], bank[7][:], -1.0, None, ALU.mult).then_inc(sem("m_den"), 1)
                dve.wait_ge(sem("m_den"), hd * 4 + 1)
                V.tensor_tensor(mxr[:, 0, :], mxr[:, 0, :], bank[7][:], ALU.max).then_inc(sem("m_den"), 1)
                dve.wait_ge(sem("m_den"), hd * 4 + 2)
                V.tensor_tensor(mxr[:, 0, :], mxr[:, 0, :], emm[:], ALU.max).then_inc(sem("m_den"), 1)
                dve.wait_ge(sem("m_den"), hd * 4 + 3)
                V.reciprocal(mxr[:, 1, :], mxr[:, 0, :]).then_inc(sem("m_den"), 1)
                dve.wait_ge(sem("m_den"), hd * 4 + 4)
                for j in range(2):
                    V.tensor_tensor(hm[:, j, :], bank[5 + j][:], mxr[:, 1, :], ALU.mult).then_inc(sem("m_out"), 1)
                dve.wait_ge(sem("m_rstd"), hd + 1)
                for j in range(2):
                    V.scalar_tensor_tensor(hn[:, j, :], hm[:, j, :], c1("mlstm_norm", hd * 2 + j), hrs[:], ALU.mult,
                                           ALU.mult).then_inc(sem("m_normed"), 1)
                dve.wait_ge(sem("m_sig"), hd * 2 + 2)
                dve.wait_ge(sem("m_normed"), primed(hd * 2 + 2))
                for j in range(2):
                    V.tensor_tensor(hn[:, j, :], hn[:, j, :], so[:, j, :], ALU.mult).then_inc(sem("m_gated"), 1)
                if more:
                    convolve(hd + 1)
                for j in range(2):
                    dve.wait_ge(sem("m_yhi"), hd * 2 + (j + 1))
                    V.tensor_tensor(chunk(yal, hd * 2 + j), hn[:, j, :], chunk(yah, hd * 2 + j).bitcast(F32),
                                    ALU.subtract).then_inc(sem("m_y"), 1)

            convolve(0)
            split_rows(2, slice(32, 48), cs[32:48, :])
            with dve.Fori(0, MH - 1) as hd:
                mlstm_head(hd)
            mlstm_head(MH - 1, more=False)

            UA = AH * NB

            def fox_maxima(t, k):
                maxima(t * 8 + UA, k, (k % NB + 1) * P)

            def fox_scale(t, k):
                st = stat[:, k % 2, :]
                W = (k % NB + 1) * P
                dve.wait_ge(sem("probs"), t * 8 + (UA + k + 1))
                V.reciprocal(st[:, 5:6], st[:, 2:3]).then_inc(sem("rden"), 1)
                dve.wait_ge(sem("rden"), t * 8 + (UA + k + 1))
                V.tensor_scalar(fprob[:, k % 2, 0:W], fprob[:, k % 2, 0:W], st[:, 5:6], None,
                                ALU.mult).then_inc(sem("probs_scaled"), 1)

            def fox_normed(p, par, j):
                dve.wait_ge(sem("f_rstd"), p * 2 + (j + 1))
                V.scalar_tensor_tensor((fq, fk)[j][:, par, :], fraw[:, j, :], c1(("fox_q", "fox_k")[j], p), frs[:, j, :], ALU.mult,
                                       ALU.mult).then_inc(sem("f_qk"), 1)

            def fox_pair(i, tt, more=True):
                t = i * 2 + tt
                for k in range(8):
                    if k > 0:
                        fox_scale(t, k)
                    if k + 2 < 8:
                        fox_maxima(t, k + 2)
                    if more and k >= 5 and k < 7:
                        fox_normed(t + 1, 1 - tt, k - 5)
                if more:
                    fox_maxima(t + 1, 0)
                    fox_scale(t + 1, 0)
                    fox_maxima(t + 1, 1)
                dve.wait_ge(sem("yb_hi"), t + 1)
                V.tensor_tensor(chunk(ybl, t), bank[7][:], chunk(ybh, t).bitcast(F32), ALU.subtract).then_inc(sem("yb_lo"), 1)

            dve.wait_ge(sem("q_scale"), 2)
            for j in range(2):
                fox_normed(0, 0, j)
            fox_maxima(0, 0)
            fox_maxima(0, 1)
            fox_scale(0, 0)
            with dve.Fori(0, FH // 4 - 1) as i:
                for tt in range(2):
                    fox_pair(i, tt)
            fox_pair(FH // 4 - 1, 0)
            fox_pair(FH // 4 - 1, 1, more=False)

            def branch(m, j):
                matmuls(m * 4 + (SLAB["merge"] + 2 * j + 2))
                dve.wait_ge(sem("mg"), primed(m))
                dve.wait_ge(sem("evac0"), primed(m * 2 + (TILE["merge"] // 2 + j + 1)))
                V.tensor_tensor(br[:, j, :], proj[1][:], sg[:, j, :], ALU.mult).then_inc(sem("evac1"), 1)

            def merged(m):
                dve.wait_ge(sem("evac1"), primed(m * 2 + (TILE["merge"] // 2 + 2)))
                dve.wait_ge(sem("mg_lo"), primed(m))
                V.tensor_tensor(mg[:, 0, :], br[:, 0, :], br[:, 1, :], ALU.add).then_inc(sem("mg"), 1)
                dve.wait_ge(sem("mg_hi"), m + 1)
                V.tensor_tensor(chunk(mgl, m), mg[:, 0, :], chunk(mgh, m).bitcast(F32), ALU.subtract).then_inc(sem("mg_lo"), 1)

            dve.wait_ge(sem("evac1"), primed(TILE["merge"] // 2 + 1))
            dve.wait_ge(sem("mg_sig"), 2)
            V.tensor_tensor(br[:, 0, :], br[:, 0, :], sg[:, 0, :], ALU.mult).then_inc(sem("mg_first"), 1)
            branch(0, 1)
            dve.wait_ge(sem("mg_first"), 1)
            merged(0)
            with dve.Fori(0, KC - 1) as i:
                for j in range(2):
                    branch(i + 1, j)
                merged(i + 1)
            add_tiles("out2", 1, 4, gate(1))
            norm(4, lambda c: scl[:, 2 * KC + c:2 * KC + c + 1], shift=6)
            ff_products(2)
            add_tiles("down2", 2, None, gate(2))


def constants():
    p = np.arange(P)
    ident = np.eye(P, dtype=np.float32)
    blk = (p[:, None] // DH == p[None, :] // DH).astype(np.float32)
    rot = np.zeros((P, P), np.float32)
    for o in range(P):
        if o % DH < DH // 2:
            rot[o + DH // 2, o] = -1.0
        else:
            rot[o - DH // 2, o] = 1.0
    ge = np.where(p[None, :] >= p[:, None], 0.0, NEG).astype(np.float32)
    le = np.where(p[None, :] <= p[:, None], 0.0, NEG).astype(np.float32)
    inv = (np.float32(10000.0) ** (-np.arange(0, DH, 2, dtype=np.float32) / np.float32(DH))).astype(np.float32)
    ang = inv[p % (DH // 2)][:, None] * np.arange(S, dtype=np.float32)[None, :]
    const = np.concatenate([ident, blk, rot, ge, le, np.cos(ang), np.sin(ang)], 1).astype(np.float32)
    diff = np.arange(REL)[None, :] - (REL - S) - p[:, None]
    rel = np.concatenate([np.maximum(diff, 0)[:, S - P:], np.maximum(-diff, 0)[:, :S]], 1).astype(np.float32)
    sel = np.zeros((P, FH), np.float32)
    for g in range(FH):
        sel[[g, 32 + g, 64 + g], g] = -1.0
    return const, rel, sel


def kernel(**inputs):
    import concourse.bacc as bacc
    from concourse.bass_utils import run_bass_kernel_spmd

    a = {k: np.asarray(v) for k, v in inputs.items()}

    def tile(w, cols):
        w = w[:, cols]
        return w.reshape(-1, P, w.shape[1]).transpose(1, 0, 2).reshape(P, -1)

    def tiles(w):
        return [tile(w, slice(m * P, (m + 1) * P)) for m in range(w.shape[1] // P)]

    def pairs(w, v):
        return [t for both in zip(tiles(w), tiles(v)) for t in both]

    w_in, w_mix, b_mix = a["w_in"][0], a["w_mix_2"][0], a["b_mix_2"][0]
    pair = [np.r_[t * DH:(t + 1) * DH, (t + 4) * DH:(t + 5) * DH] for t in range(AH // 2)]
    kv0 = AH * DH
    att = [tile(w_in, c) for c in (slice(kv0, kv0 + P), *pair, slice(kv0 + P, kv0 + 2 * P))]
    r0 = kv0 + 2 * P
    RW = RH * DH
    ret = [tile(w_in, slice(r0 + j * RW + t * P, r0 + j * RW + (t + 1) * P)) for t in range(RH // 2) for j in range(4)]
    order = np.concatenate([c for t in range(AH // 2) for c in (pair[t], np.arange(AH * DH + t * P, AH * DH + (t + 1) * P))])
    out1 = tiles(a["w_out"][0][order])
    o = np.cumsum([0, 512, 512, 1024, 1024, MH, MH, D, D, D, FH, D, D])
    m_at = [s for hd in range(MH) for s in (o[0] + hd * P, o[1] + hd * P, o[2] + hd * DV, o[2] + hd * DV + P,
                                            o[3] + hd * DV, o[3] + hd * DV + P)]
    f_at = [o[j] + t * P for t in range(FH // 2) for j in (6, 7, 8)]
    g_at = [o[j] + m * P for m in range(KC) for j in (10, 11)]
    gates = tiles(np.ascontiguousarray(w_mix[:, o[10]:o[12]]))
    wa, wb = tiles(a["w_branch_a_2"][0]), tiles(a["w_branch_b_2"][0])
    merge = [t for m in range(KC) for t in (gates[m], wa[m], gates[KC + m], wb[m])]
    f1, f2 = a["ffn1_w_in_2"][0], a["ffn2_w_in_2"][0]
    w_all = np.stack(att + ret + out1 + pairs(a["w_gate"][0], a["w_up"][0]) + pairs(f1[:, :FF], f1[:, FF:])
                     + [tile(w_mix, slice(c, c + P)) for c in m_at + f_at] + merge + tiles(a["w_out_2"][0])
                     + pairs(f2[:, :FF], f2[:, FF:]))
    wd_all = np.stack([tile(w[f * DC:(f + 1) * DC], slice(m * P, (m + 1) * P))
                       for w in (a["w_down"][0], a["ffn1_w_out_2"][0], a["ffn2_w_out_2"][0]) for m in range(KC) for f in range(2)])
    ada = a["w_ada_2"][0].reshape(D, NMOD * KC, P).transpose(1, 2, 0)

    gate_rows = ((0, slice(o[5], o[6])), (32, slice(o[9], o[10])), (64, slice(o[4], o[5])))
    gw = np.zeros((D, 96), np.float32)
    gb = np.zeros((P, 1), np.float32)
    for at, c in gate_rows:
        gw[:, at:at + c.stop - c.start] = w_mix[:, c]
        gb[at:at + c.stop - c.start, 0] = b_mix[c]

    def columns(v):
        return v.reshape(-1, P).T

    def everywhere(v):
        return np.broadcast_to(v[None, :], (P, v.size))

    const, rel, sel = constants()
    conv = a["conv_w_2"][0].reshape(CONV, 2, MH, P).transpose(3, 2, 1, 0).reshape(P, -1)
    convb = a["conv_b_2"][0].reshape(2, MH, P).transpose(2, 1, 0).reshape(P, -1)
    at_cols = lambda starts: np.stack([b_mix[c:c + P] for c in starts], 1)
    cols = np.concatenate([
        columns(a["attn_norm_w"][0]), columns(a["ffn_norm_w"][0]), columns(a["ffn1_norm_g_2"][0]), columns(a["mix_norm_g_2"][0]),
        columns(a["ffn2_norm_g_2"][0]), np.tile(a["q_norm_w"][0], 2)[:, None], np.tile(a["k_norm_w"][0], 2)[:, None],
        columns(a["ret_norm_w"][0]), everywhere(a["attn_sink"][0]), everywhere(a["ret_log_decay_fwd"][0]),
        everywhere(a["ret_log_decay_bwd"][0]), columns(a["b_ada_2"][0]), gb, at_cols(m_at), conv, convb,
        columns(a["mlstm_norm_g_2"][0].reshape(-1)), at_cols(f_at), columns(a["fox_q_norm_g_2"][0].reshape(-1)),
        columns(a["fox_k_norm_g_2"][0].reshape(-1)), at_cols(g_at), sel], 1)
    assert cols.shape == (P, NCOL)
    x = a["x"][0].reshape(S, KC, P).transpose(2, 1, 0).reshape(P, KC * S)

    arrays = {"x": x, "cols": cols, "const": const, "rel": rel, "w": w_all, "wd": wd_all,
              "ada": ada, "c": everywhere(a["c_2"][0]), "gates": tile(gw, slice(0, 96))}
    arrays = {k: np.ascontiguousarray(v) for k, v in arrays.items()}
    nc = bacc.Bacc("TRN2", target_bir_lowering=False, num_devices=1)
    args = [nc.dram_tensor(k + "_dram", v.shape, F32, kind="ExternalInput").ap() for k, v in arrays.items()]
    out = nc.dram_tensor("out_dram", (P, KC * S), F32, kind="ExternalOutput").ap()
    arrays = {k + "_dram": v for k, v in arrays.items()}
    build(nc, *args, out)
    r = run_bass_kernel_spmd(nc, [arrays], core_ids=[0])
    got = r.results[0]["out_dram"]
    return np.ascontiguousarray(got.reshape(P, KC, S).transpose(2, 1, 0).reshape(1, S, D))
```
